# Optimizing a Trainium2 kernel written in Bass

```python
import math
import jax, jax.numpy as jnp
from jax import lax
import numpy as np

D_MODEL = 1024
BATCH = 1
SEQ = 256
DEPTH = 2

N_EVEN = (DEPTH + 1) // 2
N_ODD = DEPTH // 2
DN_ALPHA = (2.0 * DEPTH) ** 0.25
DN_BETA = (8.0 * DEPTH) ** -0.25
LN_EPS = 1e-5
NEG = -1e30
Q_BLOCK = 128

GM_WIDTH = D_MODEL // 2
GM_GROUPS = 4
GM_GROUP_DIM = GM_WIDTH // GM_GROUPS
GM_CHUNK = 128

MLA_HEADS = 8
MLA_NOPE = 64
MLA_ROPE = 32
MLA_V = 64
MLA_Q_RANK = D_MODEL // 4
MLA_KV_RANK = D_MODEL // 8
ROPE_BASE = 10000.0
AB_IN = 2 * GM_WIDTH + MLA_Q_RANK + MLA_KV_RANK + MLA_ROPE
AB_MIX = GM_WIDTH + MLA_HEADS * MLA_V
AB_SPLITS = (GM_WIDTH, 2 * GM_WIDTH, 2 * GM_WIDTH + MLA_Q_RANK,
             2 * GM_WIDTH + MLA_Q_RANK + MLA_KV_RANK)

NSA_HEADS = 16
NSA_GROUPS = 2
NSA_HPG = NSA_HEADS // NSA_GROUPS
NSA_DH = 64
NSA_CMP_LEN = 32
NSA_CMP_STRIDE = 16
NSA_CMP_HIDDEN = 256
NSA_SEL_LEN = 64
NSA_TOPK = 8
NSA_SEL_QBLOCK = 64
NSA_WINDOW = 512
NSA_BRANCHES = 3
NSA_KV = NSA_GROUPS * NSA_DH
C_MIX = NSA_HEADS * NSA_DH
C_IN = C_MIX + 6 * NSA_KV + NSA_BRANCHES * NSA_HEADS
NSA_SPLITS = tuple(C_MIX + i * NSA_KV for i in range(7))
NSA_FORCE = 1e4

MOE_GROUPS = 4
MOE_EPG = 8
MOE_EXPERTS = MOE_GROUPS * MOE_EPG
MOE_TOPK = 2
MOE_HIDDEN = D_MODEL // 4


def layer_norm(x, g, b):
    xf = x.astype(jnp.float32)
    mu = xf.mean(-1, keepdims=True)
    var = jnp.square(xf - mu).mean(-1, keepdims=True)
    return ((xf - mu) * lax.rsqrt(var + LN_EPS) * g + b).astype(x.dtype)

def rms_norm(x, g):
    xf = x.astype(jnp.float32)
    return (xf * lax.rsqrt(jnp.mean(xf * xf, -1, keepdims=True) + LN_EPS) * g).astype(x.dtype)

def rope(x, pos):
    half = x.shape[-1] // 2
    freq = jnp.exp(-math.log(ROPE_BASE) * jnp.arange(half, dtype=jnp.float32) / half)
    ang = pos.astype(jnp.float32)[:, :, None, None] * freq
    cos, sin = jnp.cos(ang), jnp.sin(ang)
    x1 = x[..., :half].astype(jnp.float32)
    x2 = x[..., half:].astype(jnp.float32)
    return jnp.concatenate([x1 * cos - x2 * sin, x1 * sin + x2 * cos], -1).astype(x.dtype)

def gmlp_mix(u, v, ln_g, ln_b, w_s, b_s):
    B, S, _ = u.shape
    nc = S // GM_CHUNK
    vn = layer_norm(v, ln_g, ln_b).reshape(B, nc, GM_CHUNK, GM_GROUPS, GM_GROUP_DIM)
    causal = jnp.tril(jnp.ones((GM_CHUNK, GM_CHUNK), dtype=bool))
    ws = jnp.where(causal, w_s, 0.0).astype(vn.dtype)
    s = jnp.einsum('gts,bnsgc->bntgc', ws, vn) + jnp.transpose(b_s)[:, :, None]
    return u * s.reshape(B, S, GM_WIDTH)

def mla_mix(c_q, c_kv, k_r, pos, q_norm_g, kv_norm_g, w_uq, w_uk, w_uv):
    B, S, _ = c_q.shape
    q = (rms_norm(c_q, q_norm_g) @ w_uq).reshape(B, S, MLA_HEADS, MLA_NOPE + MLA_ROPE)
    q_nope = q[..., :MLA_NOPE]
    q_rope = rope(q[..., MLA_NOPE:], pos)
    ckv = rms_norm(c_kv, kv_norm_g)
    k_nope = (ckv @ w_uk).reshape(B, S, MLA_HEADS, MLA_NOPE)
    v = (ckv @ w_uv).reshape(B, S, MLA_HEADS, MLA_V)
    k_rope = rope(k_r[:, :, None, :], pos)[:, :, 0]
    scale = (MLA_NOPE + MLA_ROPE) ** -0.5
    outs = []
    for i in range(S // Q_BLOCK):
        q0, q1 = i * Q_BLOCK, (i + 1) * Q_BLOCK
        s = (jnp.einsum('bqhd,bkhd->bhqk', q_nope[:, q0:q1], k_nope[:, :q1])
             + jnp.einsum('bqhr,bkr->bhqk', q_rope[:, q0:q1], k_rope[:, :q1]))
        mask = (q0 + jnp.arange(Q_BLOCK))[:, None] >= jnp.arange(q1)[None, :]
        s = jnp.where(mask, s.astype(jnp.float32) * scale, NEG)
        p = jax.nn.softmax(s, axis=-1).astype(v.dtype)
        outs.append(jnp.einsum('bhqk,bkhd->bqhd', p, v[:, :q1]))
    return jnp.concatenate(outs, axis=1).reshape(B, S, MLA_HEADS * MLA_V)

def ab_mixer(x, pos, w_in, gm_ln_g, gm_ln_b, gm_ws, gm_bs, q_norm_g, kv_norm_g,
             w_uq, w_uk, w_uv, w_o):
    h = x @ w_in
    u, v, c_q, c_kv, k_r = jnp.split(h, AB_SPLITS, axis=-1)
    y_a = gmlp_mix(jax.nn.gelu(u), jax.nn.gelu(v), gm_ln_g, gm_ln_b, gm_ws, gm_bs)
    y_b = mla_mix(c_q, c_kv, k_r, pos, q_norm_g, kv_norm_g, w_uq, w_uk, w_uv)
    return jnp.concatenate([y_a, y_b], axis=-1) @ w_o

def compress_kv(k, pos_emb, w1, w2):
    B, S, G, D = k.shape
    r = NSA_CMP_LEN // NSA_CMP_STRIDE
    sub = k.reshape(B, S // NSA_CMP_STRIDE, NSA_CMP_STRIDE, G, D)
    nc = S // NSA_CMP_STRIDE - r + 1
    blocks = jnp.concatenate([sub[:, j:j + nc] for j in range(r)], axis=2) + pos_emb[:, None, :]
    flat = blocks.transpose(0, 1, 3, 2, 4).reshape(B, nc, G, NSA_CMP_LEN * D)
    return jax.nn.gelu(flat @ w1) @ w2

def nsa_compressed(q, k_cmp, v_cmp):
    S, nc = q.shape[1], k_cmp.shape[1]
    s = jnp.einsum('btgid,bngd->bgitn', q, k_cmp).astype(jnp.float32) * NSA_DH ** -0.5
    end = jnp.arange(nc) * NSA_CMP_STRIDE + NSA_CMP_LEN - 1
    mask = jnp.arange(S)[:, None] >= end[None, :]
    p = jnp.where(mask, jax.nn.softmax(jnp.where(mask, s, NEG), axis=-1), 0.0)
    o = jnp.einsum('bgitn,bngd->btgid', p.astype(v_cmp.dtype), v_cmp)
    return o, p

def nsa_select_blocks(p_cmp):
    S, nc = p_cmp.shape[3], p_cmp.shape[4]
    nsel = S // NSA_SEL_LEN
    c0 = jnp.arange(nc) * NSA_CMP_STRIDE
    s0 = jnp.arange(nsel) * NSA_SEL_LEN
    cover = ((c0[:, None] < s0[None, :] + NSA_SEL_LEN)
             & (c0[:, None] + NSA_CMP_LEN > s0[None, :])).astype(jnp.float32)
    imp = jnp.einsum('bgitn,nj->bgtj', p_cmp, cover)
    jj = jnp.arange(nsel)[None, :]
    tb = (jnp.arange(S) // NSA_SEL_LEN)[:, None]
    forced = (jj == 0) | (jj == tb) | (jj == tb - 1)
    score = jnp.where(forced, NSA_FORCE, jnp.where(jj <= tb, imp, -NSA_FORCE))
    _, idx = lax.top_k(score, min(NSA_TOPK, nsel))
    return idx

def nsa_selected(q, k_s, v_s, sel_idx):
    B, S, G, HPG, D = q.shape
    K = sel_idx.shape[-1]
    nsel = S // NSA_SEL_LEN
    kb = k_s.reshape(B, nsel, NSA_SEL_LEN, G, D).transpose(0, 3, 1, 2, 4)
    vb = v_s.reshape(B, nsel, NSA_SEL_LEN, G, D).transpose(0, 3, 1, 2, 4)
    nqb = S // NSA_SEL_QBLOCK
    q_b = q.reshape(B, nqb, NSA_SEL_QBLOCK, G, HPG, D).transpose(1, 0, 2, 3, 4, 5)
    idx_b = sel_idx.reshape(B, G, nqb, NSA_SEL_QBLOCK, K).transpose(2, 0, 1, 3, 4)
    bi = jnp.arange(B)[:, None, None, None]
    gi = jnp.arange(G)[None, :, None, None]

    def one_block(args):
        i, qi, idx = args
        tq = i * NSA_SEL_QBLOCK + jnp.arange(NSA_SEL_QBLOCK)
        kg = kb[bi, gi, idx]
        vg = vb[bi, gi, idx]
        kpos = idx[..., None] * NSA_SEL_LEN + jnp.arange(NSA_SEL_LEN)
        mask = kpos <= tq[None, None, :, None, None]
        s = jnp.einsum('bqgid,bgqkld->bgiqkl', qi, kg).astype(jnp.float32) * NSA_DH ** -0.5
        s = jnp.where(mask[:, :, None], s, NEG)
        p = jax.nn.softmax(s.reshape(B, G, HPG, NSA_SEL_QBLOCK, K * NSA_SEL_LEN), axis=-1)
        p = p.reshape(s.shape).astype(vg.dtype)
        return jnp.einsum('bgiqkl,bgqkld->bqgid', p, vg)

    o = lax.map(one_block, (jnp.arange(nqb), q_b, idx_b))
    return o.transpose(1, 0, 2, 3, 4, 5).reshape(B, S, G, HPG, D)

def nsa_window(q, k_w, v_w):
    B, S, G, HPG, D = q.shape
    nb = S // Q_BLOCK
    span = NSA_WINDOW + Q_BLOCK
    kp = jnp.pad(k_w, ((0, 0), (NSA_WINDOW, 0), (0, 0), (0, 0)))
    vp = jnp.pad(v_w, ((0, 0), (NSA_WINDOW, 0), (0, 0), (0, 0)))
    q_b = q.reshape(B, nb, Q_BLOCK, G, HPG, D).transpose(1, 0, 2, 3, 4, 5)

    def one_block(args):
        i, qi = args
        start = i * Q_BLOCK
        kb = lax.dynamic_slice_in_dim(kp, start, span, axis=1)
        vb = lax.dynamic_slice_in_dim(vp, start, span, axis=1)
        tq = (start + jnp.arange(Q_BLOCK))[:, None]
        kpos = (start - NSA_WINDOW + jnp.arange(span))[None, :]
        mask = (kpos <= tq) & (kpos > tq - NSA_WINDOW) & (kpos >= 0)
        s = jnp.einsum('bqgid,bkgd->bgiqk', qi, kb).astype(jnp.float32) * NSA_DH ** -0.5
        p = jax.nn.softmax(jnp.where(mask, s, NEG), axis=-1).astype(vb.dtype)
        return jnp.einsum('bgiqk,bkgd->bqgid', p, vb)

    o = lax.map(one_block, (jnp.arange(nb), q_b))
    return o.transpose(1, 0, 2, 3, 4, 5).reshape(B, S, G, HPG, D)

def nsa_mixer(x, w_in, cmp_pos, w_ck1, w_ck2, w_cv1, w_cv2, gate_b, w_o):
    B, S, _ = x.shape
    h = x @ w_in
    q, kc, vc, ks, vs, kw, vw, g = jnp.split(h, NSA_SPLITS, axis=-1)
    q = q.reshape(B, S, NSA_GROUPS, NSA_HPG, NSA_DH)

    def kv(t):
        return t.reshape(B, S, NSA_GROUPS, NSA_DH)

    k_cmp = compress_kv(kv(kc), cmp_pos[0], w_ck1, w_ck2)
    v_cmp = compress_kv(kv(vc), cmp_pos[1], w_cv1, w_cv2)
    o_cmp, p_cmp = nsa_compressed(q, k_cmp, v_cmp)
    sel_idx = nsa_select_blocks(p_cmp)
    o_slc = nsa_selected(q, kv(ks), kv(vs), sel_idx)
    o_win = nsa_window(q, kv(kw), kv(vw))
    gates = jax.nn.sigmoid(g + gate_b).reshape(B, S, NSA_BRANCHES, NSA_GROUPS, NSA_HPG, 1)
    o = gates[:, :, 0] * o_cmp + gates[:, :, 1] * o_slc + gates[:, :, 2] * o_win
    return o.reshape(B, S, C_MIX) @ w_o

def hier_moe(x, w_rg, b_rg, w_re, b_re, w_gate, w_up, w_down):
    B, S, D = x.shape
    T = B * S
    xt = x.reshape(T, D)
    g_logits = (xt @ w_rg + b_rg).astype(jnp.float32)
    g_prob = jax.nn.softmax(g_logits, axis=-1)
    g_sel = jnp.argmax(g_logits, axis=-1)
    g_w = jnp.take_along_axis(g_prob, g_sel[:, None], axis=-1)
    e_logits = (xt @ w_re + b_re).astype(jnp.float32).reshape(T, MOE_GROUPS, MOE_EPG)
    e_sel = jnp.take_along_axis(e_logits, g_sel[:, None, None], axis=1)[:, 0]
    top_p, top_i = lax.top_k(jax.nn.softmax(e_sel, axis=-1), MOE_TOPK)
    top_p = top_p / top_p.sum(-1, keepdims=True)
    w_grp = (jax.nn.one_hot(top_i, MOE_EPG, dtype=jnp.float32) * top_p[..., None]).sum(1) * g_w
    y = jnp.zeros_like(xt)
    for gi in range(MOE_GROUPS):
        e0 = gi * MOE_EPG
        wg = jnp.where(g_sel[:, None] == gi, w_grp, 0.0).astype(x.dtype)
        hg = (jax.nn.silu(jnp.einsum('td,edf->tef', xt, w_gate[e0:e0 + MOE_EPG]))
              * jnp.einsum('td,edf->tef', xt, w_up[e0:e0 + MOE_EPG]))
        y = y + jnp.einsum('tef,efd->td', hg * wg[..., None], w_down[e0:e0 + MOE_EPG])
    return y.reshape(B, S, D)

def first_inputs(seed: int = 0) -> dict:
    key = jax.random.key(seed)
    keys = iter(jax.random.split(key, 48))

    def nrm(shape, scale):
        return jax.random.normal(next(keys), shape, jnp.float32) * scale

    def gain(shape):
        return 1.0 + nrm(shape, 0.1)

    x = nrm((BATCH, SEQ, D_MODEL), 1.0)
    offset = jax.random.randint(next(keys), (BATCH, 1), 0, 4096, dtype=jnp.int32)
    positions = (offset + jnp.arange(SEQ, dtype=jnp.int32)[None, :]).astype(jnp.int32)
    return {
        'x': x,
        'positions': positions,
        'ab_w_in': nrm((N_EVEN, D_MODEL, AB_IN), D_MODEL ** -0.5),
        'ab_gm_ln_g': gain((N_EVEN, GM_WIDTH)),
        'ab_gm_ln_b': nrm((N_EVEN, GM_WIDTH), 0.02),
        'ab_gm_ws': nrm((N_EVEN, GM_GROUPS, GM_CHUNK, GM_CHUNK), GM_CHUNK ** -0.5),
        'ab_gm_bs': gain((N_EVEN, GM_GROUPS, GM_CHUNK)),
        'ab_mla_q_norm': gain((N_EVEN, MLA_Q_RANK)),
        'ab_mla_kv_norm': gain((N_EVEN, MLA_KV_RANK)),
        'ab_mla_w_uq': nrm((N_EVEN, MLA_Q_RANK, MLA_HEADS * (MLA_NOPE + MLA_ROPE)), MLA_Q_RANK ** -0.5),
        'ab_mla_w_uk': nrm((N_EVEN, MLA_KV_RANK, MLA_HEADS * MLA_NOPE), MLA_KV_RANK ** -0.5),
        'ab_mla_w_uv': nrm((N_EVEN, MLA_KV_RANK, MLA_HEADS * MLA_V), MLA_KV_RANK ** -0.5),
        'ab_w_o': nrm((N_EVEN, AB_MIX, D_MODEL), AB_MIX ** -0.5 * DN_BETA),
        'c_w_in': nrm((N_ODD, D_MODEL, C_IN), D_MODEL ** -0.5),
        'c_cmp_pos': nrm((N_ODD, 2, NSA_CMP_LEN, NSA_DH), 0.1),
        'c_w_ck1': nrm((N_ODD, NSA_CMP_LEN * NSA_DH, NSA_CMP_HIDDEN), (NSA_CMP_LEN * NSA_DH) ** -0.5),
        'c_w_ck2': nrm((N_ODD, NSA_CMP_HIDDEN, NSA_DH), NSA_CMP_HIDDEN ** -0.5),
        'c_w_cv1': nrm((N_ODD, NSA_CMP_LEN * NSA_DH, NSA_CMP_HIDDEN), (NSA_CMP_LEN * NSA_DH) ** -0.5),
        'c_w_cv2': nrm((N_ODD, NSA_CMP_HIDDEN, NSA_DH), NSA_CMP_HIDDEN ** -0.5),
        'c_gate_b': nrm((N_ODD, NSA_BRANCHES * NSA_HEADS), 0.1),
        'c_w_o': nrm((N_ODD, C_MIX, D_MODEL), C_MIX ** -0.5 * DN_BETA),
        'moe_w_rg': nrm((DEPTH, D_MODEL, MOE_GROUPS), D_MODEL ** -0.5),
        'moe_b_rg': nrm((DEPTH, MOE_GROUPS), 0.01),
        'moe_w_re': nrm((DEPTH, D_MODEL, MOE_EXPERTS), D_MODEL ** -0.5),
        'moe_b_re': nrm((DEPTH, MOE_EXPERTS), 0.01),
        'moe_w_gate': nrm((DEPTH, MOE_EXPERTS, D_MODEL, MOE_HIDDEN), D_MODEL ** -0.5),
        'moe_w_up': nrm((DEPTH, MOE_EXPERTS, D_MODEL, MOE_HIDDEN), D_MODEL ** -0.5),
        'moe_w_down': nrm((DEPTH, MOE_EXPERTS, MOE_HIDDEN, D_MODEL), MOE_HIDDEN ** -0.5 * DN_BETA),
        'ln1_g': gain((DEPTH, D_MODEL)),
        'ln1_b': nrm((DEPTH, D_MODEL), 0.02),
        'ln2_g': gain((DEPTH, D_MODEL)),
        'ln2_b': nrm((DEPTH, D_MODEL), 0.02),
    }

def first_block(x, positions, ab_w_in, ab_gm_ln_g, ab_gm_ln_b, ab_gm_ws, ab_gm_bs,
              ab_mla_q_norm, ab_mla_kv_norm, ab_mla_w_uq, ab_mla_w_uk, ab_mla_w_uv, ab_w_o,
              c_w_in, c_cmp_pos, c_w_ck1, c_w_ck2, c_w_cv1, c_w_cv2, c_gate_b, c_w_o,
              moe_w_rg, moe_b_rg, moe_w_re, moe_b_re, moe_w_gate, moe_w_up, moe_w_down,
              ln1_g, ln1_b, ln2_g, ln2_b):
    for layer in range(DEPTH):
        j = layer // 2
        if layer % 2 == 0:
            mix = ab_mixer(x, positions, ab_w_in[j], ab_gm_ln_g[j], ab_gm_ln_b[j], ab_gm_ws[j],
                           ab_gm_bs[j], ab_mla_q_norm[j], ab_mla_kv_norm[j], ab_mla_w_uq[j],
                           ab_mla_w_uk[j], ab_mla_w_uv[j], ab_w_o[j])
        else:
            mix = nsa_mixer(x, c_w_in[j], c_cmp_pos[j], c_w_ck1[j], c_w_ck2[j], c_w_cv1[j],
                            c_w_cv2[j], c_gate_b[j], c_w_o[j])
        x = layer_norm(DN_ALPHA * x + mix, ln1_g[layer], ln1_b[layer])
        ffn = hier_moe(x, moe_w_rg[layer], moe_b_rg[layer], moe_w_re[layer], moe_b_re[layer],
                       moe_w_gate[layer], moe_w_up[layer], moe_w_down[layer])
        x = layer_norm(DN_ALPHA * x + ffn, ln2_g[layer], ln2_b[layer])
    return x


N_MEM = 256
MLSTM_HEADS = 4
MLSTM_HEAD_DIM = D_MODEL // 16
MLSTM_WIDTH = MLSTM_HEADS * MLSTM_HEAD_DIM
MLSTM_CHUNK = 64
MLSTM_CONV = 4
CONF_CHANNELS = D_MODEL // 4
CONF_KERNEL = 31
FOX_HEADS = 8
FOX_HEAD_DIM = D_MODEL // 16
FOX_WIDTH = FOX_HEADS * FOX_HEAD_DIM
FOX_BLOCK = 128
MIX_WIDTH = MLSTM_WIDTH + CONF_CHANNELS + FOX_WIDTH
XATTN_HEADS = 4
XATTN_HEAD_DIM = D_MODEL // 8
XATTN_WIDTH = XATTN_HEADS * XATTN_HEAD_DIM
D_FF = ((8 * D_MODEL // 3) + 255) // 256 * 256
N_EXPERTS = 8
TOP_K = 2
EXPERT_FF = D_FF
N_DENSE_LAYERS = (DEPTH + 1) // 2
N_MOE_LAYERS = DEPTH // 2
EPS = 1e-6

IN_SPLITS = (2 * MLSTM_WIDTH, MLSTM_WIDTH, MLSTM_WIDTH, MLSTM_HEADS, MLSTM_HEADS,
             2 * CONF_CHANNELS, FOX_WIDTH, FOX_WIDTH, FOX_WIDTH, FOX_HEADS)
IN_WIDTH = sum(IN_SPLITS)
IN_SPLIT_IDX = tuple(int(i) for i in np.cumsum(IN_SPLITS)[:-1])


def rmsnorm(x, w):
    xf = x.astype(jnp.float32)
    y = xf * lax.rsqrt(jnp.mean(xf * xf, axis=-1, keepdims=True) + EPS)
    return (y * w.astype(jnp.float32)).astype(x.dtype)

def layernorm_f32(x, w, b):
    mu = jnp.mean(x, axis=-1, keepdims=True)
    xc = x - mu
    var = jnp.mean(xc * xc, axis=-1, keepdims=True)
    return xc * lax.rsqrt(var + EPS) * w.astype(jnp.float32) + b.astype(jnp.float32)

def causal_dwconv(x, w, b):
    K, C = w.shape
    y = lax.conv_general_dilated(
        x, w.astype(jnp.float32)[:, None, :], window_strides=(1,), padding=[(K - 1, 0)],
        dimension_numbers=("NWC", "WIO", "NWC"), feature_group_count=C)
    return y + b.astype(jnp.float32)

def mlstm_chunkwise(q, k, v, i_pre, f_pre):
    B, S, H, Dh = q.shape
    L = MLSTM_CHUNK
    nc = S // L
    log_f = jax.nn.log_sigmoid(f_pre)
    log_i = i_pre

    def chunks(t):
        return t.reshape(B, nc, L, H, Dh).transpose(1, 0, 3, 2, 4)

    def gchunks(t):
        return t.reshape(B, nc, L, H).transpose(1, 0, 3, 2)

    causal = jnp.tril(jnp.ones((L, L), dtype=bool))

    def step(carry, xs):
        C, n, m = carry
        qc, kc, vc, lic, lfc = xs
        b = jnp.cumsum(lfc, axis=-1)
        d_log = b[..., :, None] - b[..., None, :] + lic[..., None, :]
        d_log = jnp.where(causal, d_log, -jnp.inf)
        inter = b + m[..., None]
        m_t = jnp.maximum(jnp.max(d_log, axis=-1), inter)
        s = jnp.einsum("bhtd,bhsd->bhts", qc, kc) * jnp.exp(d_log - m_t[..., None])
        w_inter = jnp.exp(inter - m_t)
        num = (jnp.einsum("bhts,bhsd->bhtd", s, vc)
               + w_inter[..., None] * jnp.einsum("bhtk,bhkv->bhtv", qc, C))
        den = jnp.sum(s, axis=-1) + w_inter * jnp.einsum("bhtk,bhk->bht", qc, n)
        h = num / jnp.maximum(jnp.abs(den), jnp.exp(-m_t))[..., None]
        b_tot = b[..., -1]
        g = b_tot[..., None] - b + lic
        m_new = jnp.maximum(b_tot + m, jnp.max(g, axis=-1))
        wg = jnp.exp(g - m_new[..., None])
        decay = jnp.exp(b_tot + m - m_new)
        C_new = decay[..., None, None] * C + jnp.einsum("bhsk,bhsv->bhkv", kc * wg[..., None], vc)
        n_new = decay[..., None] * n + jnp.einsum("bhs,bhsk->bhk", wg, kc)
        return (C_new, n_new, m_new), h

    init = (jnp.zeros((B, H, Dh, Dh), jnp.float32), jnp.zeros((B, H, Dh), jnp.float32),
            jnp.zeros((B, H), jnp.float32))
    _, hs = lax.scan(step, init, (chunks(q), chunks(k), chunks(v), gchunks(log_i), gchunks(log_f)))
    return hs.transpose(1, 0, 3, 2, 4).reshape(B, S, H, Dh)

def forgetting_attention(q, k, v, log_f):
    B, S, H, Dh = q.shape
    nb = S // FOX_BLOCK
    c = jnp.cumsum(log_f, axis=1).transpose(0, 2, 1)
    kh = k.transpose(0, 2, 1, 3)
    vh = v.transpose(0, 2, 1, 3)
    qb = (q * (Dh ** -0.5)).reshape(B, nb, FOX_BLOCK, H, Dh).transpose(1, 0, 3, 2, 4)
    cb = c.reshape(B, H, nb, FOX_BLOCK).transpose(2, 0, 1, 3)
    qpos = jnp.arange(S).reshape(nb, FOX_BLOCK)
    kpos = jnp.arange(S)

    def one_block(args):
        qi, ci, pi = args
        logits = jnp.einsum("bhqd,bhkd->bhqk", qi, kh) + ci[..., None] - c[:, :, None, :]
        logits = jnp.where(pi[:, None] >= kpos[None, :], logits, -jnp.inf)
        p = jax.nn.softmax(logits, axis=-1)
        return jnp.einsum("bhqk,bhkd->bhqd", p, vh)

    o = lax.map(one_block, (qb, cb, qpos))
    return o.transpose(1, 0, 3, 2, 4).reshape(B, S, H * Dh)

def hybrid_mixer(h, w_in, mlstm_conv_w, mlstm_conv_b, mlstm_b_i, mlstm_b_f, mlstm_norm_w,
                 conf_conv_w, conf_conv_b, conf_ln_w, conf_ln_b, fox_b_f, w_out):
    B, S, _ = h.shape
    z = jnp.einsum("bsd,de->bse", h, w_in).astype(jnp.float32)
    m_qk, m_v, m_o, m_i, m_f, c_glu, f_q, f_k, f_v, f_f = jnp.split(z, IN_SPLIT_IDX, axis=-1)

    qk = jax.nn.silu(causal_dwconv(m_qk, mlstm_conv_w, mlstm_conv_b))
    mq, mk = jnp.split(qk, 2, axis=-1)
    hd = (B, S, MLSTM_HEADS, MLSTM_HEAD_DIM)
    hm = mlstm_chunkwise(mq.reshape(hd), mk.reshape(hd) * (MLSTM_HEAD_DIM ** -0.5), m_v.reshape(hd),
                         m_i + mlstm_b_i.astype(jnp.float32), m_f + mlstm_b_f.astype(jnp.float32))
    hm = hm * lax.rsqrt(jnp.mean(hm * hm, axis=-1, keepdims=True) + EPS)
    hm = hm.reshape(B, S, MLSTM_WIDTH) * mlstm_norm_w.astype(jnp.float32) * jax.nn.sigmoid(m_o)

    a, g = jnp.split(c_glu, 2, axis=-1)
    hc = causal_dwconv(a * jax.nn.sigmoid(g), conf_conv_w, conf_conv_b)
    hc = jax.nn.silu(layernorm_f32(hc, conf_ln_w, conf_ln_b))

    fd = (B, S, FOX_HEADS, FOX_HEAD_DIM)
    log_f = jax.nn.log_sigmoid(f_f + fox_b_f.astype(jnp.float32))
    hf = forgetting_attention(f_q.reshape(fd), f_k.reshape(fd), f_v.reshape(fd), log_f)

    cat = jnp.concatenate([hm, hc, hf], axis=-1).astype(h.dtype)
    return jnp.einsum("bse,ed->bsd", cat, w_out)

def memory_cross_attention(h, mem_n, w_q, w_kv, w_o):
    B, S, _ = h.shape
    q = jnp.einsum("bsd,de->bse", h, w_q).reshape(B, S, XATTN_HEADS, XATTN_HEAD_DIM)
    kv = jnp.einsum("bmd,de->bme", mem_n, w_kv)
    k, v = jnp.split(kv, 2, axis=-1)
    k = k.reshape(B, N_MEM, XATTN_HEADS, XATTN_HEAD_DIM)
    v = v.reshape(B, N_MEM, XATTN_HEADS, XATTN_HEAD_DIM)
    logits = jnp.einsum("bshd,bmhd->bhsm", q.astype(jnp.float32), k.astype(jnp.float32))
    p = jax.nn.softmax(logits * (XATTN_HEAD_DIM ** -0.5), axis=-1)
    o = jnp.einsum("bhsm,bmhd->bshd", p, v.astype(jnp.float32)).reshape(B, S, XATTN_WIDTH)
    return jnp.einsum("bse,ed->bsd", o.astype(h.dtype), w_o)

def swiglu(h, w_gate, w_up, w_down):
    a = jnp.einsum("bsd,df->bsf", h, w_gate)
    u = jnp.einsum("bsd,df->bsf", h, w_up)
    return jnp.einsum("bsf,fd->bsd", jax.nn.silu(a) * u, w_down)

def moe_swiglu(h, router_w, w_gate, w_up, w_down):
    logits = jnp.einsum("bsd,de->bse", h, router_w).astype(jnp.float32)
    top_v, top_i = lax.top_k(logits, TOP_K)
    top_w = jax.nn.softmax(top_v, axis=-1)
    gates = jnp.sum(jax.nn.one_hot(top_i, N_EXPERTS, dtype=jnp.float32) * top_w[..., None], axis=-2)
    y = jnp.zeros(h.shape, jnp.float32)
    for e in range(N_EXPERTS):
        y = y + gates[..., e:e + 1] * swiglu(h, w_gate[e], w_up[e], w_down[e]).astype(jnp.float32)
    return y.astype(h.dtype)

def second_inputs(seed: int = 0) -> dict:
    key = jax.random.key(seed)
    ks = jax.random.split(key, 32)

    def nrm(k, shape, scale):
        return jax.random.normal(k, shape, jnp.float32) * scale

    D, L = D_MODEL, DEPTH
    return {
        "x": nrm(ks[0], (BATCH, SEQ, D), 1.0),
        "mem": nrm(ks[1], (BATCH, N_MEM, D), 1.0),
        "norm_mix_w": 1.0 + nrm(ks[2], (L, D), 0.02),
        "w_in": nrm(ks[3], (L, D, IN_WIDTH), D ** -0.5),
        "mlstm_conv_w": nrm(ks[4], (L, MLSTM_CONV, 2 * MLSTM_WIDTH), MLSTM_CONV ** -0.5),
        "mlstm_conv_b": nrm(ks[5], (L, 2 * MLSTM_WIDTH), 0.02),
        "mlstm_b_i": nrm(ks[6], (L, MLSTM_HEADS), 0.1),
        "mlstm_b_f": 3.0 + nrm(ks[7], (L, MLSTM_HEADS), 0.5),
        "mlstm_norm_w": 1.0 + nrm(ks[8], (L, MLSTM_WIDTH), 0.02),
        "conf_conv_w": nrm(ks[9], (L, CONF_KERNEL, CONF_CHANNELS), CONF_KERNEL ** -0.5),
        "conf_conv_b": nrm(ks[10], (L, CONF_CHANNELS), 0.02),
        "conf_ln_w": 1.0 + nrm(ks[11], (L, CONF_CHANNELS), 0.02),
        "conf_ln_b": nrm(ks[12], (L, CONF_CHANNELS), 0.02),
        "fox_b_f": 2.0 + nrm(ks[13], (L, FOX_HEADS), 0.5),
        "w_out": nrm(ks[14], (L, MIX_WIDTH, D), MIX_WIDTH ** -0.5),
        "norm_xattn_w": 1.0 + nrm(ks[15], (L, D), 0.02),
        "norm_mem_w": 1.0 + nrm(ks[16], (L, D), 0.02),
        "xattn_w_q": nrm(ks[17], (L, D, XATTN_WIDTH), D ** -0.5),
        "xattn_w_kv": nrm(ks[18], (L, D, 2 * XATTN_WIDTH), D ** -0.5),
        "xattn_w_o": nrm(ks[19], (L, XATTN_WIDTH, D), XATTN_WIDTH ** -0.5),
        "norm_ffn_w": 1.0 + nrm(ks[20], (L, D), 0.02),
        "ffn_w_gate": nrm(ks[21], (N_DENSE_LAYERS, D, D_FF), D ** -0.5),
        "ffn_w_up": nrm(ks[22], (N_DENSE_LAYERS, D, D_FF), D ** -0.5),
        "ffn_w_down": nrm(ks[23], (N_DENSE_LAYERS, D_FF, D), D_FF ** -0.5),
        "router_w": nrm(ks[24], (N_MOE_LAYERS, D, N_EXPERTS), D ** -0.5),
        "moe_w_gate": nrm(ks[25], (N_MOE_LAYERS, N_EXPERTS, D, EXPERT_FF), D ** -0.5),
        "moe_w_up": nrm(ks[26], (N_MOE_LAYERS, N_EXPERTS, D, EXPERT_FF), D ** -0.5),
        "moe_w_down": nrm(ks[27], (N_MOE_LAYERS, N_EXPERTS, EXPERT_FF, D), EXPERT_FF ** -0.5),
        "norm_final_w": 1.0 + nrm(ks[28], (D,), 0.02),
    }

def second_block(x, mem, norm_mix_w, w_in, mlstm_conv_w, mlstm_conv_b, mlstm_b_i, mlstm_b_f,
              mlstm_norm_w, conf_conv_w, conf_conv_b, conf_ln_w, conf_ln_b, fox_b_f, w_out,
              norm_xattn_w, norm_mem_w, xattn_w_q, xattn_w_kv, xattn_w_o, norm_ffn_w,
              ffn_w_gate, ffn_w_up, ffn_w_down, router_w, moe_w_gate, moe_w_up, moe_w_down,
              norm_final_w):
    for l in range(DEPTH):
        h = rmsnorm(x, norm_mix_w[l])
        x = x + hybrid_mixer(h, w_in[l], mlstm_conv_w[l], mlstm_conv_b[l], mlstm_b_i[l], mlstm_b_f[l],
                             mlstm_norm_w[l], conf_conv_w[l], conf_conv_b[l], conf_ln_w[l],
                             conf_ln_b[l], fox_b_f[l], w_out[l])
        h = rmsnorm(x, norm_xattn_w[l])
        mem_n = rmsnorm(mem, norm_mem_w[l])
        x = x + memory_cross_attention(h, mem_n, xattn_w_q[l], xattn_w_kv[l], xattn_w_o[l])
        h = rmsnorm(x, norm_ffn_w[l])
        if l % 2 == 0:
            j = l // 2
            x = x + swiglu(h, ffn_w_gate[j], ffn_w_up[j], ffn_w_down[j])
        else:
            j = l // 2
            x = x + moe_swiglu(h, router_w[j], moe_w_gate[j], moe_w_up[j], moe_w_down[j])
    return rmsnorm(x, norm_final_w)


def setup_inputs(seed=0):
    out = dict(first_inputs(seed))
    for name, value in second_inputs(seed + 1).items():
        if name != "x":
            out[name + "_2"] = value
    return out


def reference(
    x, positions, ab_w_in, ab_gm_ln_g, ab_gm_ln_b, ab_gm_ws, ab_gm_bs, ab_mla_q_norm,
    ab_mla_kv_norm, ab_mla_w_uq, ab_mla_w_uk, ab_mla_w_uv, ab_w_o, c_w_in, c_cmp_pos, c_w_ck1,
    c_w_ck2, c_w_cv1, c_w_cv2, c_gate_b, c_w_o, moe_w_rg, moe_b_rg, moe_w_re, moe_b_re,
    moe_w_gate, moe_w_up, moe_w_down, ln1_g, ln1_b, ln2_g, ln2_b, mem_2, norm_mix_w_2, w_in_2,
    mlstm_conv_w_2, mlstm_conv_b_2, mlstm_b_i_2, mlstm_b_f_2, mlstm_norm_w_2, conf_conv_w_2,
    conf_conv_b_2, conf_ln_w_2, conf_ln_b_2, fox_b_f_2, w_out_2, norm_xattn_w_2, norm_mem_w_2,
    xattn_w_q_2, xattn_w_kv_2, xattn_w_o_2, norm_ffn_w_2, ffn_w_gate_2, ffn_w_up_2,
    ffn_w_down_2, router_w_2, moe_w_gate_2, moe_w_up_2, moe_w_down_2, norm_final_w_2,
):
    x = first_block(
        x, positions, ab_w_in, ab_gm_ln_g, ab_gm_ln_b, ab_gm_ws, ab_gm_bs, ab_mla_q_norm,
        ab_mla_kv_norm, ab_mla_w_uq, ab_mla_w_uk, ab_mla_w_uv, ab_w_o, c_w_in, c_cmp_pos,
        c_w_ck1, c_w_ck2, c_w_cv1, c_w_cv2, c_gate_b, c_w_o, moe_w_rg, moe_b_rg, moe_w_re,
        moe_b_re, moe_w_gate, moe_w_up, moe_w_down, ln1_g, ln1_b, ln2_g, ln2_b,
    )
    return second_block(
        x, mem_2, norm_mix_w_2, w_in_2, mlstm_conv_w_2, mlstm_conv_b_2, mlstm_b_i_2,
        mlstm_b_f_2, mlstm_norm_w_2, conf_conv_w_2, conf_conv_b_2, conf_ln_w_2, conf_ln_b_2,
        fox_b_f_2, w_out_2, norm_xattn_w_2, norm_mem_w_2, xattn_w_q_2, xattn_w_kv_2,
        xattn_w_o_2, norm_ffn_w_2, ffn_w_gate_2, ffn_w_up_2, ffn_w_down_2, router_w_2,
        moe_w_gate_2, moe_w_up_2, moe_w_down_2, norm_final_w_2,
    )


_drawn_inputs = setup_inputs


def setup_inputs(seed=0):
    import zlib

    import numpy as np

    out = dict(_drawn_inputs(seed))
    spreads = {}
    factors = {'ab_gm_ln_b': 3.218,
     'ab_mla_q_norm': 4.335,
     'c_gate_b': 2.726,
     'mlstm_b_i_2': 45.608,
     'mlstm_norm_w_2': 3.019,
     'norm_xattn_w_2': 8.0,
     'norm_mem_w_2': 3.113,
     'norm_final_w_2': 8.411}
    for name, (base, spread) in spreads.items():
        noise = np.random.default_rng([zlib.crc32(name.encode()), seed]).standard_normal(out[name].shape)
        drawn = base * np.exp(spread * noise) if base else spread * noise
        out[name] = __import__('jax').numpy.asarray(drawn.astype(out[name].dtype))
    for name, factor in factors.items():
        out[name] = (out[name] * factor).astype(out[name].dtype)
    return out
```

```python
import math
from contextlib import ExitStack

import numpy as np

import concourse.bass as bass
from concourse import mybir

F32 = mybir.dt.float32
I32 = mybir.dt.int32
U32 = mybir.dt.uint32
ALU = mybir.AluOpType
ACT = mybir.ActivationFunctionType
AX_X = mybir.AxisListType.X

P = 128
TOK = 256
TT = TOK // P
D = 1024
KD = D // P
SLOT = 2048
RING = 12
NEG = -1e30
DEPTH = 2
DN_ALPHA = (2.0 * DEPTH) ** 0.25
LN_EPS = 1e-5
RMS_EPS = 1e-6


class Signal:

    def __init__(self, sem):
        self.sem, self.count, self.base = sem, 0, 0

    def up(self, n=1):
        self.count += n
        return self.sem, n

    def at(self, n):
        assert n > 0
        return self.sem, self.base + n

    def now(self):
        return self.sem, self.count


class WeightRing:

    def __init__(self, core):
        self.buf = core.sb("weight_ring", [P, RING, SLOT])
        self.full = [core.new_sem(f"weights_full_{i}") for i in range(RING)]
        self.used = core.new_sem("weights_used")
        self.loaded = [0] * RING
        self.tiles = 0
        self.plan = []

    def view(self, n, kt, cols):
        return self.buf[:, n % RING, 0:kt * cols].rearrange("p (k n) -> p k n", k=kt)

    def take(self, pe, src):
        kt, cols = src.shape[1], src.shape[2]
        n = self.tiles
        dst = self.view(n, kt, cols)
        self.plan.append(("tile", n, dst[0:src.shape[0]], src))
        self.tiles += 1
        self.loaded[n % RING] += 16
        pe.wait_ge(self.full[n % RING], self.loaded[n % RING])
        return dst


def k_tiles(w):
    return w.rearrange("(k p) n -> p k n", p=P)


class Core:

    def __init__(self, nc, ctx):
        self.nc, self.ctx = nc, ctx
        self.signals = {}
        self.order = []
        self.ended = 0
        self.names = {}

    def sb(self, name, shape, dt=F32, ctx=None):
        times = self.names[name] = self.names.get(name, 0) + 1
        return (ctx or self.ctx).enter_context(
            self.nc.sbuf_tensor(name if times == 1 else f"{name}_{times}", shape, dt))

    def new_sem(self, name):
        return self.ctx.enter_context(self.nc.semaphore(name))

    def sig(self, name):
        if name not in self.signals:
            self.signals[name] = Signal(self.new_sem(name))
        return self.signals[name]

    def link(self, eng, ins):
        name = {self.nc.vector: "dve", self.nc.scalar: "act", self.nc.gpsimd: "pool"}[eng]
        s = self.sig(f"{name}_step")
        ins.then_inc(*s.up())
        eng.wait_ge(*s.now())

    def dve(self, ins):
        self.link(self.nc.vector, ins)

    def act(self, ins):
        self.link(self.nc.scalar, ins)

    def pool(self, ins):
        self.link(self.nc.gpsimd, ins)

    def join(self):
        s = self.sig("stage_ended")
        self.ended += 1
        total = 4 * self.ended

        @self.block.tensor
        def _(pe):
            pe.drain().then_inc(*s.up())
            pe.wait_ge(s.sem, total)

        @self.block.scalar
        def _(act):
            act.drain().then_inc(*s.up())
            act.wait_ge(s.sem, total)

        @self.block.vector
        def _(dve):
            dve.drain().then_inc(*s.up())
            dve.wait_ge(s.sem, total)

        @self.block.gpsimd
        def _(pool):
            pool.drain().then_inc(*s.up())
            pool.wait_ge(s.sem, total)

        for x in self.signals.values():
            x.base = x.count


def constants(c):
    nc = c.nc
    c.ident = c.sb("ident", [P, P])
    c.tri01 = c.sb("tri01", [P, P])
    c.ones = c.sb("ones", [P, P])
    c.S = c.sb("scores", [P, 2, 8, TOK])
    c.PT = c.sb("probs_turned", [P, 2, 512])
    c.neg_max, c.row_sum = c.sb("neg_max", [P, 2, 8]), c.sb("row_sum", [P, 2, 8])
    c.recip = c.sb("recip", [P, 8])
    c.stats, c.rstd = c.sb("norm_stats", [P, 4, 8, 2]), c.sb("norm_rstd", [P, 4, 8, 1])
    c.var, c.newton = c.sb("norm_var", [P, 4, 8, 1]), c.sb("norm_newton", [P, 8, 1])
    c.bn = c.sb("norm_parts", [P, 8, 2, 6])
    c.gain, c.bias = c.sb("gain", [P, D]), c.sb("bias", [P, D])
    c.mask = c.sb("mask", [P, TOK])
    c.x = c.sb("x", [P, TT, D])
    c.xT = c.sb("xT", [P, KD, TOK])
    c.psum = c.ctx.enter_context(nc.psum_tensor("psum", [P, 8, 512], F32))
    x_landed = c.sig("params_landed")

    @c.block.gpsimd
    def _(pool):
        nc.gpsimd.memset(c.ident[:, :], 0.0)
        nc.gpsimd.memset(c.tri01[:, :], 1.0)
        nc.gpsimd.memset(c.ones[:, :], 1.0)
        c.pool(nc.gpsimd.memset(c.mask[:, :], 0.0))
        pool.drain()
        nc.gpsimd.affine_select(out=c.ident[:, :], in_=c.ident[:, :], compare_op=ALU.not_equal, fill=1.0,
                                base=0, pattern=[[-1, P]], channel_multiplier=1)
        nc.gpsimd.affine_select(out=c.tri01[:, :], in_=c.tri01[:, :], compare_op=ALU.is_ge, fill=0.0,
                                base=0, pattern=[[1, P]], channel_multiplier=-1)
        nc.gpsimd.affine_select(out=c.mask[:, :], in_=c.mask[:, :], compare_op=ALU.is_ge, fill=NEG,
                                base=P, pattern=[[-1, TOK]], channel_multiplier=1)

    @c.block.scalar
    def _(act):
        act.dma_start(c.x[:, :, :], c.arg["x"][0].rearrange("(t p) d -> p t d", p=P)).then_inc(*x_landed.up(16))
        act.wait_ge(*x_landed.now())
    c.join()


def load_params(c, items):
    landed = c.sig("params_landed")

    @c.block.scalar
    def _(act):
        for dst, src in items:
            act.dma_start(dst, src, allow_slow_non_contiguous=True).then_inc(*landed.up(16))
        act.wait_ge(*landed.now())


def bcast(v, n=P):
    return v.partition_broadcast(n)


def transpose_stage(c, groups, join=True):
    nc = c.nc
    turned, copied = c.sig("blocks_turned"), {"act": c.sig("turned_copied_act"), "dve": c.sig("turned_copied_dve")}

    @c.block.tensor
    def _(pe):
        for g, (ins, dst, who) in enumerate(groups):
            if g >= 8:
                w0 = groups[g - 8][2]
                pe.wait_ge(*copied[w0].at(sum(x[2] == w0 for x in groups[:g - 7])))
            for i, a in enumerate(ins):
                last = nc.tensor.transpose(c.psum[0:a.shape[1], g % 8, i * P:(i + 1) * P], a, c.ident[:, :])
            last.then_inc(*turned.up())

    def copies(eng, name, copy):
        for g, (ins, dst, who) in enumerate(groups):
            if who != name:
                continue
            w = ins[0].shape[1]
            src = c.psum[0:w, g % 8, 0:len(ins) * P]
            if len(dst.shape) == 3:
                src = src.rearrange("p (a b) -> p a b", a=dst.shape[1])
            eng.wait_ge(*turned.at(g + 1))
            copy(dst, src).then_inc(*copied[name].up())

    @c.block.scalar
    def _(act):
        copies(act, "act", lambda d, s: nc.scalar.activation(d, s, ACT.Copy))

    @c.block.vector
    def _(dve):
        copies(dve, "dve", nc.vector.tensor_copy)
    if join:
        c.join()


def rows_to_columns(c, src, dst, n, join=True):
    groups = []
    for k in range(0, n, 2):
        kk = min(2, n - k)
        ins = [src[:, t, j * P:(j + 1) * P] for j in range(k, k + kk) for t in range(TT)]
        groups.append((ins, dst[:, k:k + kk, :].rearrange("p k t -> p (k t)"), "dve" if k % 4 else "act"))
    transpose_stage(c, groups, join)


def norm_stage(c, items, join=True):
    nc = c.nc
    stats = c.stats
    have_stats, have_rstd = c.sig("norm_stats"), c.sig("norm_rstd")

    @c.block.vector
    def _(dve):
        for j, it in enumerate(items):
            n, w = it["src"].shape[1:]
            m = stats[:, j]
            for i in range(n):
                s = it["src"][:, i, :]
                if it["kind"] == "ln":
                    parts = max(1, w // 512)
                    for h in range(parts):
                        last = nc.vector.bn_stats(c.bn[:, i, h, :], s[:, h * (w // parts):(h + 1) * (w // parts)])
                    dve.drain()
                    nc.vector.bn_aggr(m[:, i, :], c.bn[:, i, 0:parts, :].rearrange("p a b -> p (a b)"))
                else:
                    nc.vector.tensor_tensor_reduce(it["dst"][:, i, :], s, s, 1.0 / w, 0.0, ALU.mult,
                                                   ALU.add, m[:, i, 1:2])
            dve.drain()
            nc.vector.tensor_scalar(c.var[:, j, 0:n, :], m[:, 0:n, 1:2], it["eps"], None, ALU.add).then_inc(*have_stats.up())

    @c.block.scalar
    def _(act):
        for j, it in enumerate(items):
            n = it["src"].shape[1]
            act.wait_ge(*have_stats.at(j + 1))
            nc.scalar.activation(c.rstd[:, j, 0:n, :], c.var[:, j, 0:n, :], ACT.Sqrt).then_inc(*have_rstd.up())

    @c.block.vector
    def _(dve):
        for j, it in enumerate(items):
            n, w = it["src"].shape[1:]
            dve.wait_ge(*have_rstd.at(j + 1))
            r, v, h = c.rstd[:, j, 0:n, :], c.var[:, j, 0:n, :], c.newton[:, 0:n, :]
            c.dve(nc.vector.reciprocal(r, r))
            c.dve(nc.vector.tensor_tensor(h, r, r, ALU.mult))
            c.dve(nc.vector.tensor_tensor(h, h, v, ALU.mult))
            c.dve(nc.vector.tensor_scalar(h, h, -0.5, 1.5, ALU.mult, ALU.add))
            c.dve(nc.vector.tensor_tensor(r, r, h, ALU.mult))
            for i in range(n):
                src, dst, r = it["src"][:, i, :], it["dst"][:, i, :], c.rstd[:, j, i, :]
                if it["kind"] == "rms":
                    if it["gain"] is None:
                        c.dve(nc.vector.tensor_scalar(dst, src, r, None, ALU.mult))
                    else:
                        c.dve(nc.vector.scalar_tensor_tensor(dst, src, r, it["gain"], ALU.mult, ALU.mult))
                    continue
                c.dve(nc.vector.tensor_scalar(dst, src, stats[:, j, i, 0:1], r, ALU.subtract, ALU.mult))
                c.dve(nc.vector.tensor_tensor(dst, dst, it["gain"], ALU.mult))
                c.dve(nc.vector.tensor_tensor(dst, dst, it["bias"], ALU.add))
    if join:
        c.join()


class Rows:

    def __init__(self, xT, w, n0, width, who, take):
        self.xT, self.w, self.n0, self.width, self.who, self.take = xT, w, n0, width, who, take

    def multiply(self, c, pe, pair):
        kt = self.w.shape[0] // P
        per = min(kt, SLOT // 512)
        src = k_tiles(self.w)
        for k0 in range(0, kt, per):
            w = c.ring.take(pe, src[:, k0:k0 + per, self.n0:self.n0 + self.width])
            for t in range(TT):
                for k in range(per):
                    last = c.nc.tensor.matmul(
                        c.psum[:, 2 * pair + t, 0:self.width], self.xT[:, k0 + k, t * P:(t + 1) * P],
                        w[:, k, :], start=(k0 + k == 0), stop=(k0 + k == kt - 1))
            last.then_inc(c.ring.used, 1)

    def out(self, c, pair):
        return c.psum[:, 2 * pair:2 * pair + 2, 0:self.width]


class Cols:

    def __init__(self, xT, w, n0, width, who, take):
        self.xT, self.w, self.n0, self.width, self.who, self.take = xT, w, n0, width, who, take

    def multiply(self, c, pe, pair):
        kt = self.w.shape[0] // P
        w = c.ring.take(pe, k_tiles(self.w)[:, :, self.n0:self.n0 + self.width])
        for m in range(self.width // P):
            for k in range(kt):
                last = c.nc.tensor.matmul(c.psum[:, 2 * pair, m * TOK:(m + 1) * TOK], w[:, k, m * P:(m + 1) * P],
                                          self.xT[:, k, :], start=(k == 0), stop=(k == kt - 1))
        last.then_inc(c.ring.used, 1)

    def out(self, c, pair):
        return c.psum[:, 2 * pair, 0:self.width // P * TOK].rearrange("p (m t) -> p m t", t=TOK)


def projection(c, jobs, join=True):
    ready = c.ring.used
    taken = {"act": c.sig("results_taken_act"), "dve": c.sig("results_taken_dve")}
    tile_of = []

    @c.block.tensor
    def _(pe):
        for j, job in enumerate(jobs):
            if j >= 4:
                w0 = jobs[j - 4].who
                pe.wait_ge(*taken[w0].at(sum(x.who == w0 for x in jobs[:j - 3])))
            job.multiply(c, pe, j % 4)
            tile_of.append(c.ring.tiles)

    def takes(eng, name):
        for j, job in enumerate(jobs):
            if job.who == name:
                eng.wait_ge(ready, tile_of[j])
                last = job.take(job.out(c, j % 4))
                last.then_inc(*taken[name].up())

    @c.block.scalar
    def _(act):
        takes(act, "act")

    @c.block.vector
    def _(dve):
        takes(dve, "dve")
    if join:
        c.join()


def heads_position(i, n, paired):
    return (n // 2) * (i % 2) + i // 2 if paired else i


def attention(c, batches, n, dv, q, k, v, out, scale, bias, paired=True, causal=True, gated=None, join=True):
    nc = c.nc
    S, PT = c.S, c.PT
    scored, scaled, maxed = c.sig("scores_ready"), c.sig("scores_scaled"), c.sig("maxima_ready")
    probs, turned, copied = c.sig("probs_ready"), c.sig("probs_turned"), c.sig("turned_probs_copied")
    pv_group, written = c.sig("pv_group_done"), c.sig("outputs_written")
    kts = [t + 1 if causal else TT for t, _ in batches]
    groups = []
    last_group = []
    for j, kt in enumerate(kts):
        blocks = [(i, s) for i in range(n) for s in range(kt)]
        groups += [(j, blocks[a:a + 4]) for a in range(0, len(blocks), 4)]
        last_group.append(len(groups))

    @c.block.tensor
    def _(pe):
        def scores(j):
            (t, b), nk = batches[j], kts[j] * P
            if j >= 1:
                pe.wait_ge(*scaled.at(j))
            for i in range(n):
                pos = heads_position(i, n, paired)
                last = nc.tensor.matmul(c.psum[:, pos // 2, (pos % 2) * TOK:(pos % 2) * TOK + nk],
                                        q(t, b, i), k(b, i, nk), start=True, stop=True)
            last.then_inc(*scored.up())

        def turn(g):
            j, blocks = groups[g]
            if g == 0 or groups[g - 1][0] != j:
                pe.wait_ge(*probs.at(j + 1))
            if g >= 2:
                pe.wait_ge(*copied.at(g - 1))
            for a, (i, s) in enumerate(blocks):
                pos = heads_position(i, n, paired)
                last = nc.tensor.transpose(c.psum[:, 4 + g % 2, a * P:(a + 1) * P],
                                           S[:, j % 2, pos, s * P:(s + 1) * P], c.ident[:, :])
            last.then_inc(*turned.up())

        def pv(g):
            j, blocks = groups[g]
            t, b = batches[j]
            pe.wait_ge(*copied.at(g + 1))
            if j >= 2:
                pe.wait_ge(*written.at(j - 1))
            for a, (i, s) in enumerate(blocks):
                last = nc.tensor.matmul(c.psum[:, 6 + j % 2, i * dv:(i + 1) * dv], PT[:, g % 2, a * P:(a + 1) * P],
                                        v(b, i, s), start=(s == 0), stop=(s == kts[j] - 1))
            last.then_inc(*pv_group.up())

        for j in range(len(batches) + 1):
            if j < len(batches):
                scores(j)
            if j >= 1:
                mine = [g for g in range(len(groups)) if groups[g][0] == j - 1]
                for g in mine:
                    turn(g)
                    if g > mine[0]:
                        pv(g - 1)
                pv(mine[-1])

    @c.block.scalar
    def _(act):
        for j in range(len(batches)):
            nk = kts[j] * P
            if gated is None:
                act.wait_ge(*maxed.at(j + 1))
                for pos in range(n):
                    last = nc.scalar.activation(S[:, j % 2, pos, 0:nk], S[:, j % 2, pos, 0:nk], ACT.Exp,
                                                bias=c.neg_max[:, j % 2, pos:pos + 1],
                                                accum_out=c.row_sum[:, j % 2, pos:pos + 1])
                last.then_inc(*probs.up())
            for g in [g for g in range(len(groups)) if groups[g][0] == j]:
                act.wait_ge(*turned.at(g + 1))
                if g >= 2:
                    act.wait_ge(*pv_group.at(g - 1))
                nc.scalar.activation(PT[:, g % 2, 0:len(groups[g][1]) * P],
                                     c.psum[:, 4 + g % 2, 0:len(groups[g][1]) * P], ACT.Copy).then_inc(*copied.up())

    @c.block.vector
    def _(dve):
        def finish(j):
            t, b = batches[j]
            dve.wait_ge(*pv_group.at(last_group[j]))
            r = c.row_sum[:, j % 2, 0:n]
            if gated is not None:
                c.dve(nc.vector.scalar_tensor_tensor(r, r, -1.0, r, ALU.mult, ALU.max))
                c.dve(nc.vector.tensor_tensor(r, r, gated[1](t), ALU.max))
            if j >= 1:
                dve.wait_ge(*written.at(j))
            c.dve(nc.vector.reciprocal(c.recip[:, 0:n], r))
            rr = c.recip[:, 0:n]
            o = c.psum[:, 6 + j % 2, 0:n * dv]
            if paired:
                rr = rr.rearrange("p (a b) -> p b a", a=2).unsqueeze(3).broadcast_to([P, n // 2, 2, dv])
                o = o.rearrange("p (b a d) -> p b a d", a=2, d=dv)
                dst = out(t, b).rearrange("p (b a) d -> p b a d", a=2)
            else:
                rr = rr.unsqueeze(2).broadcast_to([P, n, dv])
                o = o.rearrange("p (b d) -> p b d", d=dv)
                dst = out(t, b)
            nc.vector.tensor_tensor(dst, o, rr, ALU.mult).then_inc(*written.up())

        for j in range(len(batches)):
            (t, b), nk = batches[j], kts[j] * P
            dve.wait_ge(*scored.at(j + 1))
            if j >= 2:
                dve.wait_ge(*turned.at(last_group[j - 2]))
            sc = c.psum[:, 0:(n + 1) // 2, :].rearrange("p a (b k) -> p (a b) k", b=2)[:, 0:n, 0:nk]
            dst = S[:, j % 2, 0:n, 0:nk]
            if gated is not None:
                nc.vector.scalar_tensor_tensor(dst, sc, scale, gated[0](t, nk), ALU.mult, ALU.mult).then_inc(*scaled.up())
                dve.wait_ge(*scaled.now())
                nc.vector.tensor_reduce(c.row_sum[:, j % 2, 0:n], dst, AX_X, ALU.add).then_inc(*probs.up())
            else:
                if bias is None:
                    nc.vector.tensor_scalar(dst, sc, scale, None, ALU.mult).then_inc(*scaled.up())
                else:
                    nc.vector.scalar_tensor_tensor(dst, sc, scale, bias(t, b, nk), ALU.mult, ALU.add).then_inc(*scaled.up())
                dve.wait_ge(*scaled.now())
                nc.vector.tensor_reduce(c.neg_max[:, j % 2, 0:n], dst, AX_X, ALU.max, negate=True).then_inc(*maxed.up())
            if j >= 1:
                finish(j - 1)
        finish(len(batches) - 1)
    if join:
        c.join()



GM_W, GM_G = 512, 4
MLA_H, MLA_NOPE, MLA_ROPE, MLA_V = 8, 64, 32, 64
MLA_QK = MLA_NOPE + MLA_ROPE
MLA_QR, MLA_KVR = 256, 128
ROPE_BASE = 10000.0


def causal_bias(c, n):
    def bias(t, b, nk):
        m = c.mask[:, TOK - nk:TOK]
        return m.unsqueeze(1).broadcast_to([P, n, nk])
    return bias


def residual(c, xT, w, alpha, params=()):
    nc = c.nc
    if params:
        load_params(c, params)

    def add(n0):
        part = c.x[:, :, n0:n0 + 512]
        return lambda r: nc.vector.scalar_tensor_tensor(part, part, alpha, r, ALU.mult, ALU.add)
    projection(c, [Rows(xT, w, n0, 512, "dve", add(n0)) for n0 in (0, 512)])


def post_norm(c, gain, bias):
    norm_stage(c, [dict(src=c.x[:, :, :], dst=c.x[:, :, :], kind="ln", eps=LN_EPS, gain=c.gain[:, :],
                        bias=c.bias[:, :])])
    rows_to_columns(c, c.x, c.xT, KD)


def rope(c, x, cos, sin, tmp, shape):
    nc = c.nc
    x1, x2 = x
    a, b, e, f = tmp
    nc.vector.tensor_tensor(a, x1, cos, ALU.mult)
    nc.vector.tensor_tensor(b, x2, sin, ALU.mult)
    nc.vector.tensor_tensor(e, x1, sin, ALU.mult)
    c.dve(nc.vector.tensor_tensor(f, x2, cos, ALU.mult))
    nc.vector.drain()
    nc.vector.tensor_tensor(x1, a, b, ALU.subtract)
    c.dve(nc.vector.tensor_tensor(x2, e, f, ALU.add))


def ab_mixer(c, cat, ctx):
    nc, arg = c.nc, c.arg
    sb = lambda name, shape, dt=F32: c.sb("ab_" + name, shape, dt, ctx)
    half = MLA_ROPE // 2
    u, v = sb("u", [P, TT, GM_W]), sb("v", [P, TT, GM_W])
    low = sb("low", [P, TT, MLA_QR + MLA_KVR + MLA_ROPE])
    lown = sb("lown", [P, TT, MLA_QR + MLA_KVR])
    lowT = sb("lowT", [P, (MLA_QR + MLA_KVR) // P, TOK])
    gm_g, gm_b = sb("gm_g", [P, GM_W]), sb("gm_b", [P, GM_W])
    low_g = sb("low_g", [P, MLA_QR + MLA_KVR])
    bs = sb("bs", [P, GM_G])
    pos_i, pos = sb("pos_i", [P, TT], I32), sb("pos", [P, TT])
    freq, turns = sb("freq", [P, half]), sb("turns", [P, TT, half])
    ang, over = sb("ang", [P, 2, TT, half]), sb("over", [P, TT, half])
    trig = sb("trig", [P, 2, TT, half])
    wsT = sb("wsT", [P, GM_G, P])
    qrow, krow = sb("qrow", [P, TT, MLA_H, MLA_QK]), sb("krow", [P, TT, MLA_H, MLA_QK])
    vrow = sb("vrow", [P, TT, MLA_H * MLA_V])
    qT, kT = sb("qT", [P, MLA_H, TOK]), c.xT
    tmp = [sb(f"rot{i}", [P, MLA_H * half]) for i in range(4)]
    load_params(c, [
        (gm_g[:, :], bcast(arg["ab_gm_ln_g"][0])), (gm_b[:, :], bcast(arg["ab_gm_ln_b"][0])),
        (low_g[:, 0:MLA_QR], bcast(arg["ab_mla_q_norm"][0])), (low_g[:, MLA_QR:], bcast(arg["ab_mla_kv_norm"][0])),
        (bs[:, :], arg["ab_gm_bs"][0].rearrange("g t -> t g")),
        (pos_i[:, :], arg["positions"][0].rearrange("(t p) -> p t", p=P))])
    w_in = arg["ab_w_in"][0]
    projection(c, [
        Rows(c.xT, w_in, 0, 512, "act", lambda r: nc.scalar.activation(u[:, :, :], r, ACT.Gelu_apprx_tanh)),
        Rows(c.xT, w_in, 512, 512, "act", lambda r: nc.scalar.activation(v[:, :, :], r, ACT.Gelu_apprx_tanh)),
        Rows(c.xT, w_in, 1024, 416, "dve", lambda r: nc.vector.tensor_copy(low[:, :, :], r))])

    angles = c.sig("angles_ready")
    two_pi = 2 * math.pi
    c1 = 6.28125
    c2 = float(np.float32(round((two_pi - c1) * 2 ** 20) / 2 ** 20))
    c3 = float(np.float32(two_pi - c1 - c2))
    big = float(1.5 * 2 ** 23)
    pi_low = float(np.nextafter(np.float32(math.pi), np.float32(0)))

    @c.block.vector
    def _(dve):
        for i in range(half):
            f = float(np.exp(np.float32(-math.log(ROPE_BASE)) * np.float32(i) / np.float32(half), dtype=np.float32))
            nc.vector.memset(freq[:, i:i + 1], f)
        c.dve(nc.vector.tensor_copy(pos[:, :], pos_i[:, :]))
        dve.drain()
        for t in range(TT):
            last = nc.vector.tensor_scalar(ang[:, 0, t, :], freq[:, :], pos[:, t:t + 1], None, ALU.mult)
        c.dve(last)
        dve.drain()
        a = ang[:, 0]
        c.dve(nc.vector.tensor_scalar(turns[:, :, :], a, 1.0 / two_pi, big, ALU.mult, ALU.add))
        c.dve(nc.vector.tensor_scalar(turns[:, :, :], turns[:, :, :], big, None, ALU.subtract))
        for part in (c1, c2, c3):
            c.dve(nc.vector.scalar_tensor_tensor(a, turns[:, :, :], -part, a, ALU.mult, ALU.add))
        c.dve(nc.vector.tensor_scalar(ang[:, 1], a, math.pi / 2, None, ALU.add))
        c.dve(nc.vector.tensor_scalar(over[:, :, :], ang[:, 1], math.pi, None, ALU.is_gt))
        c.dve(nc.vector.scalar_tensor_tensor(ang[:, 1], over[:, :, :], -two_pi, ang[:, 1], ALU.mult, ALU.add))
        both = ang[:, :, :, :].rearrange("p a t f -> p (a t f)")
        nc.vector.tensor_scalar(both, both, pi_low, -pi_low, ALU.min, ALU.max).then_inc(*angles.up())

    @c.block.scalar
    def _(act):
        act.wait_ge(*angles.at(1))
        nc.scalar.activation(trig[:, :, :, :], ang[:, :, :, :], ACT.Sin)

    ws_turned, ws_masked = c.sig("spatial_turned"), c.sig("spatial_masked")

    @c.block.tensor
    def _(pe):
        ws = c.ring.take(pe, arg["ab_gm_ws"][0].rearrange("g t s -> t g s"))
        for g in range(GM_G):
            last = nc.tensor.transpose(c.psum[:, 0, g * P:(g + 1) * P], ws[:, g, :], c.ident[:, :])
        last.then_inc(c.ring.used, 1)
        c.ws_tile = c.ring.tiles

    @c.block.vector
    def _(dve):
        dve.wait_ge(c.ring.used, c.ws_tile)
        nc.vector.tensor_tensor(wsT[:, :, :], c.psum[:, 0, :].rearrange("p (g t) -> p g t", g=GM_G),
                                c.tri01[:, :].unsqueeze(1).broadcast_to([P, GM_G, P]), ALU.mult)
    norm_stage(c, [
        dict(src=v[:, :, :], dst=v[:, :, :], kind="ln", eps=LN_EPS, gain=gm_g[:, :], bias=gm_b[:, :]),
        dict(src=low[:, :, 0:MLA_QR], dst=lown[:, :, 0:MLA_QR], kind="rms", eps=LN_EPS, gain=low_g[:, 0:MLA_QR], bias=None),
        dict(src=low[:, :, MLA_QR:MLA_QR + MLA_KVR], dst=lown[:, :, MLA_QR:], kind="rms", eps=LN_EPS,
             gain=low_g[:, MLA_QR:], bias=None)])
    rows_to_columns(c, lown, lowT, 3)

    mixed = c.sig("spatial_mixed")

    @c.block.tensor
    def _(pe):
        for t in range(TT):
            for g in range(GM_G):
                last = nc.tensor.matmul(c.psum[:, t, g * P:(g + 1) * P], wsT[:, g, :], v[:, t, g * P:(g + 1) * P],
                                        start=True, stop=True)
            last.then_inc(*mixed.up())

    @c.block.vector
    def _(dve):
        for t in range(TT):
            dve.wait_ge(*mixed.at(t + 1))
            for g in range(GM_G):
                s = slice(g * P, (g + 1) * P)
                nc.vector.scalar_tensor_tensor(cat[:, t, s], c.psum[:, t, s], bs[:, g:g + 1], u[:, t, s],
                                               ALU.add, ALU.mult)
    c.join()

    qf = qrow[:, :, :, :].rearrange("p t h d -> p t (h d)")

    def keep_keys(r):
        for t in range(TT):
            last = nc.vector.tensor_copy(krow[:, t, :, 0:MLA_NOPE], r[:, t, :].rearrange("p (h d) -> p h d", h=MLA_H))
            if t == 0:
                c.dve(last)
        return last
    projection(c, [
        Rows(lowT[:, 0:2, :], arg["ab_mla_w_uq"][0], 0, 512, "act", lambda r: nc.scalar.activation(qf[:, :, 0:512], r, ACT.Copy)),
        Rows(lowT[:, 0:2, :], arg["ab_mla_w_uq"][0], 512, 256, "act", lambda r: nc.scalar.activation(qf[:, :, 512:768], r, ACT.Copy)),
        Rows(lowT[:, 2:3, :], arg["ab_mla_w_uk"][0], 0, 512, "dve", keep_keys),
        Rows(lowT[:, 2:3, :], arg["ab_mla_w_uv"][0], 0, 512, "act", lambda r: nc.scalar.activation(vrow[:, :, :], r, ACT.Copy))])

    @c.block.vector
    def _(dve):
        kr = low[:, :, MLA_QR + MLA_KVR:]
        for t in range(TT):
            cos, sin = (trig[:, i, t, :].unsqueeze(1).broadcast_to([P, MLA_H, half]) for i in (1, 0))
            q = qrow[:, t, :, MLA_NOPE:]
            rope(c, (q[:, :, 0:half], q[:, :, half:]), cos, sin,
                 [x[:, :].rearrange("p (h d) -> p h d", h=MLA_H) for x in tmp], None)
            rope(c, (kr[:, t, 0:half], kr[:, t, half:]), trig[:, 1, t, :], trig[:, 0, t, :], [x[:, 0:half] for x in tmp], None)
            dve.drain()
            nc.vector.tensor_copy(krow[:, t, :, MLA_NOPE:], kr[:, t, :].unsqueeze(1).broadcast_to([P, MLA_H, MLA_ROPE]))
    c.join()
    transpose_stage(c, [([row[:, t, h, :] for h in (2 * g, 2 * g + 1) for t in range(TT)],
                         colT[0:MLA_QK, 2 * g:2 * g + 2, :].rearrange("p h t -> p (h t)"), who)
                        for row, colT, who in ((qrow, qT, "act"), (krow, kT, "dve")) for g in range(MLA_H // 2)])
    attention(c, [(t, 0) for t in range(TT)], MLA_H, MLA_V,
              q=lambda t, b, i: qT[0:MLA_QK, i, t * P:(t + 1) * P], k=lambda b, i, nk: kT[0:MLA_QK, i, 0:nk],
              v=lambda b, i, s: vrow[:, s, i * MLA_V:(i + 1) * MLA_V],
              out=lambda t, b: cat[:, t, GM_W:].rearrange("p (h d) -> p h d", h=MLA_H),
              scale=MLA_QK ** -0.5, bias=causal_bias(c, MLA_H), paired=False)



NSA_H, NSA_G, NSA_D = 16, 2, 64
NSA_HPG = NSA_H // NSA_G
CMP_LEN, CMP_STRIDE, CMP_HID = 32, 16, 256
NCMP = TOK // CMP_STRIDE - CMP_LEN // CMP_STRIDE + 1
C_MIX = NSA_H * NSA_D
NSA_KV = NSA_G * NSA_D
assert TOK // 64 <= 8 and TOK <= 512


def nsa_mixer(c, cat, ctx):
    nc, arg = c.nc, c.arg
    sb = lambda name, shape, dt=F32: c.sb("c_" + name, shape, dt, ctx)
    qT = sb("qT", [P, NSA_H // 2, TOK])
    kvT = sb("kvT", [P, 4, NSA_G, TOK])
    vs, vwg = sb("vs", [P, TT, NSA_KV]), sb("vwg", [P, TT, NSA_KV + 3 * NSA_H])
    blocks = sb("blocks", [P, 2, CMP_LEN // 2, NSA_G, NCMP])
    pos = sb("pos", [P, 2, CMP_LEN // 2])
    hid = sb("hid", [P, 2, CMP_HID // P, NSA_G * NCMP])
    w2 = sb("w2", [P, 2, CMP_HID // P, NSA_D])
    kc = sb("kc", [P, NSA_G * NCMP])
    vc = sb("vc", [NCMP, NSA_G, NSA_D])
    gate_b, gates = sb("gate_b", [P, 3 * NSA_H]), sb("gates", [P, TT, 3 * NSA_H])
    ends, ends01 = sb("ends", [P, TT, NCMP]), sb("ends01", [P, TT, NCMP])
    oc, osel = sb("oc", [P, TT, C_MIX]), sb("osel", [P, TT, C_MIX])
    pcT = sb("pcT", [NCMP, 2, NSA_HPG, P])
    sc = sb("sc", [P, TT, NSA_H, NCMP])
    red = sb("red", [P, TT, NSA_H])
    posv = arg["c_cmp_pos"][0].rearrange("i (j a) d -> a d i j", a=2)
    load_params(c, [(gate_b[:, :], bcast(arg["c_gate_b"][0])),
                    (w2[:, 0], k_tiles(arg["c_w_ck2"][0])), (w2[:, 1], k_tiles(arg["c_w_cv2"][0]))] +
                [(pos[a * 64:(a + 1) * 64, i, :], posv[a, :, i, :]) for a in range(2) for i in range(2)])

    @c.block.gpsimd
    def _(pool):
        nc.gpsimd.memset(ends[:, :, :], 0.0)
        c.pool(nc.gpsimd.memset(ends01[:, :, :], 1.0))
        pool.drain()
        for t in range(TT):
            for m, fill in ((ends, NEG), (ends01, 0.0)):
                nc.gpsimd.affine_select(out=m[:, t, :], in_=m[:, t, :], compare_op=ALU.is_ge, fill=fill,
                                        base=t * P - CMP_LEN + 1, pattern=[[-CMP_STRIDE, NCMP]], channel_multiplier=1)
    w_in = arg["c_w_in"][0]
    act_copy = lambda dst: (lambda r: nc.scalar.activation(dst, r, ACT.Copy))
    dve_copy = lambda dst: (lambda r: nc.vector.tensor_copy(dst, r))
    at = lambda i: C_MIX + i * NSA_KV

    def spread(i, copy):
        def take(r):
            for g in range(NSA_G):
                for a in range(2):
                    last = copy(kvT[a * 64:(a + 1) * 64, i, g, :], r[g * 64:(g + 1) * 64, 0, :])
            return last
        return take
    projection(c, [
        Cols(c.xT, w_in, at(0), NSA_KV, "act", spread(0, lambda d, r: nc.scalar.activation(d, r, ACT.Copy))),
        Cols(c.xT, w_in, at(1), NSA_KV, "dve", spread(1, nc.vector.tensor_copy)),
        Cols(c.xT, w_in, at(2), NSA_KV, "act", spread(2, lambda d, r: nc.scalar.activation(d, r, ACT.Copy))),
        Cols(c.xT, w_in, at(4), NSA_KV, "dve", spread(3, nc.vector.tensor_copy)),
        Rows(c.xT, w_in, at(3), NSA_KV, "act", act_copy(vs[:, :, :])),
        Rows(c.xT, w_in, at(5), NSA_KV + 3 * NSA_H, "dve", dve_copy(vwg[:, :, :]))] + [
        Cols(c.xT, w_in, j * 256, 256, "dve" if j % 2 else "act",
             (dve_copy if j % 2 else act_copy)(qT[:, 2 * j:2 * j + 2, :])) for j in range(4)])

    pair = CMP_LEN // 2
    built, hidden, squashed, compressed = c.sig("blocks_built"), c.sig("cmp_hidden"), c.sig("cmp_squashed"), c.sig("cmp_ready")

    @c.block.vector
    def _(dve):
        for i in range(2):
            for a in range(2):
                h = slice(a * 64, (a + 1) * 64)
                for g in range(NSA_G):
                    src = kvT[h, i, g, :].rearrange("p (m r) -> p r m", r=CMP_STRIDE)
                    for half in range(2):
                        js = slice(half * 8, half * 8 + 8)
                        last = nc.vector.tensor_tensor(
                            blocks[h, i, js, g, :], src[:, a:CMP_STRIDE:2, half:half + NCMP],
                            pos[h, i, js].unsqueeze(2).broadcast_to([64, 8, NCMP]), ALU.add)
            dve.drain().then_inc(*built.up())
        for t in range(TT):
            last = nc.vector.tensor_tensor(gates[:, t, :], vwg[:, t, NSA_KV:], gate_b[:, :], ALU.add)
        dve.drain().then_inc(*built.up())

    @c.block.tensor
    def _(pe):
        for i, name in enumerate(("c_w_ck1", "c_w_cv1")):
            pe.wait_ge(*built.at(i + 1))
            src = k_tiles(arg[name][0])
            for m in range(2):
                w1 = c.ring.take(pe, src[:, :, m * P:(m + 1) * P])
                for j in range(pair):
                    last = nc.tensor.matmul(c.psum[:, 2 * i + m, 0:NSA_G * NCMP], w1[:, j, :],
                                            blocks[:, i, j].rearrange("p g n -> p (g n)"), start=(j == 0), stop=(j == pair - 1))
                last.then_inc(c.ring.used, 1)
        c.cmp_tile = c.ring.tiles
        pe.wait_ge(*squashed.at(1))
        for m in range(2):
            last = nc.tensor.matmul(c.psum[0:64, 4, 0:NSA_G * NCMP], w2[:, 0, m, :], hid[:, 0, m, :], start=(m == 0), stop=(m == 1))
        last.then_inc(*compressed.up())
        for m in range(2):
            last = nc.tensor.matmul(c.psum[64:128, 5, 0:NSA_G * NCMP], w2[:, 0, m, :], hid[:, 0, m, :], start=(m == 0), stop=(m == 1))
        last.then_inc(*compressed.up())
        for g in range(NSA_G):
            for m in range(2):
                last = nc.tensor.matmul(c.psum[0:NCMP, 6 + g, 0:NSA_D], hid[:, 1, m, g * NCMP:(g + 1) * NCMP], w2[:, 1, m, :],
                                        start=(m == 0), stop=(m == 1))
        last.then_inc(*compressed.up())

    @c.block.scalar
    def _(act):
        act.wait_ge(c.ring.used, c.cmp_tile)
        for i in range(2):
            last = nc.scalar.activation(hid[:, i], c.psum[:, 2 * i:2 * i + 2, 0:NSA_G * NCMP], ACT.Gelu_apprx_tanh)
        act.drain().then_inc(*squashed.up())
        act.wait_ge(*built.at(3))
        nc.scalar.activation(gates[:, :, :], gates[:, :, :], ACT.Sigmoid)

    @c.block.vector
    def _(dve):
        dve.wait_ge(*compressed.at(3))
        nc.vector.tensor_copy(kc[0:64, :], c.psum[0:64, 4, 0:NSA_G * NCMP])
        nc.vector.tensor_copy(kc[64:128, :], c.psum[64:128, 5, 0:NSA_G * NCMP])
        for g in range(NSA_G):
            nc.vector.tensor_copy(vc[:, g, :], c.psum[0:NCMP, 6 + g, 0:NSA_D])
    c.join()

    scored, softened = c.sig("cmp_scores"), c.sig("cmp_probs")
    exped = c.sig("cmp_exp")
    in_exp = c.sig("cmp_centred")

    @c.block.tensor
    def _(pe):
        for t in range(TT):
            for h in range(NSA_H):
                g, a = h // NSA_HPG, h % 2
                rows = slice(a * 64, a * 64 + 64)
                last = nc.tensor.matmul(c.psum[:, 2 * a + t, (h // 2) * NCMP:(h // 2 + 1) * NCMP],
                                        qT[rows, h // 2, t * P:(t + 1) * P], kc[rows, g * NCMP:(g + 1) * NCMP], start=True, stop=True)
        last.then_inc(*scored.up())

    @c.block.vector
    def _(dve):
        dve.wait_ge(*scored.at(1))
        for t in range(TT):
            for a in range(2):
                nc.vector.scalar_tensor_tensor(
                    sc[:, t, a:NSA_H:2, :], c.psum[:, 2 * a + t, 0:8 * NCMP].rearrange("p (h n) -> p h n", n=NCMP), NSA_D ** -0.5,
                    ends[:, t, :].unsqueeze(1).broadcast_to([P, 8, NCMP]), ALU.mult, ALU.add)
        dve.drain()
        c.dve(nc.vector.tensor_reduce(red[:, :, :], sc[:, :, :, :], AX_X, ALU.max))
        nc.vector.tensor_tensor(sc[:, :, :, :], sc[:, :, :, :], red[:, :, :].unsqueeze(3).broadcast_to([P, TT, NSA_H, NCMP]),
                                ALU.subtract).then_inc(*in_exp.up())
        dve.wait_ge(*exped.at(1))
        c.dve(nc.vector.tensor_reduce(red[:, :, :], sc[:, :, :, :], AX_X, ALU.add))
        c.dve(nc.vector.reciprocal(red[:, :, :], red[:, :, :]))
        c.dve(nc.vector.tensor_tensor(sc[:, :, :, :], sc[:, :, :, :], red[:, :, :].unsqueeze(3).broadcast_to([P, TT, NSA_H, NCMP]), ALU.mult))
        nc.vector.tensor_tensor(sc[:, :, :, :], sc[:, :, :, :], ends01[:, :, :].unsqueeze(2).broadcast_to([P, TT, NSA_H, NCMP]),
                                ALU.mult).then_inc(*softened.up())

    @c.block.scalar
    def _(act):
        act.wait_ge(*in_exp.at(1))
        nc.scalar.activation(sc[:, :, :, :], sc[:, :, :, :], ACT.Exp).then_inc(*exped.up())

    turned, copied, out_ready, taken = c.sig("cmp_turned"), c.sig("cmp_copied"), c.sig("cmp_out"), c.sig("cmp_taken")

    @c.block.tensor
    def _(pe):
        pe.wait_ge(*softened.at(1))
        for t in range(TT):
            for g in range(NSA_G):
                j = 2 * t + g
                if j >= 2:
                    pe.wait_ge(*copied.at(j - 1))
                for i in range(NSA_HPG):
                    last = nc.tensor.transpose(c.psum[0:NCMP, 4 + 2 * (j % 2) + i // 4, (i % 4) * P:(i % 4 + 1) * P],
                                               sc[:, t, g * NSA_HPG + i, :], c.ident[:, :])
                last.then_inc(*turned.up())
                pe.wait_ge(*copied.at(j + 1))
                if j >= 4:
                    pe.wait_ge(*taken.at(j - 3))
                for i in range(NSA_HPG):
                    last = nc.tensor.matmul(c.psum[:, j, i * NSA_D:(i + 1) * NSA_D], pcT[:, j % 2, i, :], vc[:, g, :], start=True, stop=True)
                last.then_inc(*out_ready.up())

    @c.block.vector
    def _(dve):
        for j in range(4):
            t, g = j // 2, j % 2
            dve.wait_ge(*turned.at(j + 1))
            if j >= 2:
                dve.wait_ge(*out_ready.at(j - 1))
            b0 = [4, 6][j % 2]
            nc.vector.tensor_copy(pcT[:, j % 2].rearrange("p (b i) t -> p b (i t)", b=2), c.psum[0:NCMP, b0:b0 + 2, :]).then_inc(*copied.up())
            dve.wait_ge(*out_ready.at(j + 1))
            gt = gates[:, t, g * 8:g * 8 + 8].unsqueeze(2).broadcast_to([P, 8, NSA_D])
            nc.vector.tensor_tensor(oc[:, t, g * 512:(g + 1) * 512].rearrange("p (h d) -> p h d", d=NSA_D),
                                    c.psum[:, j, :].rearrange("p (h d) -> p h d", d=NSA_D), gt, ALU.mult).then_inc(*taken.up())
    c.join()
    for branch, (ki, vals) in enumerate(((2, vs), (3, vwg))):
        attention(c, [(t, g) for t in range(TT) for g in range(NSA_G)], NSA_HPG, NSA_D,
                  q=lambda t, g, i: qT[(i % 2) * 64:(i % 2) * 64 + 64, g * 4 + i // 2, t * P:(t + 1) * P],
                  k=lambda g, i, nk: kvT[(i % 2) * 64:(i % 2) * 64 + 64, ki, g, 0:nk],
                  v=lambda g, i, s: vals[:, s, g * NSA_D:(g + 1) * NSA_D],
                  out=lambda t, g: (osel, cat)[branch][:, t, g * 512:(g + 1) * 512].rearrange("p (h d) -> p h d", h=8),
                  scale=NSA_D ** -0.5, bias=causal_bias(c, 8))

    @c.block.vector
    def _(dve):
        for branch, o in ((1, osel), (2, cat)):
            for t in range(TT):
                gt = gates[:, t, branch * 16:branch * 16 + 16].unsqueeze(2).broadcast_to([P, 16, NSA_D])
                ov = o[:, t, :].rearrange("p (h d) -> p h d", d=NSA_D)
                nc.vector.tensor_tensor(ov, ov, gt, ALU.mult)
            dve.drain()
            nc.vector.tensor_tensor(o[:, :, :], o[:, :, :], (oc, osel)[branch - 1][:, :, :], ALU.add)
            dve.drain()
    c.join()



CH = 256


def stream_ffn(c, n, gate, up, down, weight, ctx):
    nc, ring = c.nc, c.ring
    y = c.y
    squashed = c.sb("ffn_squashed", [P, 2, 2 * TOK], ctx=ctx)
    hidden = c.sb("ffn_hidden", [P, 2, 2, TOK], ctx=ctx)
    gate_squashed, hidden_ready, added = c.sig("gate_squashed"), c.sig("hidden_ready"), c.sig("chunk_added")
    p0 = ring.tiles
    loaded0 = list(ring.loaded)
    ring.plan.append(("stream", p0, n, gate, up, down))
    ring.tiles += 3 * n
    for x in range(p0, p0 + 3 * n):
        ring.loaded[x % RING] += 16
    FIRST, U = 1, 4
    loops = max(0, (n - 1 - FIRST) // U)
    rest = range(FIRST + U * loops, n - 1)

    def nth_load(x):
        first = x - (x - p0) // RING * RING
        return loaded0[x % RING] + 16 * ((x - first) // RING + 1)

    def gate_tile(j):
        return p0 if j == 0 else p0 + 2 + 3 * (j - 1)

    def up_tile(j):
        return gate_tile(j) + 1

    def down_tile(j):
        return p0 + 2 + 3 * j + (2 if j < n - 1 else 0)

    def two_products(pe, j, i):
        if j >= 2:
            pe.wait_ge(hidden_ready.sem, hidden_ready.base + (j - 1) + U * i)
        for tile, bank in ((gate_tile(j), 0), (up_tile(j), 2)):
            pe.wait_ge(ring.full[tile % RING], nth_load(tile) + 16 * i)
            w = ring.view(tile, KD, CH)
            for m in range(2):
                for k in range(KD):
                    last = nc.tensor.matmul(c.psum[:, bank + j % 2, m * TOK:(m + 1) * TOK], w[:, k, m * P:(m + 1) * P],
                                            c.xT[:, k, :], start=(k == 0), stop=(k == KD - 1))
            last.then_inc(ring.used, 1)

    def third_product(pe, j, i):
        tile = down_tile(j)
        pe.wait_ge(hidden_ready.sem, hidden_ready.base + j + 1 + U * i)
        if j >= 1:
            pe.wait_ge(added.sem, added.base + 2 * j + 2 * U * i)
        pe.wait_ge(ring.full[tile % RING], nth_load(tile) + 16 * i)
        w = ring.view(tile, 2, D)
        for t in range(TT):
            for h in range(2):
                for m in range(2):
                    last = nc.tensor.matmul(c.psum[:, 4 + 2 * t + h, :], hidden[:, j % 2, m, t * P:(t + 1) * P],
                                            w[:, m, h * 512:(h + 1) * 512], start=(m == 0), stop=(m == 1))
        last.then_inc(ring.used, 1)

    def squash(act, j, i):
        act.wait_ge(ring.used, gate_tile(j) + 1 + 3 * U * i)
        nc.scalar.activation(squashed[:, j % 2, :], c.psum[:, j % 2, :], ACT.Silu).then_inc(gate_squashed.sem, 1)

    def combine(dve, j, i):
        dve.wait_ge(ring.used, up_tile(j) + 1 + 3 * U * i)
        dve.wait_ge(gate_squashed.sem, gate_squashed.base + j + 1 + U * i)
        nc.vector.tensor_tensor(hidden[:, j % 2].rearrange("p m t -> p (m t)"), squashed[:, j % 2, :],
                                c.psum[:, 2 + j % 2, :], ALU.mult).then_inc(hidden_ready.sem, 1)

    def add(dve, j, jj, i):
        dve.wait_ge(ring.used, down_tile(j) + 1 + 3 * U * i)
        for t in range(TT):
            part = c.psum[:, 4 + 2 * t:6 + 2 * t, :].rearrange("p h n -> p (h n)")
            if j >= 1:
                dve.wait_ge(added.sem, added.base + 2 * j - 1 + t + 2 * U * i)
            if weight is None:
                last = nc.vector.tensor_tensor(y[:, t, :], part, y[:, t, :], ALU.add)
            else:
                last = nc.vector.scalar_tensor_tensor(y[:, t, :], part, weight(t, jj), y[:, t, :], ALU.mult, ALU.add)
            last.then_inc(added.sem, 1)

    @c.block.tensor
    def _(pe):
        two_products(pe, 0, 0)
        for j in range(FIRST):
            two_products(pe, j + 1, 0)
            third_product(pe, j, 0)
        if loops:
            with pe.Fori(0, loops) as i:
                for j in range(FIRST, FIRST + U):
                    two_products(pe, j + 1, i)
                    third_product(pe, j, i)
        for j in rest:
            two_products(pe, j + 1, 0)
            third_product(pe, j, 0)
        third_product(pe, n - 1, 0)

    @c.block.scalar
    def _(act):
        for j in range(FIRST + 1):
            squash(act, j, 0)
        if loops:
            with act.Fori(0, loops) as i:
                for j in range(FIRST, FIRST + U):
                    squash(act, j + 1, i)
        for j in rest:
            squash(act, j + 1, 0)

    @c.block.vector
    def _(dve):
        nc.vector.memset(y[:, :, :], 0.0)
        dve.drain()
        combine(dve, 0, 0)
        for j in range(FIRST):
            combine(dve, j + 1, 0)
            add(dve, j, j, 0)
        if loops:
            with dve.Fori(0, loops) as i:
                for j in range(FIRST, FIRST + U):
                    combine(dve, j + 1, i)
                    add(dve, j, i * U + j, i)
        for j in rest:
            combine(dve, j + 1, 0)
            add(dve, j, j, 0)
        add(dve, n - 1, n - 1, 0)
    gate_squashed.count += n
    hidden_ready.count += n
    added.count += 2 * n
    c.join()


def logits_stage(c, wr, br, n, logits):
    nc = c.nc
    ready = c.sig("router_logits")

    @c.block.tensor
    def _(pe):
        for t in range(TT):
            for k in range(KD):
                last = nc.tensor.matmul(c.psum[:, t, 0:n], c.xT[:, k, t * P:(t + 1) * P], wr[:, k, :],
                                        start=(k == 0), stop=(k == KD - 1))
        last.then_inc(*ready.up())

    @c.block.vector
    def _(dve):
        dve.wait_ge(*ready.at(1))
        c.dve(nc.vector.tensor_tensor(logits, c.psum[:, 0:TT, 0:n], br.unsqueeze(1).broadcast_to([P, TT, n]), ALU.add))


MOE_G, MOE_E = 4, 8


def route_hier(c, layer, ctx):
    nc, arg = c.nc, c.arg
    sb = lambda name, shape, dt=F32: c.sb(f"r{layer}_" + name, shape, dt, ctx)
    n = MOE_G + MOE_G * MOE_E
    wr, br = sb("wr", [P, KD, n]), sb("br", [P, n])
    lg = sb("lg", [P, TT, n])
    g8, top, topi = sb("g8", [P, TT, 8]), sb("top", [P, TT, 8]), sb("topi", [P, TT, 8], U32)
    idx = sb("idx", [P, TT, 2])
    iota, iota_i = sb("iota", [P, 8]), sb("iota_i", [P, 8], I32)
    ohg, eg, gw = sb("ohg", [P, TT, MOE_G]), sb("eg", [P, TT, MOE_G]), sb("gw", [P, TT, 1])
    prod, es, red = sb("prod", [P, TT, MOE_G, MOE_E]), sb("es", [P, TT, MOE_E]), sb("red", [P, TT, 1])
    pw, w8, w8b = sb("pw", [P, TT, 2]), sb("w8", [P, TT, MOE_E]), sb("w8b", [P, TT, MOE_E])
    wts = sb("wts", [P, TT, MOE_G * MOE_E])
    load_params(c, [(wr[:, :, 0:MOE_G], k_tiles(arg["moe_w_rg"][layer])), (wr[:, :, MOE_G:], k_tiles(arg["moe_w_re"][layer])),
                    (br[:, 0:MOE_G], bcast(arg["moe_b_rg"][layer])), (br[:, MOE_G:], bcast(arg["moe_b_re"][layer]))])
    iotas = c.sig("iota_ready")

    @c.block.gpsimd
    def _(pool):
        nc.gpsimd.iota(iota_i[:, :], pattern=[[1, 8]], base=0, channel_multiplier=0).then_inc(*iotas.up())
    c.join()
    logits_stage(c, wr, br[:, :], n, lg[:, :, :])
    centred, exped = c.sig("router_centred"), c.sig("router_exp")

    @c.block.vector
    def _(dve):
        c.dve(nc.vector.tensor_copy(iota[:, :], iota_i[:, :]))
        c.dve(nc.vector.memset(g8[:, :, :], -3e38))
        c.dve(nc.vector.tensor_copy(g8[:, :, 0:MOE_G], lg[:, :, 0:MOE_G]))
        for t in range(TT):
            c.dve(nc.vector.max(top[:, t, :], g8[:, t, :]))
            c.dve(nc.vector.max_index(topi[:, t, :], top[:, t, :], g8[:, t, :]))
        c.dve(nc.vector.tensor_copy(idx[:, :, 0:1], topi[:, :, 0:1]))
        for t in range(TT):
            c.dve(nc.vector.tensor_scalar(ohg[:, t, :], iota[:, 0:MOE_G], idx[:, t, 0:1], None, ALU.is_equal))
        c.dve(nc.vector.tensor_tensor(eg[:, :, :], lg[:, :, 0:MOE_G], top[:, :, 0:1].broadcast_to([P, TT, MOE_G]), ALU.subtract))
        c.dve(nc.vector.tensor_tensor(prod[:, :, :, :], lg[:, :, MOE_G:].rearrange("p t (g e) -> p t g e", g=MOE_G),
                                      ohg[:, :, :].unsqueeze(3).broadcast_to([P, TT, MOE_G, MOE_E]), ALU.mult))
        c.dve(nc.vector.tensor_reduce(es[:, :, :], prod[:, :, :, :].rearrange("p t g e -> p t e g"), AX_X, ALU.add))
        c.dve(nc.vector.tensor_reduce(red[:, :, :], es[:, :, :], AX_X, ALU.max))
        nc.vector.tensor_tensor(es[:, :, :], es[:, :, :], red[:, :, :].broadcast_to([P, TT, MOE_E]), ALU.subtract).then_inc(*centred.up())
        dve.wait_ge(*exped.at(1))
        c.dve(nc.vector.tensor_reduce(gw[:, :, :], eg[:, :, :], AX_X, ALU.add))
        c.dve(nc.vector.reciprocal(gw[:, :, :], gw[:, :, :]))
        c.dve(nc.vector.tensor_reduce(red[:, :, :], es[:, :, :], AX_X, ALU.add))
        c.dve(nc.vector.reciprocal(red[:, :, :], red[:, :, :]))
        c.dve(nc.vector.tensor_tensor(es[:, :, :], es[:, :, :], red[:, :, :].broadcast_to([P, TT, MOE_E]), ALU.mult))
        for t in range(TT):
            c.dve(nc.vector.max(top[:, t, :], es[:, t, :]))
            c.dve(nc.vector.max_index(topi[:, t, :], top[:, t, :], es[:, t, :]))
        c.dve(nc.vector.tensor_copy(idx[:, :, :], topi[:, :, 0:2]))
        c.dve(nc.vector.tensor_reduce(red[:, :, :], top[:, :, 0:2], AX_X, ALU.add))
        c.dve(nc.vector.reciprocal(red[:, :, :], red[:, :, :]))
        c.dve(nc.vector.tensor_tensor(red[:, :, :], red[:, :, :], gw[:, :, :], ALU.mult))
        c.dve(nc.vector.tensor_tensor(pw[:, :, :], top[:, :, 0:2], red[:, :, :].broadcast_to([P, TT, 2]), ALU.mult))
        for t in range(TT):
            nc.vector.tensor_scalar(w8[:, t, :], iota[:, :], idx[:, t, 0:1], pw[:, t, 0:1], ALU.is_equal, ALU.mult)
            c.dve(nc.vector.tensor_scalar(w8b[:, t, :], iota[:, :], idx[:, t, 1:2], pw[:, t, 1:2], ALU.is_equal, ALU.mult))
        dve.drain()
        c.dve(nc.vector.tensor_tensor(w8[:, :, :], w8[:, :, :], w8b[:, :, :], ALU.add))
        nc.vector.tensor_tensor(wts[:, :, :].rearrange("p t (g e) -> p t g e", g=MOE_G),
                                ohg[:, :, :].unsqueeze(3).broadcast_to([P, TT, MOE_G, MOE_E]),
                                w8[:, :, :].unsqueeze(2).broadcast_to([P, TT, MOE_G, MOE_E]), ALU.mult)

    @c.block.scalar
    def _(act):
        act.wait_ge(*centred.at(1))
        nc.scalar.activation(eg[:, :, :], eg[:, :, :], ACT.Exp)
        nc.scalar.activation(es[:, :, :], es[:, :, :], ACT.Exp)
        act.drain().then_inc(*exped.up())
    c.join()
    return wts


def hier_moe(c, layer):
    nc, arg = c.nc, c.arg
    with ExitStack() as ctx:
        c.y = c.sb("moe_y", [P, TT, D], ctx=ctx)
        wts = route_hier(c, layer, ctx)
        one = lambda v: (lambda j: v[bass.ds(j, 1)].rearrange("a p k f -> (a p) k f") if not isinstance(j, int) else v[j])
        stream_ffn(c, MOE_G * MOE_E, one(arg["moe_w_gate"][layer].rearrange("e (k p) f -> e p k f", p=P)),
                   one(arg["moe_w_up"][layer].rearrange("e (k p) f -> e p k f", p=P)),
                   one(arg["moe_w_down"][layer].rearrange("e (k p) f -> e p k f", p=P)),
                   lambda t, j: wts[:, t, j:j + 1] if isinstance(j, int) else wts[:, t, bass.ds(j, 1)], ctx)
        load_params(c, [(c.gain[:, :], bcast(arg["ln2_g"][layer])), (c.bias[:, :], bcast(arg["ln2_b"][layer]))])

        @c.block.vector
        def _(dve):
            nc.vector.scalar_tensor_tensor(c.x[:, :, :], c.x[:, :, :], DN_ALPHA, c.y[:, :, :], ALU.mult, ALU.add)
        c.join()
    post_norm(c, None, None)



ML_H, ML_D, FX_H, FX_D = 4, 64, 8, 64
ML_W, CF_W, FX_W = ML_H * ML_D, D // 4, FX_H * FX_D
ML_K, CF_K = 4, 31
Z_V, Z_O, Z_IF, Z_GLU = 2 * ML_W, 3 * ML_W, 4 * ML_W, 4 * ML_W + 2 * ML_H
Z_FQ = Z_GLU + 2 * CF_W
Z_FF = Z_FQ + 3 * FX_W


def pre_norm(c, gain, rows):
    load_params(c, [(c.gain[:, :], bcast(gain))])
    c.join()
    norm_stage(c, [dict(src=c.x[:, :, :], dst=rows[:, :, :], kind="rms", eps=RMS_EPS, gain=c.gain[:, :], bias=None)])
    rows_to_columns(c, rows, c.xT, KD)


def hybrid_mixer(c, layer, cat, ctx):
    nc, arg = c.nc, c.arg
    sb = lambda name, shape, dt=F32: c.sb(f"h{layer}_" + name, shape, dt, ctx)
    NT = 2 * ML_W // P
    qk_in, qk = sb("qk_in", [P, NT, ML_K - 1 + TOK]), sb("qk", [P, NT, TOK])
    cf_in, cf = sb("cf_in", [P, 2, CF_K - 1 + TOK]), sb("cf", [P, 2, TOK])
    sg = sb("sg", [P, 2, TOK])
    mw, mb = sb("mw", [P, NT, ML_K]), sb("mb", [P, NT])
    cw, cb = sb("cw", [P, 2, CF_K]), sb("cb", [P, 2])
    vo = sb("vo", [P, TT, 2 * ML_W])
    fq, fk, fv = sb("fq", [P, FX_H // 2, TOK]), sb("fk", [P, FX_H // 2, TOK]), sb("fv", [P, TT, FX_W])
    gates, gb = sb("gates", [P, TT, 2 * ML_H + FX_H]), sb("gb", [P, 2 * ML_H + FX_H])
    norm_w, ln_w, ln_b = sb("norm_w", [P, ML_W]), sb("ln_w", [P, CF_W]), sb("ln_b", [P, CF_W])
    NH = ML_H + FX_H
    lf, ab, F, A = (sb(x, [P, TT, NH]) for x in ("lf", "ab", "F", "A"))
    dm = sb("dm", [P, ML_H * 3 * P])
    df = sb("df", [P, FX_H * 3 * P])
    mneg, floor = sb("mneg", [P, TT, ML_H]), sb("floor", [P, TT, ML_H])

    def decay(buf, n, t):
        return buf[:, 0:n * P].rearrange("p (h k) -> p h k", h=n) if t == 0 else \
            buf[:, n * P:].rearrange("p (h k) -> p h k", h=n)
    load_params(c, [
        (mw[:, i, :], arg["mlstm_conv_w_2"][layer][:, i * P:(i + 1) * P].rearrange("k p -> p k")) for i in range(NT)] + [
        (mb[:, :], arg["mlstm_conv_b_2"][layer].rearrange("(c p) -> p c", p=P))] + [
        (cw[:, i, :], arg["conf_conv_w_2"][layer][:, i * P:(i + 1) * P].rearrange("k p -> p k")) for i in range(2)] + [
        (cb[:, :], arg["conf_conv_b_2"][layer].rearrange("(c p) -> p c", p=P)),
        (gb[:, 0:ML_H], bcast(arg["mlstm_b_i_2"][layer])), (gb[:, ML_H:2 * ML_H], bcast(arg["mlstm_b_f_2"][layer])),
        (gb[:, 2 * ML_H:], bcast(arg["fox_b_f_2"][layer])),
        (norm_w[:, :], bcast(arg["mlstm_norm_w_2"][layer])), (ln_w[:, :], bcast(arg["conf_ln_w_2"][layer])),
        (ln_b[:, :], bcast(arg["conf_ln_b_2"][layer]))])
    w = arg["w_in_2"][layer]
    cp = lambda dst: (lambda r: nc.scalar.activation(dst, r, ACT.Copy))
    dcp = lambda dst: (lambda r: nc.vector.tensor_copy(dst, r))
    pad, cpad = ML_K - 1, CF_K - 1

    @c.block.gpsimd
    def _(pool):
        nc.gpsimd.memset(qk_in[:, :, 0:pad], 0.0)
        nc.gpsimd.memset(cf_in[:, :, 0:cpad], 0.0)
    projection(c, [
        Rows(c.xT, w, Z_IF, 2 * ML_H, "dve", dcp(gates[:, :, 0:2 * ML_H])),
        Rows(c.xT, w, Z_FF, FX_H, "dve", dcp(gates[:, :, 2 * ML_H:])),
        Cols(c.xT, w, 0, 256, "act", cp(qk_in[:, 0:2, pad:])),
        Cols(c.xT, w, 256, 256, "dve", dcp(qk_in[:, 2:4, pad:])),
        Cols(c.xT, w, Z_GLU, 256, "dve", dcp(cf_in[:, :, cpad:])),
        Cols(c.xT, w, Z_GLU + 256, 256, "act", lambda r: nc.scalar.activation(sg[:, :, :], r, ACT.Sigmoid)),
        Rows(c.xT, w, Z_V, 512, "act", cp(vo[:, :, :])),
        Cols(c.xT, w, Z_FQ, 256, "dve", dcp(fq[:, 0:2, :])),
        Cols(c.xT, w, Z_FQ + 256, 256, "act", cp(fq[:, 2:4, :])),
        Cols(c.xT, w, Z_FQ + FX_W, 256, "dve", dcp(fk[:, 0:2, :])),
        Cols(c.xT, w, Z_FQ + FX_W + 256, 256, "act", cp(fk[:, 2:4, :])),
        Rows(c.xT, w, Z_FQ + 2 * FX_W, 512, "act", cp(fv[:, :, :]))])

    abs_ready, log_ready, lf_ready = c.sig("gate_abs"), c.sig("gate_log"), c.sig("log_forget_ready")
    sums, sums_taken, rows_ready = c.sig("forget_sums"), c.sig("forget_sums_taken"), c.sig("decay_rows")
    decayed, max_ready, exped = c.sig("decays_ready"), c.sig("decay_max"), c.sig("decay_exp")
    step, convolved = c.sig("conv_step"), c.sig("convolved")
    zf = gates[:, :, ML_H:]

    @c.block.vector
    def _(dve):
        c.dve(nc.vector.tensor_tensor(gates[:, :, :], gates[:, :, :], gb[:, :].unsqueeze(1).broadcast_to([P, TT, 2 * ML_H + FX_H]), ALU.add))
        nc.vector.scalar_tensor_tensor(ab[:, :, :], zf, -1.0, zf, ALU.mult, ALU.max).then_inc(*abs_ready.up())
        dve.wait_ge(*log_ready.at(1))
        nc.vector.scalar_tensor_tensor(lf[:, :, :], zf, 0.0, ab[:, :, :], ALU.min, ALU.subtract).then_inc(*lf_ready.up())
        dve.wait_ge(*sums.at(1))
        c.dve(nc.vector.tensor_copy(F[:, :, :], c.psum[:, 0:TT, 0:NH]))
        c.dve(nc.vector.tensor_scalar(A[:, :, :], F[:, :, :], -1.0, None, ALU.mult))
        nc.vector.tensor_tensor(A[:, :, 0:ML_H], A[:, :, 0:ML_H], gates[:, :, 0:ML_H], ALU.add).then_inc(*sums_taken.up())

    @c.block.scalar
    def _(act):
        act.wait_ge(*abs_ready.at(1))
        c.act(nc.scalar.activation(ab[:, :, :], ab[:, :, :], ACT.Exp, scale=-1.0))
        nc.scalar.activation(ab[:, :, :], ab[:, :, :], ACT.Ln, bias=c.ones[:, 0:1]).then_inc(*log_ready.up())

    @c.block.tensor
    def _(pe):
        pe.wait_ge(*lf_ready.at(1))
        nc.tensor.matmul(c.psum[:, 0, 0:NH], c.tri01[:, :], lf[:, 0, :], start=True, stop=True)
        nc.tensor.matmul(c.psum[:, 1, 0:NH], c.ones[:, :], lf[:, 0, :], start=True, stop=False)
        nc.tensor.matmul(c.psum[:, 1, 0:NH], c.tri01[:, :], lf[:, 1, :], start=False, stop=True).then_inc(*sums.up())
        pe.wait_ge(*sums_taken.at(1))
        for h in range(NH):
            for s in range(TT):
                last = nc.tensor.matmul(c.psum[:, 2 + h // 2, (h % 2) * TOK + s * P:(h % 2) * TOK + (s + 1) * P],
                                        A[:, s, h:h + 1].broadcast_to([P, P]), c.ident[:, :], start=True, stop=True)
        last.then_inc(*rows_ready.up())

    @c.block.vector
    def _(dve):
        dve.wait_ge(*rows_ready.at(1))
        for h in range(NH):
            n, i, buf = (ML_H, h, dm) if h < ML_H else (FX_H, h - ML_H, df)
            pos = heads_position(i, n, True)
            for t in range(TT):
                nk = (t + 1) * P
                nc.vector.scalar_tensor_tensor(decay(buf, n, t)[:, pos, :], c.psum[:, 2 + h // 2, (h % 2) * TOK:(h % 2) * TOK + nk],
                                               F[:, t, h:h + 1], c.mask[:, TOK - nk:], ALU.add, ALU.add)
        dve.drain()
        for t in range(TT):
            c.dve(nc.vector.tensor_reduce(mneg[:, t, :], decay(dm, ML_H, t), AX_X, ALU.max))
            for a in range(2):
                c.dve(nc.vector.tensor_tensor(mneg[:, t, 2 * a:2 * a + 2], mneg[:, t, 2 * a:2 * a + 2], F[:, t, a:ML_H:2], ALU.max))
        nc.vector.tensor_scalar(mneg[:, :, :], mneg[:, :, :], -1.0, None, ALU.mult).then_inc(*max_ready.up())
        c.dve(nc.vector.tensor_tensor(cf_in[:, :, cpad:], cf_in[:, :, cpad:], sg[:, :, :], ALU.mult))
        start = step.count
        for taps, n, x, acc, wt, b in ((ML_K, NT, qk_in, qk, mw, mb), (CF_K, 2, cf_in, cf, cw, cb)):
            for k in range(taps):
                for i in range(n):
                    if k:
                        dve.wait_ge(step.sem, step.count - n + 1)
                    src = x[:, i, k:k + TOK]
                    last = nc.vector.tensor_scalar(acc[:, i, :], src, wt[:, i, 0:1], b[:, i:i + 1], ALU.mult, ALU.add) if k == 0 else \
                        nc.vector.scalar_tensor_tensor(acc[:, i, :], src, wt[:, i, k:k + 1], acc[:, i, :], ALU.mult, ALU.add)
                    last.then_inc(*step.up())
            if n == NT:
                dve.drain().then_inc(*convolved.up())

    @c.block.scalar
    def _(act):
        act.wait_ge(*max_ready.at(1))
        for t in range(TT):
            for pos in range(ML_H):
                d = decay(dm, ML_H, t)[:, pos, :]
                nc.scalar.activation(d, d, ACT.Exp, bias=mneg[:, t, pos:pos + 1])
        nc.scalar.activation(floor[:, :, :], mneg[:, :, :], ACT.Exp)
        act.wait_ge(*convolved.at(1))
        nc.scalar.activation(qk[:, :, :], qk[:, :, :], ACT.Silu)
    c.join()
    half = lambda i: slice((i % 2) * 64, (i % 2) * 64 + 64)
    hm = vo[:, :, 0:ML_W]
    attention(c, [(t, 0) for t in range(TT)], ML_H, ML_D,
              q=lambda t, b, i: qk[half(i), i // 2, t * P:(t + 1) * P], k=lambda b, i, nk: qk[half(i), 2 + i // 2, 0:nk],
              v=lambda b, i, s: vo[:, s, i * ML_D:(i + 1) * ML_D],
              out=lambda t, b: cat[:, t, 0:ML_W].rearrange("p (h d) -> p h d", h=ML_H),
              scale=ML_D ** -0.5, bias=None,
              gated=(lambda t, nk: decay(dm, ML_H, t), lambda t: floor[:, t, :]))
    attention(c, [(t, 0) for t in range(TT)], FX_H, FX_D,
              q=lambda t, b, i: fq[half(i), i // 2, t * P:(t + 1) * P], k=lambda b, i, nk: fk[half(i), i // 2, 0:nk],
              v=lambda b, i, s: fv[:, s, i * FX_D:(i + 1) * FX_D],
              out=lambda t, b: cat[:, t, ML_W + CF_W:].rearrange("p (h d) -> p h d", h=FX_H),
              scale=FX_D ** -0.5, bias=lambda t, b, nk: decay(df, FX_H, t))

    transpose_stage(c, [([cf[:, i, t * P:(t + 1) * P] for i in range(2)], cat[:, t, ML_W:ML_W + CF_W], "dve") for t in range(TT)])
    og = vo[:, :, ML_W:]
    norm_stage(c, [dict(src=cat[:, t, 0:ML_W].rearrange("p (h d) -> p h d", h=ML_H),
                        dst=hm[:, t, :].rearrange("p (h d) -> p h d", h=ML_H), kind="rms", eps=RMS_EPS, gain=None, bias=None)
                   for t in range(TT)] +
               [dict(src=cat[:, :, ML_W:ML_W + CF_W], dst=cat[:, :, ML_W:ML_W + CF_W], kind="ln", eps=RMS_EPS,
                     gain=ln_w[:, :], bias=ln_b[:, :])])

    @c.block.scalar
    def _(act):
        nc.scalar.activation(cat[:, :, ML_W:ML_W + CF_W], cat[:, :, ML_W:ML_W + CF_W], ACT.Silu)
        nc.scalar.activation(og, og, ACT.Sigmoid).then_inc(*c.sig("output_gate").up())

    @c.block.vector
    def _(dve):
        c.dve(nc.vector.tensor_tensor(hm, hm, norm_w[:, :].unsqueeze(1).broadcast_to([P, TT, ML_W]), ALU.mult))
        dve.wait_ge(*c.sig("output_gate").at(1))
        nc.vector.tensor_tensor(cat[:, :, 0:ML_W], hm, og, ALU.mult)
    c.join()


XA_H, XA_D = 4, 128
XA_W = XA_H * XA_D


def cross_attention(c, layer):
    nc, arg = c.nc, c.arg
    with ExitStack() as ctx:
        sb = lambda name, shape, dt=F32: c.sb(f"x{layer}_" + name, shape, dt, ctx)
        rows, mem, memT = sb("rows", [P, TT, D]), sb("mem", [P, TT, D]), sb("memT", [P, KD, TOK])
        qT, kT, v = sb("qT", [P, XA_H, TOK]), sb("kT", [P, XA_H, TOK]), sb("v", [P, TT, XA_W])
        o, oT = sb("o", [P, TT, XA_W]), sb("oT", [P, XA_H, TOK])
        load_params(c, [(mem[:, :, :], arg["mem_2"][0].rearrange("(t p) d -> p t d", p=P)),
                        (c.bias[:, :], bcast(arg["norm_mem_w_2"][layer]))])
        pre_norm(c, arg["norm_xattn_w_2"][layer], rows)
        norm_stage(c, [dict(src=mem[:, :, :], dst=rows[:, :, :], kind="rms", eps=RMS_EPS, gain=c.bias[:, :], bias=None)])
        rows_to_columns(c, rows, memT, KD)
        cp = lambda dst: (lambda r: nc.scalar.activation(dst, r, ACT.Copy))
        dcp = lambda dst: (lambda r: nc.vector.tensor_copy(dst, r))
        wq, wkv = arg["xattn_w_q_2"][layer], arg["xattn_w_kv_2"][layer]
        projection(c, [Cols(c.xT, wq, 0, 256, "act", cp(qT[:, 0:2, :])), Cols(c.xT, wq, 256, 256, "dve", dcp(qT[:, 2:4, :])),
                       Cols(memT, wkv, 0, 256, "act", cp(kT[:, 0:2, :])), Cols(memT, wkv, 256, 256, "dve", dcp(kT[:, 2:4, :])),
                       Rows(memT, wkv, 512, 512, "act", cp(v[:, :, :]))])
        attention(c, [(t, 0) for t in range(TT)], XA_H, XA_D,
                  q=lambda t, b, i: qT[:, i, t * P:(t + 1) * P], k=lambda b, i, nk: kT[:, i, 0:nk],
                  v=lambda b, i, s: v[:, s, i * XA_D:(i + 1) * XA_D],
                  out=lambda t, b: o[:, t, :].rearrange("p (h d) -> p h d", h=XA_H),
                  scale=XA_D ** -0.5, bias=None, paired=False, causal=False)
        rows_to_columns(c, o, oT, XA_H)
        residual(c, oT, arg["xattn_w_o_2"][layer], 1.0)


F2 = 2816
FFC = F2 // CH
EXP2 = 8


def add_y(c):
    @c.block.vector
    def _(dve):
        c.nc.vector.tensor_tensor(c.x[:, :, :], c.x[:, :, :], c.y[:, :, :], ALU.add)
    c.join()


def dense_ffn(c, layer):
    arg = c.arg
    with ExitStack() as ctx:
        c.y = c.sb("ffn_y", [P, TT, D], ctx=ctx)
        pre_norm(c, arg["norm_ffn_w_2"][layer], c.y)
        cols = lambda v: (lambda j: v.rearrange("(k p) (c f) -> c p k f", p=P, f=CH)[bass.ds(j, 1)].rearrange("a p k f -> (a p) k f"))
        rows = lambda v: (lambda j: v.rearrange("(c k p) n -> c p k n", p=P, k=2)[bass.ds(j, 1)].rearrange("a p k f -> (a p) k f"))
        stream_ffn(c, FFC, cols(arg["ffn_w_gate_2"][0]), cols(arg["ffn_w_up_2"][0]), rows(arg["ffn_w_down_2"][0]), None, ctx)
        add_y(c)


def flat_moe(c, layer):
    nc, arg = c.nc, c.arg
    with ExitStack() as ctx:
        sb = lambda name, shape, dt=F32: c.sb("f_" + name, shape, dt, ctx)
        c.y = sb("y", [P, TT, D])
        wr, lg = sb("wr", [P, KD, EXP2]), sb("lg", [P, TT, EXP2])
        top, topi, idx = sb("top", [P, TT, 8]), sb("topi", [P, TT, 8], U32), sb("idx", [P, TT, 2])
        iota, iota_i = sb("iota", [P, 8]), sb("iota_i", [P, 8], I32)
        zero = sb("zero", [P, EXP2])
        e1, w = sb("e1", [P, TT, 1]), sb("w", [P, TT, 2])
        w8, w8b, wts = sb("w8", [P, TT, EXP2]), sb("w8b", [P, TT, EXP2]), sb("wts", [P, TT, EXP2, FFC])
        load_params(c, [(wr[:, :, :], k_tiles(arg["router_w_2"][0]))])
        pre_norm(c, arg["norm_ffn_w_2"][layer], c.y)

        @c.block.gpsimd
        def _(pool):
            nc.gpsimd.memset(zero[:, :], 0.0)
            nc.gpsimd.iota(iota_i[:, :], pattern=[[1, 8]], base=0, channel_multiplier=0)
        c.join()
        logits_stage(c, wr, zero[:, :], EXP2, lg[:, :, :])
        centred, exped = c.sig("router_centred"), c.sig("router_exp")

        @c.block.vector
        def _(dve):
            c.dve(nc.vector.tensor_copy(iota[:, :], iota_i[:, :]))
            for t in range(TT):
                c.dve(nc.vector.max(top[:, t, :], lg[:, t, :]))
                c.dve(nc.vector.max_index(topi[:, t, :], top[:, t, :], lg[:, t, :]))
            c.dve(nc.vector.tensor_copy(idx[:, :, :], topi[:, :, 0:2]))
            nc.vector.tensor_tensor(e1[:, :, :], top[:, :, 1:2], top[:, :, 0:1], ALU.subtract).then_inc(*centred.up())
            dve.wait_ge(*exped.at(1))
            c.dve(nc.vector.tensor_scalar(w[:, :, 0:1], e1[:, :, :], 1.0, None, ALU.add))
            c.dve(nc.vector.reciprocal(w[:, :, 0:1], w[:, :, 0:1]))
            c.dve(nc.vector.tensor_tensor(w[:, :, 1:2], w[:, :, 0:1], e1[:, :, :], ALU.mult))
            for t in range(TT):
                nc.vector.tensor_scalar(w8[:, t, :], iota[:, :], idx[:, t, 0:1], w[:, t, 0:1], ALU.is_equal, ALU.mult)
                nc.vector.tensor_scalar(w8b[:, t, :], iota[:, :], idx[:, t, 1:2], w[:, t, 1:2], ALU.is_equal, ALU.mult)
            dve.drain()
            c.dve(nc.vector.tensor_tensor(w8[:, :, :], w8[:, :, :], w8b[:, :, :], ALU.add))
            nc.vector.tensor_copy(wts[:, :, :, :], w8[:, :, :].unsqueeze(3).broadcast_to([P, TT, EXP2, FFC]))

        @c.block.scalar
        def _(act):
            act.wait_ge(*centred.at(1))
            nc.scalar.activation(e1[:, :, :], e1[:, :, :], ACT.Exp).then_inc(*exped.up())
        c.join()

        def cols(v):
            vv = v.rearrange("e (k p) (c f) -> e c p k f", p=P, f=CH)
            return lambda j: vv[bass.ds(j // FFC, 1), bass.ds(j % FFC, 1)].rearrange("a b p k f -> (a b p) k f")
        down = arg["moe_w_down_2"][0].rearrange("e (c k p) n -> (e c) p k n", p=P, k=2)
        wf = wts[:, :, :, :].rearrange("p t e c -> p t (e c)")
        stream_ffn(c, EXP2 * FFC, cols(arg["moe_w_gate_2"][0]), cols(arg["moe_w_up_2"][0]),
                   lambda j: down[bass.ds(j, 1)].rearrange("a p k n -> (a p) k n"),
                   lambda t, j: wf[:, t, bass.ds(j, 1)], ctx)
        add_y(c)


def load_weights(c):
    ring = c.ring

    @c.block.sync
    def _(sp):
        def load(n, i, dst_n, src):
            if dst_n >= RING:
                sp.wait_ge(ring.used, n - RING + 1)
            kt, cols = src.shape[1:]
            sp.dma_start(ring.view(dst_n, kt, cols), src).then_inc(ring.full[dst_n % RING], 16)

        for entry in ring.plan:
            if entry[0] == "tile":
                _, n, dst, src = entry
                load(n, 0, n, src)
                continue
            _, p0, n, gate, up, down = entry
            U = 4
            loops = max(0, (n - 2) // U)

            def chunk(j, first, i):
                at = p0 + 2 + 3 * first
                load(at + 12 * i, i, at, gate(j + 1))
                load(at + 1 + 12 * i, i, at + 1, up(j + 1))
                load(at + 2 + 12 * i, i, at + 2, down(j))
            load(p0, 0, p0, gate(0))
            load(p0 + 1, 0, p0 + 1, up(0))
            chunk(0, 0, 0)
            if loops:
                with sp.Fori(0, loops) as i:
                    for r in range(U):
                        chunk(i * U + 1 + r, 1 + r, i)
            for j in range(1 + U * loops, n - 1):
                chunk(j, j, 0)
            load(p0 + 3 * n - 1, 0, p0 + 3 * n - 1, down(n - 1))


def build(nc, arg, out):
    with ExitStack() as ctx:
        c = Core(nc, ctx)
        c.arg = arg
        c.ring = WeightRing(c)
        c.block = ctx.enter_context(nc.Block(no_gpsimd_drain=True))
        constants(c)
        rows_to_columns(c, c.x, c.xT, KD)

        def stages():
            for layer, mixer in enumerate((ab_mixer, nsa_mixer)):
                with ExitStack() as m:
                    cat = c.sb(f"cat{layer}", [P, TT, D], ctx=m)
                    mixer(c, cat, m)
                    rows_to_columns(c, cat, c.xT, KD)
                residual(c, c.xT, arg[("ab_w_o", "c_w_o")[layer]][0], DN_ALPHA,
                         [(c.gain[:, :], bcast(arg["ln1_g"][layer])), (c.bias[:, :], bcast(arg["ln1_b"][layer]))])
                post_norm(c, None, None)
                hier_moe(c, layer)
            for layer in range(DEPTH):
                with ExitStack() as m:
                    cat = c.sb(f"cat{2 + layer}", [P, TT, D], ctx=m)
                    pre_norm(c, arg["norm_mix_w_2"][layer], cat)
                    hybrid_mixer(c, layer, cat, m)
                    rows_to_columns(c, cat, c.xT, KD)
                residual(c, c.xT, arg["w_out_2"][layer], 1.0)
                cross_attention(c, layer)
                (dense_ffn, flat_moe)[layer % 2](c, layer)
        stages()
        res = c.sb("result", [P, TT, D])
        load_params(c, [(c.gain[:, :], bcast(arg["norm_final_w_2"]))])
        c.join()
        norm_stage(c, [dict(src=c.x[:, :, :], dst=res[:, :, :], kind="rms", eps=RMS_EPS, gain=c.gain[:, :], bias=None)])
        stored = c.sig("result_stored")

        @c.block.scalar
        def _(act):
            act.dma_start(out[0].rearrange("(t p) d -> p t d", p=P), res[:, :, :]).then_inc(*stored.up(16))
            act.wait_ge(*stored.now())
        load_weights(c)


_OUTS = [((1, TOK, D), "float32")]


def kernel(**inputs):
    import numpy as _np
    import concourse.bacc as _bacc
    from concourse import mybir as _mybir
    from concourse.bass_utils import run_bass_kernel_spmd as _run

    nc = _bacc.Bacc("TRN2", target_bir_lowering=False, num_devices=1)
    arrays, arg = {}, {}
    for name, a in inputs.items():
        a = _np.ascontiguousarray(a)
        arrays[f"in_{name}_dram"] = a
        arg[name] = nc.dram_tensor(f"in_{name}_dram", a.shape, _mybir.dt.from_np(a.dtype), kind="ExternalInput").ap()
    shape, dtype = _OUTS[0]
    out = nc.dram_tensor("out_0_dram", shape, _mybir.dt.from_np(_np.dtype(dtype)), kind="ExternalOutput").ap()
    build(nc, arg, out)
    r = _run(nc, [arrays], core_ids=[0])
    return r.results[0]["out_0_dram"]
```

```python
import math
from contextlib import ExitStack

import numpy as np

import concourse.bass as bass
from concourse import mybir

F32 = mybir.dt.float32
I32 = mybir.dt.int32
U32 = mybir.dt.uint32
ALU = mybir.AluOpType
ACT = mybir.ActivationFunctionType
AX_X = mybir.AxisListType.X

P = 128
TOK = 256
TT = TOK // P
D = 1024
KD = D // P
SLOT = 2048
RING = 12
NEG = -1e30
DEPTH = 2
DN_ALPHA = (2.0 * DEPTH) ** 0.25
LN_EPS = 1e-5
RMS_EPS = 1e-6


class Signal:

    def __init__(self, sem):
        self.sem, self.count, self.base = sem, 0, 0

    def up(self, n=1):
        self.count += n
        return self.sem, n

    def at(self, n):
        assert n > 0
        return self.sem, self.base + n

    def now(self):
        return self.sem, self.count


class WeightRing:

    def __init__(self, core):
        self.buf = core.sb("weight_ring", [P, RING, SLOT])
        self.full = [core.new_sem(f"weights_full_{i}") for i in range(RING)]
        self.used = core.new_sem("weights_used")
        self.loaded = [0] * RING
        self.tiles = 0
        self.plan = []

    def view(self, n, kt, cols):
        return self.buf[:, n % RING, 0:kt * cols].rearrange("p (k n) -> p k n", k=kt)

    def take(self, pe, src):
        kt, cols = src.shape[1], src.shape[2]
        n = self.tiles
        dst = self.view(n, kt, cols)
        self.plan.append(("tile", n, dst[0:src.shape[0]], src))
        self.tiles += 1
        self.loaded[n % RING] += 16
        pe.wait_ge(self.full[n % RING], self.loaded[n % RING])
        return dst


def k_tiles(w):
    return w.rearrange("(k p) n -> p k n", p=P)


class Core:

    def __init__(self, nc, ctx):
        self.nc, self.ctx = nc, ctx
        self.signals = {}
        self.order = []
        self.ended = 0
        self.names = {}

    def sb(self, name, shape, dt=F32, ctx=None):
        times = self.names[name] = self.names.get(name, 0) + 1
        return (ctx or self.ctx).enter_context(
            self.nc.sbuf_tensor(name if times == 1 else f"{name}_{times}", shape, dt))

    def new_sem(self, name):
        return self.ctx.enter_context(self.nc.semaphore(name))

    def sig(self, name):
        if name not in self.signals:
            self.signals[name] = Signal(self.new_sem(name))
        return self.signals[name]

    def link(self, eng, ins):
        name = {self.nc.vector: "dve", self.nc.scalar: "act", self.nc.gpsimd: "pool"}[eng]
        s = self.sig(f"{name}_step")
        ins.then_inc(*s.up())
        eng.wait_ge(*s.now())

    def dve(self, ins):
        self.link(self.nc.vector, ins)

    def act(self, ins):
        self.link(self.nc.scalar, ins)

    def pool(self, ins):
        self.link(self.nc.gpsimd, ins)

    def join(self):
        s = self.sig("stage_ended")
        self.ended += 1
        total = 4 * self.ended

        @self.block.tensor
        def _(pe):
            pe.drain().then_inc(*s.up())
            pe.wait_ge(s.sem, total)

        @self.block.scalar
        def _(act):
            act.drain().then_inc(*s.up())
            act.wait_ge(s.sem, total)

        @self.block.vector
        def _(dve):
            dve.drain().then_inc(*s.up())
            dve.wait_ge(s.sem, total)

        @self.block.gpsimd
        def _(pool):
            pool.drain().then_inc(*s.up())
            pool.wait_ge(s.sem, total)

        for x in self.signals.values():
            x.base = x.count


def constants(c):
    nc = c.nc
    c.ident = c.sb("ident", [P, P])
    c.tri01 = c.sb("tri01", [P, P])
    c.ones = c.sb("ones", [P, P])
    c.S = c.sb("scores", [P, 2, 8, TOK])
    c.PT = c.sb("probs_turned", [P, 2, 512])
    c.diag = c.PT[:, :, :].rearrange("p j (t n) -> p j t n", n=P)[:, :, 0:TT]
    c.scaled = c.S[:, :, :, :].rearrange("p a b t -> p (a b t)")[:, 0:TT * D].rearrange("p (t d) -> p t d", d=D)
    c.neg_max, c.row_sum = c.sb("neg_max", [P, 2, 8]), c.sb("row_sum", [P, 2, 8])
    c.recip = c.sb("recip", [P, 8])
    c.stats, c.rstd = c.sb("norm_stats", [P, 4, 8, 2]), c.sb("norm_rstd", [P, 4, 8, 1])
    c.var, c.newton = c.sb("norm_var", [P, 4, 8, 1]), c.sb("norm_newton", [P, 8, 1])
    c.bn = c.sb("norm_parts", [P, 8, 2, 6])
    c.gain, c.bias = c.sb("gain", [P, D]), c.sb("bias", [P, D])
    c.mask = c.sb("mask", [P, TOK])
    c.x = c.sb("x", [P, TT, D])
    c.xT = c.sb("xT", [P, KD, TOK])
    c.psum = c.ctx.enter_context(nc.psum_tensor("psum", [P, 8, 512], F32))
    x_landed = c.sig("params_landed")

    @c.block.gpsimd
    def _(pool):
        nc.gpsimd.memset(c.ident[:, :], 0.0)
        nc.gpsimd.memset(c.tri01[:, :], 1.0)
        nc.gpsimd.memset(c.ones[:, :], 1.0)
        c.pool(nc.gpsimd.memset(c.mask[:, :], 0.0))
        pool.drain()
        nc.gpsimd.affine_select(out=c.ident[:, :], in_=c.ident[:, :], compare_op=ALU.not_equal, fill=1.0,
                                base=0, pattern=[[-1, P]], channel_multiplier=1)
        nc.gpsimd.affine_select(out=c.tri01[:, :], in_=c.tri01[:, :], compare_op=ALU.is_ge, fill=0.0,
                                base=0, pattern=[[1, P]], channel_multiplier=-1)
        nc.gpsimd.affine_select(out=c.mask[:, :], in_=c.mask[:, :], compare_op=ALU.is_ge, fill=NEG,
                                base=P, pattern=[[-1, TOK]], channel_multiplier=1)

    @c.block.scalar
    def _(act):
        act.dma_start(c.x[:, :, :], c.arg["x"][0].rearrange("(t p) d -> p t d", p=P)).then_inc(*x_landed.up(16))
        act.wait_ge(*x_landed.now())
    c.join()


def load_ahead(c, name, items):
    landed = c.sig(name)

    @c.block.gpsimd
    def _(pool):
        for dst, src in items:
            pool.dma_start(dst, src, allow_slow_non_contiguous=True).then_inc(*landed.up(16))


def load_params(c, items):
    landed = c.sig("params_landed")

    @c.block.scalar
    def _(act):
        for dst, src in items:
            act.dma_start(dst, src, allow_slow_non_contiguous=True).then_inc(*landed.up(16))
        act.wait_ge(*landed.now())


def bcast(v, n=P):
    return v.partition_broadcast(n)


def transpose_stage(c, groups, join=True, before=None):
    nc = c.nc
    turned, copied = c.sig("blocks_turned"), {"act": c.sig("turned_copied_act"), "dve": c.sig("turned_copied_dve")}

    @c.block.tensor
    def _(pe):
        for g, (ins, dst, who) in enumerate(groups):
            if before is not None:
                pe.wait_ge(*before(g))
            if g >= 8:
                w0 = groups[g - 8][2]
                pe.wait_ge(*copied[w0].at(sum(x[2] == w0 for x in groups[:g - 7])))
            for i, a in enumerate(ins):
                last = nc.tensor.transpose(c.psum[0:a.shape[1], g % 8, i * P:(i + 1) * P], a, c.ident[:, :])
            last.then_inc(*turned.up())

    def copies(eng, name, copy):
        for g, (ins, dst, who) in enumerate(groups):
            if who != name:
                continue
            w = ins[0].shape[1]
            src = c.psum[0:w, g % 8, 0:len(ins) * P]
            if len(dst.shape) == 3:
                src = src.rearrange("p (a b) -> p a b", a=dst.shape[1])
            eng.wait_ge(*turned.at(g + 1))
            copy(dst, src).then_inc(*copied[name].up())

    @c.block.scalar
    def _(act):
        copies(act, "act", lambda d, s: nc.scalar.activation(d, s, ACT.Copy))

    @c.block.vector
    def _(dve):
        copies(dve, "dve", nc.vector.tensor_copy)
    if join:
        c.join()


def rows_to_columns(c, src, dst, n, join=True):
    groups = []
    for k in range(0, n, 2):
        kk = min(2, n - k)
        ins = [src[:, t, j * P:(j + 1) * P] for j in range(k, k + kk) for t in range(TT)]
        groups.append((ins, dst[:, k:k + kk, :].rearrange("p k t -> p (k t)"), "dve" if k % 4 else "act"))
    transpose_stage(c, groups, join)


def norm_stage(c, items, join=True, done=None):
    nc = c.nc
    stats = c.stats
    have_stats, have_rstd = c.sig("norm_stats"), c.sig("norm_rstd")

    @c.block.vector
    def _(dve):
        for j, it in enumerate(items):
            n, w = it["src"].shape[1:]
            m = stats[:, j]
            for i in range(n):
                s = it["src"][:, i, :]
                if it["kind"] == "ln":
                    parts = max(1, w // 512)
                    for h in range(parts):
                        last = nc.vector.bn_stats(c.bn[:, i, h, :], s[:, h * (w // parts):(h + 1) * (w // parts)])
                    dve.drain()
                    nc.vector.bn_aggr(m[:, i, :], c.bn[:, i, 0:parts, :].rearrange("p a b -> p (a b)"))
                else:
                    nc.vector.tensor_tensor_reduce(it["dst"][:, i, :], s, s, 1.0 / w, 0.0, ALU.mult,
                                                   ALU.add, m[:, i, 1:2])
            dve.drain()
            nc.vector.tensor_scalar(c.var[:, j, 0:n, :], m[:, 0:n, 1:2], it["eps"], None, ALU.add).then_inc(*have_stats.up())

    @c.block.scalar
    def _(act):
        for j, it in enumerate(items):
            n = it["src"].shape[1]
            act.wait_ge(*have_stats.at(j + 1))
            nc.scalar.activation(c.rstd[:, j, 0:n, :], c.var[:, j, 0:n, :], ACT.Sqrt).then_inc(*have_rstd.up())

    @c.block.vector
    def _(dve):
        for j, it in enumerate(items):
            if it["kind"] == "ln":
                for i in range(it["src"].shape[1]):
                    nc.vector.scalar_tensor_tensor(it["dst"][:, i, :], it["src"][:, i, :], stats[:, j, i, 0:1],
                                                   it["gain"], ALU.subtract, ALU.mult)
        for j, it in enumerate(items):
            n, w = it["src"].shape[1:]
            dve.wait_ge(*have_rstd.at(j + 1))
            inverse_root(c, c.rstd[:, j, 0:n, :], c.var[:, j, 0:n, :], c.newton[:, 0:n, :])
            for i in range(n):
                src, dst, r = it["src"][:, i, :], it["dst"][:, i, :], c.rstd[:, j, i, :]
                if it["kind"] == "ln":
                    last = nc.vector.scalar_tensor_tensor(dst, dst, r, it["bias"], ALU.mult, ALU.add)
                elif it["gain"] is None:
                    last = nc.vector.tensor_scalar(dst, src, r, None, ALU.mult)
                else:
                    last = nc.vector.scalar_tensor_tensor(dst, src, r, it["gain"], ALU.mult, ALU.mult)
                if done is not None:
                    last.then_inc(*done.up())
        dve.drain()
    if join:
        c.join()


def inverse_root(c, r, v, h):
    nc = c.nc
    nc.vector.drain()
    c.dve(nc.vector.reciprocal(r, r))
    c.dve(nc.vector.tensor_tensor(h, r, r, ALU.mult))
    c.dve(nc.vector.tensor_tensor(h, h, v, ALU.mult))
    c.dve(nc.vector.tensor_scalar(h, h, -0.5, 1.5, ALU.mult, ALU.add))
    c.dve(nc.vector.tensor_tensor(r, r, h, ALU.mult))


def rms_scales(c, j, src, gain, y, landed):
    nc = c.nc
    summed, rooted, ready = c.sig(f"squares_summed_{j}"), c.sig(f"rms_root_{j}"), c.sig(f"rms_diagonal_{j}")
    ss, var, r = c.stats[:, j, 0:TT, 0:1], c.var[:, j, 0:TT, :], c.rstd[:, j, 0:TT, :]

    @c.block.scalar
    def _(act):
        if landed is not None:
            act.wait_ge(*landed)
        for t in range(TT):
            junk = c.psum[:, 4 * j + 2 * t:4 * j + 2 * t + 2, :].rearrange("p a b -> p (a b)")
            nc.scalar.activation(junk, src[:, t, :], ACT.Square, accum_out=c.stats[:, j, t, 0:1])
        act.drain().then_inc(*summed.up())

    @c.block.vector
    def _(dve):
        if landed is not None:
            dve.wait_ge(*landed)
        for t in range(TT):
            nc.vector.tensor_tensor(y[:, t, :], src[:, t, :], gain, ALU.mult)
        dve.wait_ge(*summed.now())
        nc.vector.tensor_scalar(var, ss, 1.0 / D, RMS_EPS, ALU.mult, ALU.add).then_inc(*rooted.up())

    @c.block.scalar
    def _(act):
        act.wait_ge(*rooted.now())
        nc.scalar.activation(r, var, ACT.Sqrt).then_inc(*rooted.up())

    @c.block.vector
    def _(dve):
        dve.wait_ge(*rooted.now())
        inverse_root(c, r, var, c.newton[:, 0:TT, :])
        for t in range(TT):
            nc.vector.tensor_scalar(c.diag[:, j, t, :], c.ident[:, :], c.rstd[:, j, t, :], None, ALU.mult)
        dve.drain().then_inc(*ready.up())


def rms_columns(c, parts, join=True):
    nc = c.nc
    turned, copied = c.sig("rms_turned"), {"act": c.sig("rms_copied_act"), "dve": c.sig("rms_copied_dve")}
    groups = [(j, y, dst, k, t) for j, y, dst in parts for k in (0, 4) for t in range(TT)]
    bank = lambda g: 4 * groups[g][0] + g % 4

    @c.block.tensor
    def _(pe):
        for g, (j, y, dst, k0, t) in enumerate(groups):
            pe.wait_ge(*c.sig(f"rms_diagonal_{j}").now())
            for i in range(4):
                last = nc.tensor.matmul(c.psum[:, bank(g), i * P:(i + 1) * P], y[:, t, (k0 + i) * P:(k0 + i + 1) * P],
                                        c.diag[:, j, t, :], start=True, stop=True)
            last.then_inc(*turned.up())

    def copies(eng, which, copy):
        for g, (j, y, dst, k0, t) in enumerate(groups):
            if g % 2 == which:
                eng.wait_ge(*turned.at(g + 1))
                copy(dst[:, k0:k0 + 4, t * P:(t + 1) * P], c.psum[:, bank(g), :].rearrange("p (k t) -> p k t", k=4))

    @c.block.scalar
    def _(act):
        copies(act, 0, lambda d, s: nc.scalar.activation(d, s, ACT.Copy))

    @c.block.vector
    def _(dve):
        copies(dve, 1, nc.vector.tensor_copy)
    if join:
        c.join()


class Rows:

    def __init__(self, xT, w, n0, width, who, take):
        self.xT, self.w, self.n0, self.width, self.who, self.take = xT, w, n0, width, who, take

    def multiply(self, c, pe, pair):
        kt = self.w.shape[0] // P
        per = min(kt, SLOT // (512 if self.width > 256 else 256))
        src = k_tiles(self.w)
        for k0 in range(0, kt, per):
            w = c.ring.take(pe, src[:, k0:k0 + per, self.n0:self.n0 + self.width])
            for t in range(TT):
                for k in range(per):
                    last = c.nc.tensor.matmul(
                        c.psum[:, 2 * pair + t, 0:self.width], self.xT[:, k0 + k, t * P:(t + 1) * P],
                        w[:, k, :], start=(k0 + k == 0), stop=(k0 + k == kt - 1))
            last.then_inc(c.ring.used, 1)

    def out(self, c, pair):
        return c.psum[:, 2 * pair:2 * pair + 2, 0:self.width]

    def ready(self, c):
        return c.ring.used, c.ring.tiles


class Cols:

    def __init__(self, xT, w, n0, width, who, take):
        self.xT, self.w, self.n0, self.width, self.who, self.take = xT, w, n0, width, who, take

    def multiply(self, c, pe, pair):
        kt = self.w.shape[0] // P
        w = c.ring.take(pe, k_tiles(self.w)[:, :, self.n0:self.n0 + self.width])
        for m in range(self.width // P):
            for k in range(kt):
                last = c.nc.tensor.matmul(c.psum[:, 2 * pair, m * TOK:(m + 1) * TOK], w[:, k, m * P:(m + 1) * P],
                                          self.xT[:, k, :], start=(k == 0), stop=(k == kt - 1))
        last.then_inc(c.ring.used, 1)

    def out(self, c, pair):
        return c.psum[:, 2 * pair, 0:self.width // P * TOK].rearrange("p (m t) -> p m t", t=TOK)

    def ready(self, c):
        return c.ring.used, c.ring.tiles


class Own:

    def __init__(self, fill, who, take):
        self.fill, self.who, self.take = fill, who, take

    def multiply(self, c, pe, pair):
        self.fill(pe, self.out(c, pair)).then_inc(*c.sig("own_products").up())

    def out(self, c, pair):
        return c.psum[:, 2 * pair:2 * pair + 2, :]

    def ready(self, c):
        return c.sig("own_products").now()


class Step:

    def __init__(self, who, run):
        self.who, self.run = who, run


def projection(c, jobs, join=True):
    taken = {"act": c.sig("results_taken_act"), "dve": c.sig("results_taken_dve")}
    order, jobs = jobs, [x for x in jobs if not isinstance(x, Step)]
    ready = []

    @c.block.tensor
    def _(pe):
        for j, job in enumerate(jobs):
            if j >= 4:
                w0 = jobs[j - 4].who
                pe.wait_ge(*taken[w0].at(sum(x.who == w0 for x in jobs[:j - 3])))
            job.multiply(c, pe, j % 4)
            ready.append(job.ready(c))

    def takes(eng, name):
        for job in order:
            if job.who != name:
                continue
            if isinstance(job, Step):
                job.run(eng)
                continue
            j = jobs.index(job)
            eng.wait_ge(*ready[j])
            job.take(job.out(c, j % 4)).then_inc(*taken[name].up())

    @c.block.scalar
    def _(act):
        takes(act, "act")

    @c.block.vector
    def _(dve):
        takes(dve, "dve")
    if join:
        c.join()


def heads_position(i, n, paired):
    return (n // 2) * (i % 2) + i // 2 if paired else i


def attention(c, batches, n, dv, q, k, v, out, scale, bias, paired=True, causal=True, gated=None, join=True):
    nc = c.nc
    S, PT = c.S, c.PT
    scored, scaled, maxed = c.sig("scores_ready"), c.sig("scores_scaled"), c.sig("maxima_ready")
    probs, turned, copied = c.sig("probs_ready"), c.sig("probs_turned"), c.sig("turned_probs_copied")
    pv_group, written = c.sig("pv_group_done"), c.sig("outputs_written")
    kts = [t + 1 if causal else TT for t, _ in batches]
    groups = []
    last_group = []
    for j, kt in enumerate(kts):
        blocks = [(i, s) for i in range(n) for s in range(kt)]
        groups += [(j, blocks[a:a + 4]) for a in range(0, len(blocks), 4)]
        last_group.append(len(groups))

    @c.block.tensor
    def _(pe):
        def scores(j):
            (t, b), nk = batches[j], kts[j] * P
            if j >= 1:
                pe.wait_ge(*scaled.at(j))
            for i in range(n):
                pos = heads_position(i, n, paired)
                last = nc.tensor.matmul(c.psum[:, pos // 2, (pos % 2) * TOK:(pos % 2) * TOK + nk],
                                        q(t, b, i), k(b, i, nk), start=True, stop=True)
            last.then_inc(*scored.up())

        def turn(g):
            j, blocks = groups[g]
            if g == 0 or groups[g - 1][0] != j:
                pe.wait_ge(*probs.at(j + 1))
            if g >= 2:
                pe.wait_ge(*copied.at(g - 1))
            for a, (i, s) in enumerate(blocks):
                pos = heads_position(i, n, paired)
                last = nc.tensor.transpose(c.psum[:, 4 + g % 2, a * P:(a + 1) * P],
                                           S[:, j % 2, pos, s * P:(s + 1) * P], c.ident[:, :])
            last.then_inc(*turned.up())

        def pv(g):
            j, blocks = groups[g]
            t, b = batches[j]
            pe.wait_ge(*copied.at(g + 1))
            if j >= 2:
                pe.wait_ge(*written.at(j - 1))
            for a, (i, s) in enumerate(blocks):
                last = nc.tensor.matmul(c.psum[:, 6 + j % 2, i * dv:(i + 1) * dv], PT[:, g % 2, a * P:(a + 1) * P],
                                        v(b, i, s), start=(s == 0), stop=(s == kts[j] - 1))
            last.then_inc(*pv_group.up())

        for j in range(len(batches) + 1):
            if j < len(batches):
                scores(j)
            if j >= 1:
                mine = [g for g in range(len(groups)) if groups[g][0] == j - 1]
                for g in mine:
                    turn(g)
                    if g > mine[0]:
                        pv(g - 1)
                pv(mine[-1])

    @c.block.scalar
    def _(act):
        for j in range(len(batches)):
            nk = kts[j] * P
            if gated is None:
                act.wait_ge(*maxed.at(j + 1))
                for pos in range(n):
                    last = nc.scalar.activation(S[:, j % 2, pos, 0:nk], S[:, j % 2, pos, 0:nk], ACT.Exp,
                                                bias=c.neg_max[:, j % 2, pos:pos + 1],
                                                accum_out=c.row_sum[:, j % 2, pos:pos + 1])
                last.then_inc(*probs.up())
            for g in [g for g in range(len(groups)) if groups[g][0] == j]:
                act.wait_ge(*turned.at(g + 1))
                if g >= 2:
                    act.wait_ge(*pv_group.at(g - 1))
                nc.scalar.activation(PT[:, g % 2, 0:len(groups[g][1]) * P],
                                     c.psum[:, 4 + g % 2, 0:len(groups[g][1]) * P], ACT.Copy).then_inc(*copied.up())

    @c.block.vector
    def _(dve):
        def finish(j):
            t, b = batches[j]
            dve.wait_ge(*pv_group.at(last_group[j]))
            r = c.row_sum[:, j % 2, 0:n]
            if gated is not None:
                c.dve(nc.vector.scalar_tensor_tensor(r, r, -1.0, r, ALU.mult, ALU.max))
                c.dve(nc.vector.tensor_tensor(r, r, gated[1](t), ALU.max))
            if j >= 1:
                dve.wait_ge(*written.at(j))
            c.dve(nc.vector.reciprocal(c.recip[:, 0:n], r))
            rr = c.recip[:, 0:n]
            o = c.psum[:, 6 + j % 2, 0:n * dv]
            if paired:
                rr = rr.rearrange("p (a b) -> p b a", a=2).unsqueeze(3).broadcast_to([P, n // 2, 2, dv])
                o = o.rearrange("p (b a d) -> p b a d", a=2, d=dv)
                dst = out(t, b).rearrange("p (b a) d -> p b a d", a=2)
            else:
                rr = rr.unsqueeze(2).broadcast_to([P, n, dv])
                o = o.rearrange("p (b d) -> p b d", d=dv)
                dst = out(t, b)
            nc.vector.tensor_tensor(dst, o, rr, ALU.mult).then_inc(*written.up())

        for j in range(len(batches)):
            (t, b), nk = batches[j], kts[j] * P
            dve.wait_ge(*scored.at(j + 1))
            if j >= 2:
                dve.wait_ge(*turned.at(last_group[j - 2]))
            sc = c.psum[:, 0:(n + 1) // 2, :].rearrange("p a (b k) -> p (a b) k", b=2)[:, 0:n, 0:nk]
            dst = S[:, j % 2, 0:n, 0:nk]
            if gated is not None:
                nc.vector.scalar_tensor_tensor(dst, sc, scale, gated[0](t, nk), ALU.mult, ALU.mult).then_inc(*scaled.up())
                dve.wait_ge(*scaled.now())
                nc.vector.tensor_reduce(c.row_sum[:, j % 2, 0:n], dst, AX_X, ALU.add).then_inc(*probs.up())
            else:
                if bias is None:
                    nc.vector.tensor_scalar(dst, sc, scale, None, ALU.mult).then_inc(*scaled.up())
                else:
                    nc.vector.scalar_tensor_tensor(dst, sc, scale, bias(t, b, nk), ALU.mult, ALU.add).then_inc(*scaled.up())
                dve.wait_ge(*scaled.now())
                nc.vector.tensor_reduce(c.neg_max[:, j % 2, 0:n], dst, AX_X, ALU.max, negate=True).then_inc(*maxed.up())
            if j >= 1:
                finish(j - 1)
        finish(len(batches) - 1)
    if join:
        c.join()



GM_W, GM_G = 512, 4
MLA_H, MLA_NOPE, MLA_ROPE, MLA_V = 8, 64, 32, 64
MLA_QK = MLA_NOPE + MLA_ROPE
MLA_QR, MLA_KVR = 256, 128
ROPE_BASE = 10000.0


def causal_bias(c, n):
    def bias(t, b, nk):
        m = c.mask[:, TOK - nk:TOK]
        return m.unsqueeze(1).broadcast_to([P, n, nk])
    return bias


def residual(c, xT, w, alpha, params=()):
    nc = c.nc
    if params:
        load_params(c, params)

    def add(n0):
        part = c.x[:, :, n0:n0 + 512]
        return lambda r: nc.vector.scalar_tensor_tensor(part, part, alpha, r, ALU.mult, ALU.add)
    projection(c, [Rows(xT, w, n0, 512, "dve", add(n0)) for n0 in (0, 512)])


def post_norm(c, columns=True):
    done = c.sig("rows_normed")
    norm_stage(c, [dict(src=c.x[:, :, :], dst=c.x[:, :, :], kind="ln", eps=LN_EPS, gain=c.gain[:, :],
                        bias=c.bias[:, :])], join=False, done=done)
    if columns:
        transpose_stage(c, [([c.x[:, t, (k + i) * P:(k + i + 1) * P] for i in range(4)], c.xT[:, k:k + 4, t * P:(t + 1) * P],
                             "dve" if k else "act") for t in range(TT) for k in (0, 4)],
                        join=False, before=lambda g: done.at(g // 2 + 1))
    c.join()


def rope(c, x, cos, sin, tmp, shape):
    nc = c.nc
    x1, x2 = x
    a, b, e, f = tmp
    nc.vector.tensor_tensor(a, x1, cos, ALU.mult)
    nc.vector.tensor_tensor(b, x2, sin, ALU.mult)
    nc.vector.tensor_tensor(e, x1, sin, ALU.mult)
    c.dve(nc.vector.tensor_tensor(f, x2, cos, ALU.mult))
    nc.vector.drain()
    nc.vector.tensor_tensor(x1, a, b, ALU.subtract)
    c.dve(nc.vector.tensor_tensor(x2, e, f, ALU.add))


def ab_mixer(c, cat, ctx):
    nc, arg = c.nc, c.arg
    sb = lambda name, shape, dt=F32: c.sb("ab_" + name, shape, dt, ctx)
    half = MLA_ROPE // 2
    u, v = sb("u", [P, TT, GM_W]), sb("v", [P, TT, GM_W])
    low = sb("low", [P, TT, MLA_QR + MLA_KVR + MLA_ROPE])
    lown = sb("lown", [P, TT, MLA_QR + MLA_KVR])
    lowT = sb("lowT", [P, (MLA_QR + MLA_KVR) // P, TOK])
    gm_g, gm_b = sb("gm_g", [P, GM_W]), sb("gm_b", [P, GM_W])
    low_g = sb("low_g", [P, MLA_QR + MLA_KVR])
    bs = sb("bs", [P, GM_G])
    pos_i, pos = sb("pos_i", [P, TT], I32), sb("pos", [P, TT])
    freq, turns = sb("freq", [P, half]), sb("turns", [P, TT, half])
    ang, over = sb("ang", [P, 2, TT, half]), sb("over", [P, TT, half])
    trig = sb("trig", [P, 2, TT, half])
    wsT = sb("wsT", [P, GM_G, P])
    qrow, krow = sb("qrow", [P, TT, MLA_H, MLA_QK]), sb("krow", [P, TT, MLA_H, MLA_QK])
    vrow = sb("vrow", [P, TT, MLA_H * MLA_V])
    qT, kT = sb("qT", [P, MLA_H, TOK]), c.xT
    tmp = [sb(f"rot{i}", [P, MLA_H * half]) for i in range(4)]
    load_params(c, [
        (gm_g[:, :], bcast(arg["ab_gm_ln_g"][0])), (gm_b[:, :], bcast(arg["ab_gm_ln_b"][0])),
        (low_g[:, 0:MLA_QR], bcast(arg["ab_mla_q_norm"][0])), (low_g[:, MLA_QR:], bcast(arg["ab_mla_kv_norm"][0])),
        (bs[:, :], arg["ab_gm_bs"][0].rearrange("g t -> t g")),
        (pos_i[:, :], arg["positions"][0].rearrange("(t p) -> p t", p=P))])
    w_in = arg["ab_w_in"][0]
    projection(c, [
        Rows(c.xT, w_in, 0, 512, "act", lambda r: nc.scalar.activation(u[:, :, :], r, ACT.Gelu_apprx_tanh)),
        Rows(c.xT, w_in, 512, 512, "act", lambda r: nc.scalar.activation(v[:, :, :], r, ACT.Gelu_apprx_tanh)),
        Rows(c.xT, w_in, 1024, 416, "dve", lambda r: nc.vector.tensor_copy(low[:, :, :], r))])

    angles = c.sig("angles_ready")
    two_pi = 2 * math.pi
    c1 = 6.28125
    c2 = float(np.float32(round((two_pi - c1) * 2 ** 20) / 2 ** 20))
    c3 = float(np.float32(two_pi - c1 - c2))
    big = float(1.5 * 2 ** 23)
    pi_low = float(np.nextafter(np.float32(math.pi), np.float32(0)))

    @c.block.vector
    def _(dve):
        for i in range(half):
            f = float(np.exp(np.float32(-math.log(ROPE_BASE)) * np.float32(i) / np.float32(half), dtype=np.float32))
            nc.vector.memset(freq[:, i:i + 1], f)
        c.dve(nc.vector.tensor_copy(pos[:, :], pos_i[:, :]))
        dve.drain()
        for t in range(TT):
            last = nc.vector.tensor_scalar(ang[:, 0, t, :], freq[:, :], pos[:, t:t + 1], None, ALU.mult)
        c.dve(last)
        dve.drain()
        a = ang[:, 0]
        c.dve(nc.vector.tensor_scalar(turns[:, :, :], a, 1.0 / two_pi, big, ALU.mult, ALU.add))
        c.dve(nc.vector.tensor_scalar(turns[:, :, :], turns[:, :, :], big, None, ALU.subtract))
        for part in (c1, c2, c3):
            c.dve(nc.vector.scalar_tensor_tensor(a, turns[:, :, :], -part, a, ALU.mult, ALU.add))
        c.dve(nc.vector.tensor_scalar(ang[:, 1], a, math.pi / 2, None, ALU.add))
        c.dve(nc.vector.tensor_scalar(over[:, :, :], ang[:, 1], math.pi, None, ALU.is_gt))
        c.dve(nc.vector.scalar_tensor_tensor(ang[:, 1], over[:, :, :], -two_pi, ang[:, 1], ALU.mult, ALU.add))
        both = ang[:, :, :, :].rearrange("p a t f -> p (a t f)")
        nc.vector.tensor_scalar(both, both, pi_low, -pi_low, ALU.min, ALU.max).then_inc(*angles.up())

    @c.block.scalar
    def _(act):
        act.wait_ge(*angles.at(1))
        nc.scalar.activation(trig[:, :, :, :], ang[:, :, :, :], ACT.Sin)

    ws_turned, ws_masked = c.sig("spatial_turned"), c.sig("spatial_masked")

    @c.block.tensor
    def _(pe):
        ws = c.ring.take(pe, arg["ab_gm_ws"][0].rearrange("g t s -> t g s"))
        for g in range(GM_G):
            last = nc.tensor.transpose(c.psum[:, 0, g * P:(g + 1) * P], ws[:, g, :], c.ident[:, :])
        last.then_inc(c.ring.used, 1)
        c.ws_tile = c.ring.tiles

    @c.block.vector
    def _(dve):
        dve.wait_ge(c.ring.used, c.ws_tile)
        nc.vector.tensor_tensor(wsT[:, :, :], c.psum[:, 0, :].rearrange("p (g t) -> p g t", g=GM_G),
                                c.tri01[:, :].unsqueeze(1).broadcast_to([P, GM_G, P]), ALU.mult)
    norm_stage(c, [
        dict(src=v[:, :, :], dst=v[:, :, :], kind="ln", eps=LN_EPS, gain=gm_g[:, :], bias=gm_b[:, :]),
        dict(src=low[:, :, 0:MLA_QR], dst=lown[:, :, 0:MLA_QR], kind="rms", eps=LN_EPS, gain=low_g[:, 0:MLA_QR], bias=None),
        dict(src=low[:, :, MLA_QR:MLA_QR + MLA_KVR], dst=lown[:, :, MLA_QR:], kind="rms", eps=LN_EPS,
             gain=low_g[:, MLA_QR:], bias=None)])
    rows_to_columns(c, lown, lowT, 3)

    mixed = c.sig("spatial_mixed")

    @c.block.tensor
    def _(pe):
        for t in range(TT):
            for g in range(GM_G):
                last = nc.tensor.matmul(c.psum[:, t, g * P:(g + 1) * P], wsT[:, g, :], v[:, t, g * P:(g + 1) * P],
                                        start=True, stop=True)
            last.then_inc(*mixed.up())

    @c.block.vector
    def _(dve):
        for t in range(TT):
            dve.wait_ge(*mixed.at(t + 1))
            for g in range(GM_G):
                s = slice(g * P, (g + 1) * P)
                nc.vector.scalar_tensor_tensor(cat[:, t, s], c.psum[:, t, s], bs[:, g:g + 1], u[:, t, s],
                                               ALU.add, ALU.mult)
    c.join()

    qf = qrow[:, :, :, :].rearrange("p t h d -> p t (h d)")

    def keep_keys(r):
        for t in range(TT):
            last = nc.vector.tensor_copy(krow[:, t, :, 0:MLA_NOPE], r[:, t, :].rearrange("p (h d) -> p h d", h=MLA_H))
            if t == 0:
                c.dve(last)
        return last
    projection(c, [
        Rows(lowT[:, 0:2, :], arg["ab_mla_w_uq"][0], 0, 512, "act", lambda r: nc.scalar.activation(qf[:, :, 0:512], r, ACT.Copy)),
        Rows(lowT[:, 0:2, :], arg["ab_mla_w_uq"][0], 512, 256, "act", lambda r: nc.scalar.activation(qf[:, :, 512:768], r, ACT.Copy)),
        Rows(lowT[:, 2:3, :], arg["ab_mla_w_uk"][0], 0, 512, "dve", keep_keys),
        Rows(lowT[:, 2:3, :], arg["ab_mla_w_uv"][0], 0, 512, "act", lambda r: nc.scalar.activation(vrow[:, :, :], r, ACT.Copy))])

    @c.block.vector
    def _(dve):
        kr = low[:, :, MLA_QR + MLA_KVR:]
        for t in range(TT):
            cos, sin = (trig[:, i, t, :].unsqueeze(1).broadcast_to([P, MLA_H, half]) for i in (1, 0))
            q = qrow[:, t, :, MLA_NOPE:]
            rope(c, (q[:, :, 0:half], q[:, :, half:]), cos, sin,
                 [x[:, :].rearrange("p (h d) -> p h d", h=MLA_H) for x in tmp], None)
            rope(c, (kr[:, t, 0:half], kr[:, t, half:]), trig[:, 1, t, :], trig[:, 0, t, :], [x[:, 0:half] for x in tmp], None)
            dve.drain()
            nc.vector.tensor_copy(krow[:, t, :, MLA_NOPE:], kr[:, t, :].unsqueeze(1).broadcast_to([P, MLA_H, MLA_ROPE]))
    c.join()
    transpose_stage(c, [([row[:, t, h, :] for h in (2 * g, 2 * g + 1) for t in range(TT)],
                         colT[0:MLA_QK, 2 * g:2 * g + 2, :].rearrange("p h t -> p (h t)"), who)
                        for row, colT, who in ((qrow, qT, "act"), (krow, kT, "dve")) for g in range(MLA_H // 2)])
    attention(c, [(t, 0) for t in range(TT)], MLA_H, MLA_V,
              q=lambda t, b, i: qT[0:MLA_QK, i, t * P:(t + 1) * P], k=lambda b, i, nk: kT[0:MLA_QK, i, 0:nk],
              v=lambda b, i, s: vrow[:, s, i * MLA_V:(i + 1) * MLA_V],
              out=lambda t, b: cat[:, t, GM_W:].rearrange("p (h d) -> p h d", h=MLA_H),
              scale=MLA_QK ** -0.5, bias=causal_bias(c, MLA_H), paired=False)



NSA_H, NSA_G, NSA_D = 16, 2, 64
NSA_HPG = NSA_H // NSA_G
CMP_LEN, CMP_STRIDE, CMP_HID = 32, 16, 256
NCMP = TOK // CMP_STRIDE - CMP_LEN // CMP_STRIDE + 1
C_MIX = NSA_H * NSA_D
NSA_KV = NSA_G * NSA_D
assert TOK // 64 <= 8 and TOK <= 512


def nsa_mixer(c, cat, ctx):
    nc, arg = c.nc, c.arg
    sb = lambda name, shape, dt=F32: c.sb("c_" + name, shape, dt, ctx)
    qT = sb("qT", [P, NSA_H // 2, TOK])
    kvT = sb("kvT", [P, 4, NSA_G, TOK])
    vs, vwg = sb("vs", [P, TT, NSA_KV]), sb("vwg", [P, TT, NSA_KV + 3 * NSA_H])
    blocks = sb("blocks", [P, 2, CMP_LEN // 2, NSA_G, NCMP])
    pos = sb("pos", [P, 2, CMP_LEN // 2])
    hid = sb("hid", [P, 2, CMP_HID // P, NSA_G * NCMP])
    w2 = sb("w2", [P, 2, CMP_HID // P, NSA_D])
    kc = sb("kc", [P, NSA_G * NCMP])
    vc = sb("vc", [NCMP, NSA_G, NSA_D])
    gate_b, gates = sb("gate_b", [P, 3 * NSA_H]), sb("gates", [P, TT, 3 * NSA_H])
    ends, ends01 = sb("ends", [P, TT, NCMP]), sb("ends01", [P, TT, NCMP])
    oc, osel = sb("oc", [P, TT, C_MIX]), sb("osel", [P, TT, C_MIX])
    pcT = sb("pcT", [NCMP, 2, NSA_HPG, P])
    sc = sb("sc", [P, TT, NSA_H, NCMP])
    red = sb("red", [P, TT, NSA_H])
    posv = arg["c_cmp_pos"][0].rearrange("i (j a) d -> a d i j", a=2)
    load_params(c, [(gate_b[:, :], bcast(arg["c_gate_b"][0])),
                    (w2[:, 0], k_tiles(arg["c_w_ck2"][0])), (w2[:, 1], k_tiles(arg["c_w_cv2"][0]))] +
                [(pos[a * 64:(a + 1) * 64, i, :], posv[a, :, i, :]) for a in range(2) for i in range(2)])

    @c.block.gpsimd
    def _(pool):
        nc.gpsimd.memset(ends[:, :, :], 0.0)
        c.pool(nc.gpsimd.memset(ends01[:, :, :], 1.0))
        pool.drain()
        for t in range(TT):
            for m, fill in ((ends, NEG), (ends01, 0.0)):
                nc.gpsimd.affine_select(out=m[:, t, :], in_=m[:, t, :], compare_op=ALU.is_ge, fill=fill,
                                        base=t * P - CMP_LEN + 1, pattern=[[-CMP_STRIDE, NCMP]], channel_multiplier=1)
    w_in = arg["c_w_in"][0]
    act_copy = lambda dst: (lambda r: nc.scalar.activation(dst, r, ACT.Copy))
    dve_copy = lambda dst: (lambda r: nc.vector.tensor_copy(dst, r))
    at = lambda i: C_MIX + i * NSA_KV

    def spread(i, copy):
        def take(r):
            for g in range(NSA_G):
                for a in range(2):
                    last = copy(kvT[a * 64:(a + 1) * 64, i, g, :], r[g * 64:(g + 1) * 64, 0, :])
            return last
        return take
    projection(c, [
        Cols(c.xT, w_in, at(0), NSA_KV, "act", spread(0, lambda d, r: nc.scalar.activation(d, r, ACT.Copy))),
        Cols(c.xT, w_in, at(1), NSA_KV, "dve", spread(1, nc.vector.tensor_copy)),
        Cols(c.xT, w_in, at(2), NSA_KV, "act", spread(2, lambda d, r: nc.scalar.activation(d, r, ACT.Copy))),
        Cols(c.xT, w_in, at(4), NSA_KV, "dve", spread(3, nc.vector.tensor_copy)),
        Rows(c.xT, w_in, at(3), NSA_KV, "act", act_copy(vs[:, :, :])),
        Rows(c.xT, w_in, at(5), NSA_KV + 3 * NSA_H, "dve", dve_copy(vwg[:, :, :]))] + [
        Cols(c.xT, w_in, j * 256, 256, "dve" if j % 2 else "act",
             (dve_copy if j % 2 else act_copy)(qT[:, 2 * j:2 * j + 2, :])) for j in range(4)])

    pair = CMP_LEN // 2
    built, hidden, squashed, compressed = c.sig("blocks_built"), c.sig("cmp_hidden"), c.sig("cmp_squashed"), c.sig("cmp_ready")

    @c.block.vector
    def _(dve):
        for i in range(2):
            for a in range(2):
                h = slice(a * 64, (a + 1) * 64)
                for g in range(NSA_G):
                    src = kvT[h, i, g, :].rearrange("p (m r) -> p r m", r=CMP_STRIDE)
                    for half in range(2):
                        js = slice(half * 8, half * 8 + 8)
                        last = nc.vector.tensor_tensor(
                            blocks[h, i, js, g, :], src[:, a:CMP_STRIDE:2, half:half + NCMP],
                            pos[h, i, js].unsqueeze(2).broadcast_to([64, 8, NCMP]), ALU.add)
            dve.drain().then_inc(*built.up())
        for t in range(TT):
            last = nc.vector.tensor_tensor(gates[:, t, :], vwg[:, t, NSA_KV:], gate_b[:, :], ALU.add)
        dve.drain().then_inc(*built.up())

    @c.block.tensor
    def _(pe):
        for i, name in enumerate(("c_w_ck1", "c_w_cv1")):
            pe.wait_ge(*built.at(i + 1))
            src = k_tiles(arg[name][0])
            for m in range(2):
                w1 = c.ring.take(pe, src[:, :, m * P:(m + 1) * P])
                for j in range(pair):
                    last = nc.tensor.matmul(c.psum[:, 2 * i + m, 0:NSA_G * NCMP], w1[:, j, :],
                                            blocks[:, i, j].rearrange("p g n -> p (g n)"), start=(j == 0), stop=(j == pair - 1))
                last.then_inc(c.ring.used, 1)
        c.cmp_tile = c.ring.tiles
        pe.wait_ge(*squashed.at(1))
        for m in range(2):
            last = nc.tensor.matmul(c.psum[0:64, 4, 0:NSA_G * NCMP], w2[:, 0, m, :], hid[:, 0, m, :], start=(m == 0), stop=(m == 1))
        last.then_inc(*compressed.up())
        for m in range(2):
            last = nc.tensor.matmul(c.psum[64:128, 5, 0:NSA_G * NCMP], w2[:, 0, m, :], hid[:, 0, m, :], start=(m == 0), stop=(m == 1))
        last.then_inc(*compressed.up())
        for g in range(NSA_G):
            for m in range(2):
                last = nc.tensor.matmul(c.psum[0:NCMP, 6 + g, 0:NSA_D], hid[:, 1, m, g * NCMP:(g + 1) * NCMP], w2[:, 1, m, :],
                                        start=(m == 0), stop=(m == 1))
        last.then_inc(*compressed.up())

    @c.block.scalar
    def _(act):
        act.wait_ge(c.ring.used, c.cmp_tile)
        for i in range(2):
            last = nc.scalar.activation(hid[:, i], c.psum[:, 2 * i:2 * i + 2, 0:NSA_G * NCMP], ACT.Gelu_apprx_tanh)
        act.drain().then_inc(*squashed.up())
        act.wait_ge(*built.at(3))
        nc.scalar.activation(gates[:, :, :], gates[:, :, :], ACT.Sigmoid)

    @c.block.vector
    def _(dve):
        dve.wait_ge(*compressed.at(3))
        nc.vector.tensor_copy(kc[0:64, :], c.psum[0:64, 4, 0:NSA_G * NCMP])
        nc.vector.tensor_copy(kc[64:128, :], c.psum[64:128, 5, 0:NSA_G * NCMP])
        for g in range(NSA_G):
            nc.vector.tensor_copy(vc[:, g, :], c.psum[0:NCMP, 6 + g, 0:NSA_D])
    c.join()

    scored, softened = c.sig("cmp_scores"), c.sig("cmp_probs")
    exped = c.sig("cmp_exp")
    in_exp = c.sig("cmp_centred")

    @c.block.tensor
    def _(pe):
        for t in range(TT):
            for h in range(NSA_H):
                g, a = h // NSA_HPG, h % 2
                rows = slice(a * 64, a * 64 + 64)
                last = nc.tensor.matmul(c.psum[:, 2 * a + t, (h // 2) * NCMP:(h // 2 + 1) * NCMP],
                                        qT[rows, h // 2, t * P:(t + 1) * P], kc[rows, g * NCMP:(g + 1) * NCMP], start=True, stop=True)
        last.then_inc(*scored.up())

    @c.block.vector
    def _(dve):
        dve.wait_ge(*scored.at(1))
        for t in range(TT):
            for a in range(2):
                nc.vector.scalar_tensor_tensor(
                    sc[:, t, a:NSA_H:2, :], c.psum[:, 2 * a + t, 0:8 * NCMP].rearrange("p (h n) -> p h n", n=NCMP), NSA_D ** -0.5,
                    ends[:, t, :].unsqueeze(1).broadcast_to([P, 8, NCMP]), ALU.mult, ALU.add)
        dve.drain()
        c.dve(nc.vector.tensor_reduce(red[:, :, :], sc[:, :, :, :], AX_X, ALU.max))
        nc.vector.tensor_tensor(sc[:, :, :, :], sc[:, :, :, :], red[:, :, :].unsqueeze(3).broadcast_to([P, TT, NSA_H, NCMP]),
                                ALU.subtract).then_inc(*in_exp.up())
        dve.wait_ge(*exped.at(1))
        c.dve(nc.vector.tensor_reduce(red[:, :, :], sc[:, :, :, :], AX_X, ALU.add))
        c.dve(nc.vector.reciprocal(red[:, :, :], red[:, :, :]))
        c.dve(nc.vector.tensor_tensor(sc[:, :, :, :], sc[:, :, :, :], red[:, :, :].unsqueeze(3).broadcast_to([P, TT, NSA_H, NCMP]), ALU.mult))
        nc.vector.tensor_tensor(sc[:, :, :, :], sc[:, :, :, :], ends01[:, :, :].unsqueeze(2).broadcast_to([P, TT, NSA_H, NCMP]),
                                ALU.mult).then_inc(*softened.up())

    @c.block.scalar
    def _(act):
        act.wait_ge(*in_exp.at(1))
        nc.scalar.activation(sc[:, :, :, :], sc[:, :, :, :], ACT.Exp).then_inc(*exped.up())

    turned, copied, out_ready, taken = c.sig("cmp_turned"), c.sig("cmp_copied"), c.sig("cmp_out"), c.sig("cmp_taken")

    @c.block.tensor
    def _(pe):
        pe.wait_ge(*softened.at(1))
        for t in range(TT):
            for g in range(NSA_G):
                j = 2 * t + g
                if j >= 2:
                    pe.wait_ge(*copied.at(j - 1))
                for i in range(NSA_HPG):
                    last = nc.tensor.transpose(c.psum[0:NCMP, 4 + 2 * (j % 2) + i // 4, (i % 4) * P:(i % 4 + 1) * P],
                                               sc[:, t, g * NSA_HPG + i, :], c.ident[:, :])
                last.then_inc(*turned.up())
                pe.wait_ge(*copied.at(j + 1))
                if j >= 4:
                    pe.wait_ge(*taken.at(j - 3))
                for i in range(NSA_HPG):
                    last = nc.tensor.matmul(c.psum[:, j, i * NSA_D:(i + 1) * NSA_D], pcT[:, j % 2, i, :], vc[:, g, :], start=True, stop=True)
                last.then_inc(*out_ready.up())

    @c.block.vector
    def _(dve):
        for j in range(4):
            t, g = j // 2, j % 2
            dve.wait_ge(*turned.at(j + 1))
            if j >= 2:
                dve.wait_ge(*out_ready.at(j - 1))
            b0 = [4, 6][j % 2]
            nc.vector.tensor_copy(pcT[:, j % 2].rearrange("p (b i) t -> p b (i t)", b=2), c.psum[0:NCMP, b0:b0 + 2, :]).then_inc(*copied.up())
            dve.wait_ge(*out_ready.at(j + 1))
            gt = gates[:, t, g * 8:g * 8 + 8].unsqueeze(2).broadcast_to([P, 8, NSA_D])
            nc.vector.tensor_tensor(oc[:, t, g * 512:(g + 1) * 512].rearrange("p (h d) -> p h d", d=NSA_D),
                                    c.psum[:, j, :].rearrange("p (h d) -> p h d", d=NSA_D), gt, ALU.mult).then_inc(*taken.up())
    c.join()
    for branch, (ki, vals) in enumerate(((2, vs), (3, vwg))):
        attention(c, [(t, g) for t in range(TT) for g in range(NSA_G)], NSA_HPG, NSA_D,
                  q=lambda t, g, i: qT[(i % 2) * 64:(i % 2) * 64 + 64, g * 4 + i // 2, t * P:(t + 1) * P],
                  k=lambda g, i, nk: kvT[(i % 2) * 64:(i % 2) * 64 + 64, ki, g, 0:nk],
                  v=lambda g, i, s: vals[:, s, g * NSA_D:(g + 1) * NSA_D],
                  out=lambda t, g: (osel, cat)[branch][:, t, g * 512:(g + 1) * 512].rearrange("p (h d) -> p h d", h=8),
                  scale=NSA_D ** -0.5, bias=causal_bias(c, 8))

    @c.block.vector
    def _(dve):
        for branch, o in ((1, osel), (2, cat)):
            for t in range(TT):
                gt = gates[:, t, branch * 16:branch * 16 + 16].unsqueeze(2).broadcast_to([P, 16, NSA_D])
                ov = o[:, t, :].rearrange("p (h d) -> p h d", d=NSA_D)
                nc.vector.tensor_tensor(ov, ov, gt, ALU.mult)
            dve.drain()
            nc.vector.tensor_tensor(o[:, :, :], o[:, :, :], (oc, osel)[branch - 1][:, :, :], ALU.add)
            dve.drain()
    c.join()



CH = 256


def stream_ffn(c, n, gate, up, down, ctx):
    nc, ring = c.nc, c.ring
    y = c.x
    squashed = c.sb("ffn_squashed", [P, 2, 2 * TOK], ctx=ctx)
    hidden = c.sb("ffn_hidden", [P, 2, 2, TOK], ctx=ctx)
    gate_squashed, hidden_ready, added = c.sig("gate_squashed"), c.sig("hidden_ready"), c.sig("chunk_added")
    p0 = ring.tiles
    loaded0 = list(ring.loaded)
    ring.plan.append(("stream", p0, n, gate, up, down))
    ring.tiles += 3 * n
    for x in range(p0, p0 + 3 * n):
        ring.loaded[x % RING] += 16
    FIRST, U = 1, 4
    loops = max(0, (n - 1 - FIRST) // U)
    rest = range(FIRST + U * loops, n - 1)

    def nth_load(x):
        first = x - (x - p0) // RING * RING
        return loaded0[x % RING] + 16 * ((x - first) // RING + 1)

    def gate_tile(j):
        return p0 if j == 0 else p0 + 2 + 3 * (j - 1)

    def up_tile(j):
        return gate_tile(j) + 1

    def down_tile(j):
        return p0 + 2 + 3 * j + (2 if j < n - 1 else 0)

    def two_products(pe, j, i):
        if j >= 2:
            pe.wait_ge(hidden_ready.sem, hidden_ready.base + (j - 1) + U * i)
        for tile, bank in ((gate_tile(j), 0), (up_tile(j), 2)):
            pe.wait_ge(ring.full[tile % RING], nth_load(tile) + 16 * i)
            w = ring.view(tile, KD, CH)
            for m in range(2):
                for k in range(KD):
                    last = nc.tensor.matmul(c.psum[:, bank + j % 2, m * TOK:(m + 1) * TOK], w[:, k, m * P:(m + 1) * P],
                                            c.xT[:, k, :], start=(k == 0), stop=(k == KD - 1))
            last.then_inc(ring.used, 1)

    def third_product(pe, j, i):
        tile = down_tile(j)
        pe.wait_ge(hidden_ready.sem, hidden_ready.base + j + 1 + U * i)
        if j >= 1:
            pe.wait_ge(added.sem, added.base + 2 * j + 2 * U * i)
        pe.wait_ge(ring.full[tile % RING], nth_load(tile) + 16 * i)
        w = ring.view(tile, 2, D)
        for t in range(TT):
            for h in range(2):
                for m in range(2):
                    last = nc.tensor.matmul(c.psum[:, 4 + 2 * t + h, :], hidden[:, j % 2, m, t * P:(t + 1) * P],
                                            w[:, m, h * 512:(h + 1) * 512], start=(m == 0), stop=(m == 1))
        last.then_inc(ring.used, 1)

    def squash(act, j, i):
        act.wait_ge(ring.used, gate_tile(j) + 1 + 3 * U * i)
        nc.scalar.activation(squashed[:, j % 2, :], c.psum[:, j % 2, :], ACT.Silu).then_inc(gate_squashed.sem, 1)

    def combine(dve, j, i):
        dve.wait_ge(ring.used, up_tile(j) + 1 + 3 * U * i)
        dve.wait_ge(gate_squashed.sem, gate_squashed.base + j + 1 + U * i)
        nc.vector.tensor_tensor(hidden[:, j % 2].rearrange("p m t -> p (m t)"), squashed[:, j % 2, :],
                                c.psum[:, 2 + j % 2, :], ALU.mult).then_inc(hidden_ready.sem, 1)

    def add(dve, j, i):
        dve.wait_ge(ring.used, down_tile(j) + 1 + 3 * U * i)
        for t in range(TT):
            part = c.psum[:, 4 + 2 * t:6 + 2 * t, :].rearrange("p h n -> p (h n)")
            if j >= 1:
                dve.wait_ge(added.sem, added.base + 2 * j - 1 + t + 2 * U * i)
            nc.vector.tensor_tensor(y[:, t, :], part, y[:, t, :], ALU.add).then_inc(added.sem, 1)

    @c.block.tensor
    def _(pe):
        two_products(pe, 0, 0)
        for j in range(FIRST):
            two_products(pe, j + 1, 0)
            third_product(pe, j, 0)
        if loops:
            with pe.Fori(0, loops) as i:
                for j in range(FIRST, FIRST + U):
                    two_products(pe, j + 1, i)
                    third_product(pe, j, i)
        for j in rest:
            two_products(pe, j + 1, 0)
            third_product(pe, j, 0)
        third_product(pe, n - 1, 0)

    @c.block.scalar
    def _(act):
        for j in range(FIRST + 1):
            squash(act, j, 0)
        if loops:
            with act.Fori(0, loops) as i:
                for j in range(FIRST, FIRST + U):
                    squash(act, j + 1, i)
        for j in rest:
            squash(act, j + 1, 0)

    @c.block.vector
    def _(dve):
        combine(dve, 0, 0)
        for j in range(FIRST):
            combine(dve, j + 1, 0)
            add(dve, j, 0)
        if loops:
            with dve.Fori(0, loops) as i:
                for j in range(FIRST, FIRST + U):
                    combine(dve, j + 1, i)
                    add(dve, j, i)
        for j in rest:
            combine(dve, j + 1, 0)
            add(dve, j, 0)
        add(dve, n - 1, 0)
    gate_squashed.count += n
    hidden_ready.count += n
    added.count += 2 * n
    c.join()


def logits_stage(c, wr, br, n, logits):
    nc = c.nc
    ready = c.sig("router_logits")

    @c.block.tensor
    def _(pe):
        for t in range(TT):
            for k in range(KD):
                last = nc.tensor.matmul(c.psum[:, t, 0:n], c.xT[:, k, t * P:(t + 1) * P], wr[:, k, :],
                                        start=(k == 0), stop=(k == KD - 1))
        last.then_inc(*ready.up())

    @c.block.vector
    def _(dve):
        dve.wait_ge(*ready.at(1))
        c.dve(nc.vector.tensor_tensor(logits, c.psum[:, 0:TT, 0:n], br.unsqueeze(1).broadcast_to([P, TT, n]), ALU.add))


SLOTS = 2 * TOK


def sparse_experts(c, n, chunks, unroll, narrow, rows, oh, pw, gate, up, down, outT, alpha, ctx, params=()):
    nc, ring = c.nc, c.ring
    width = SLOTS + TOK
    sb = lambda name, shape, dt=F32: c.sb("e_" + name, shape, dt, ctx)
    if outT is None:
        outT = sb("outT", [P, KD, width])
    xg = sb("xg", [P, KD, width])
    squashed, hidden = sb("squashed", [P, 2, 2, TOK]), sb("hidden", [P, 2, 2, TOK])
    member, place, cnt = sb("member", [P, TT, n]), sb("place", [P, TT, n]), sb("cnt", [P, n])
    off, ends, prod = sb("off", [P, n]), sb("ends", [P, n]), sb("prod", [P, TT, 2, n])
    slot = sb("slot", [P, TT, 2])
    cnt_i, off_i = sb("cnt_i", [1, n], I32), sb("off_i", [1, n], I32)
    flat = outT[:, :, :].rearrange("p k s -> p (k s)")
    G = flat[:, 2048:3072].rearrange("p (t s) -> p t s", t=TT)
    GW = flat[:, 3072:4096].rearrange("p (t s) -> p t s", t=TT)
    iota_i, iota = flat[:, 4096:4608].bitcast(I32), flat[:, 4608:5120]
    part = flat[:, 5120:6144].rearrange("p (t s) -> p t s", t=TT)
    spread = c.PT[:, :, :].rearrange("p a b -> p (a b)").rearrange("p (s t) -> p s t", t=TOK)
    if params:
        load_params(c, params)

    joined, ranked, iotas, matrices = c.sig("members_ready"), c.sig("ranks_ready"), c.sig("iota_ready"), c.sig("matrices_ready")
    gathered, padded = c.sig("rows_gathered"), c.sig("gather_copied")

    @c.block.gpsimd
    def _(pool):
        nc.gpsimd.iota(iota_i, pattern=[[1, SLOTS]], base=0, channel_multiplier=0).then_inc(*iotas.up())
        nc.gpsimd.memset(xg[:, :, SLOTS:], 0.0)

    @c.block.vector
    def _(dve):
        nc.vector.tensor_tensor(member[:, :, :], oh[:, :, 0, :], oh[:, :, 1, :], ALU.add).then_inc(*joined.up())
        dve.wait_ge(*iotas.at(1))
        c.dve(nc.vector.tensor_copy(iota, iota_i))
        dve.wait_ge(*ranked.at(1))
        c.dve(nc.vector.tensor_copy(cnt[:, :], c.psum[:, 2, 0:n]))
        c.dve(nc.vector.tensor_tensor_scan(ends[:, :], c.ones[:, 0:n], cnt[:, :], 0.0, ALU.mult, ALU.add))
        c.dve(nc.vector.tensor_tensor(off[:, :], ends[:, :], cnt[:, :], ALU.subtract))
        nc.vector.tensor_copy(cnt_i[:, :], cnt[0:1, :])
        nc.vector.tensor_copy(off_i[:, :], off[0:1, :])
        for t in range(TT):
            last = nc.vector.scalar_tensor_tensor(place[:, t, :], c.psum[:, t, 0:n], -1.0, off[:, :], ALU.add, ALU.add)
        c.dve(last)
        dve.drain()
        c.dve(nc.vector.tensor_tensor(prod[:, :, :, :], oh[:, :, :, :], place[:, :, :].unsqueeze(2).broadcast_to([P, TT, 2, n]), ALU.mult))
        c.dve(nc.vector.tensor_reduce(slot[:, :, :], prod[:, :, :, :], AX_X, ALU.add))
        for t in range(TT):
            nc.vector.tensor_scalar(G[:, t, :], iota, slot[:, t, 0:1], None, ALU.is_equal)
            nc.vector.tensor_scalar(GW[:, t, :], iota, slot[:, t, 0:1], pw[:, t, 0:1], ALU.is_equal, ALU.mult)
            nc.vector.tensor_scalar(part[:, t, :], iota, slot[:, t, 1:2], pw[:, t, 1:2], ALU.is_equal, ALU.mult)
        dve.drain()
        for t in range(TT):
            nc.vector.scalar_tensor_tensor(G[:, t, :], iota, slot[:, t, 1:2], G[:, t, :], ALU.is_equal, ALU.add)
        nc.vector.tensor_tensor(GW, GW, part, ALU.add)
        dve.drain().then_inc(*matrices.up())

    @c.block.tensor
    def _(pe):
        pe.wait_ge(*joined.at(1))
        nc.tensor.matmul(c.psum[:, 0, 0:n], c.tri01[:, :], member[:, 0, :], start=True, stop=True)
        nc.tensor.matmul(c.psum[:, 1, 0:n], c.ones[:, :], member[:, 0, :], start=True, stop=False)
        nc.tensor.matmul(c.psum[:, 1, 0:n], c.tri01[:, :], member[:, 1, :], start=False, stop=True)
        for t in range(TT):
            last = nc.tensor.matmul(c.psum[:, 2, 0:n], c.ones[:, :], member[:, t, :], start=(t == 0), stop=(t == TT - 1))
        last.then_inc(*ranked.up())
        pe.wait_ge(*matrices.at(1))
        for k in range(KD):
            for t in range(TT):
                last = nc.tensor.matmul(c.psum[:, k, :], rows[:, t, k * P:(k + 1) * P], G[:, t, :], start=(t == 0), stop=(t == TT - 1))
            last.then_inc(*gathered.up())

    @c.block.vector
    def _(dve):
        for k in range(0, KD, 2):
            dve.wait_ge(*gathered.at(k + 1))
            nc.vector.tensor_copy(xg[:, k, 0:SLOTS], c.psum[:, k, :])

    @c.block.scalar
    def _(act):
        for k in range(1, KD, 2):
            act.wait_ge(*gathered.at(k + 1))
            nc.scalar.activation(xg[:, k, 0:SLOTS], c.psum[:, k, :], ACT.Copy)
    c.join()
    transpose_stage(c, [([GW[:, t, s * P:(s + 1) * P] for s in (2 * g, 2 * g + 1) for t in range(TT)],
                         spread[:, 2 * g:2 * g + 2, :].rearrange("p s t -> p (s t)"), ("act", "dve")[g]) for g in range(2)])

    windowed, gate_squashed = c.sig("window_ready"), c.sig("gate_squashed")
    hidden_ready, written = c.sig("hidden_ready"), c.sig("expert_written")
    xw = c.S
    ahead = chunks == 1
    bufs = 2 if ahead else 1
    per = 3 if ahead else -(-3 * chunks // RING) * RING
    spare = per - 3 * chunks
    assert per * unroll % RING == 0
    p0 = ring.tiles
    loaded0 = list(ring.loaded)
    turns = (n - 1) // unroll if ahead else n // unroll
    loop_end = turns * unroll
    ring.plan.append(("experts", p0, n, chunks, unroll, turns, per, gate, up, down))
    ring.tiles += n * per

    def gate_tile(x, j=0):
        if ahead:
            return p0 if x == 0 else p0 + 2 + 3 * (x - 1)
        return p0 + x * per + (0 if j == 0 else 2 + 3 * (j - 1))

    def down_tile(x, j=0):
        if ahead:
            return p0 + 2 + 3 * x + (2 if x < n - 1 else 0)
        return p0 + x * per + 2 + 3 * j + (2 if j < chunks - 1 else 0)

    real = [p0 + e * per + k for e in range(n) for k in range(3 * chunks)]
    turn_loads = [16 * sum(1 for t in real if t % RING == q and t < p0 + per * unroll) for q in range(RING)]
    for t in real:
        ring.loaded[t % RING] += 16

    def landed(pe, tile, i):
        q = tile % RING
        pe.wait_ge(ring.full[q], turn_loads[q] * i + (loaded0[q] + 16 * sum(1 for t in real if t % RING == q and t <= tile)))

    def used(eng, tile, i):
        eng.wait_ge(ring.used, (per * unroll) * i + (tile + 1))

    def nth(signal, k, i, step):
        return signal.sem, step * i + (signal.base + 1 + k)

    def by_width(eng, x, i, body):
        e = x + unroll * i
        count = eng.value_load(cnt_i[0:1, bass.ds(e, 1)], min_val=0, max_val=TOK)
        with eng.If(count < narrow + 1):
            body(narrow)
        with eng.Else():
            body(TOK)

    def offset(eng, x, i):
        return eng.value_load(off_i[0:1, bass.ds(x + unroll * i, 1)], min_val=0, max_val=SLOTS)

    cu = chunks * unroll

    def two_products(pe, x, j, i, w):
        q = x * chunks + j
        if ahead or j >= 2:
            pe.wait_ge(*nth(hidden_ready, max(0, q - 1), i, cu))
        if j == 0:
            pe.wait_ge(*nth(windowed, x + 1, i, unroll))
        par = (x if ahead else j) % 2
        for tile, bank in ((gate_tile(x, j), 0), (gate_tile(x, j) + 1, 2)):
            landed(pe, tile, i)
            wt = ring.view(tile, KD, CH)
            for m in range(2):
                for k in range(KD):
                    last = nc.tensor.matmul(c.psum[:, bank + par, m * TOK:m * TOK + w], wt[:, k, m * P:(m + 1) * P],
                                            xw[:, x % bufs, k, 0:w], start=(k == 0), stop=(k == KD - 1))
            last.then_inc(ring.used, 1)

    def third_product(pe, x, j, i, w):
        tile = down_tile(x, j)
        par = (x if ahead else j) % 2
        pe.wait_ge(*nth(hidden_ready, x * chunks + j + 1, i, cu))
        if j == 0:
            pe.wait_ge(*nth(written, x, i, unroll))
        landed(pe, tile, i)
        wt = ring.view(tile, 2, D)
        for k in range(KD):
            for m in range(2):
                last = nc.tensor.matmul(c.psum[:, 4 + k // 2, (k % 2) * TOK:(k % 2) * TOK + w], wt[:, m, k * P:(k + 1) * P],
                                        hidden[:, par, m, 0:w], start=(j == 0 and m == 0 and k % 2 == 0),
                                        stop=(j == chunks - 1 and m == 1), skip_group_check=True)
        last.then_inc(ring.used, 1 + (spare if j == chunks - 1 else 0))

    def halves(bank, w):
        return c.psum[:, bank, :].rearrange("p (m t) -> p m t", m=2)[:, :, 0:w]

    def window(act, x, i):
        if x >= bufs:
            used(act, gate_tile(x - bufs, chunks - 1) + 1, i)
        elif not ahead:
            act.wait_ge(ring.used, per * i + (p0 - per + gate_tile(0, chunks - 1) + 2 - p0))
        o = offset(act, x, i)
        by_width(act, x, i, lambda w: nc.scalar.activation(
            xw[:, x % bufs, :, 0:w], xg[:, :, bass.ds(o, w)], ACT.Copy).then_inc(windowed.sem, 1))

    def squash(act, x, j, i, w):
        par = (x if ahead else j) % 2
        used(act, gate_tile(x, j), i)
        nc.scalar.activation(squashed[:, par, :, 0:w], halves(par, w), ACT.Silu).then_inc(gate_squashed.sem, 1)

    def combine(dve, x, j, i, w):
        par = (x if ahead else j) % 2
        used(dve, gate_tile(x, j) + 1, i)
        dve.wait_ge(*nth(gate_squashed, x * chunks + j, i, cu))
        nc.vector.tensor_tensor(hidden[:, par, :, 0:w], squashed[:, par, :, 0:w], halves(2 + par, w),
                                ALU.mult).then_inc(hidden_ready.sem, 1)

    def write(dve, x, i, w, o):
        used(dve, down_tile(x, chunks - 1), i)
        dve.wait_ge(*nth(written, x, i, unroll))
        nc.vector.tensor_copy(outT[:, :, bass.ds(o, w)],
                              c.psum[:, 4:8, :].rearrange("p b (m t) -> p (b m) t", m=2)[:, :, 0:w]).then_inc(written.sem, 1)

    def steps(eng, first, step):
        first()
        with eng.Fori(0, turns) as i:
            for x in range(unroll):
                step(x, i)
        for x in range(loop_end, n):
            step(x, 0)

    @c.block.tensor
    def _(pe):
        def step(x, i):
            if not ahead:
                def expert(w):
                    two_products(pe, x, 0, i, w)
                    for j in range(chunks):
                        if j < chunks - 1:
                            two_products(pe, x, j + 1, i, w)
                        third_product(pe, x, j, i, w)
                by_width(pe, x, i, expert)
                return
            if x + 1 < n:
                by_width(pe, x + 1, i, lambda w: two_products(pe, x + 1, 0, i, w))
            by_width(pe, x, i, lambda w: third_product(pe, x, 0, i, w))
        steps(pe, lambda: ahead and by_width(pe, 0, 0, lambda w: two_products(pe, 0, 0, 0, w)), step)

    @c.block.scalar
    def _(act):
        nc.scalar.activation(squashed[:, 0, 0, 0:1], c.ones[:, 0:1], ACT.Copy).then_inc(windowed.sem, 1)

        def first():
            if ahead:
                window(act, 0, 0)
                window(act, 1, 0)
                by_width(act, 0, 0, lambda w: squash(act, 0, 0, 0, w))
                window(act, 2, 0)

        def step(x, i):
            if ahead:
                if x + 1 < n:
                    by_width(act, x + 1, i, lambda w: squash(act, x + 1, 0, i, w))
                if x + 3 < n:
                    window(act, x + 3, i)
            else:
                window(act, x, i)
                by_width(act, x, i, lambda w: [squash(act, x, j, i, w) for j in range(chunks)])
        steps(act, first, step)

    @c.block.vector
    def _(dve):
        nc.vector.memset(outT[:, 0, 0:1], 0.0).then_inc(written.sem, 1)
        nc.vector.memset(hidden[:, 0, 0, 0:1], 0.0).then_inc(hidden_ready.sem, 1)
        dve.drain()

        def step(x, i):
            o = offset(dve, x, i)
            if ahead:
                if x + 1 < n:
                    by_width(dve, x + 1, i, lambda w: combine(dve, x + 1, 0, i, w))
                by_width(dve, x, i, lambda w: write(dve, x, i, w, o))
            else:
                by_width(dve, x, i, lambda w: [combine(dve, x, j, i, w) for j in range(chunks)] and write(dve, x, i, w, o))
        steps(dve, lambda: ahead and by_width(dve, 0, 0, lambda w: combine(dve, 0, 0, 0, w)), step)
    windowed.count += n + 1
    gate_squashed.count += n * chunks
    hidden_ready.count += n * chunks + 1
    written.count += n + 1
    c.join()

    slot_rows = c.S[:, :, :, :].rearrange("p a b t -> p (a b t)").rearrange("p (s d) -> p s d", d=D)
    transpose_stage(c, [([outT[:, 4 * h + k, s * P:(s + 1) * P] for k in range(4)], slot_rows[:, s, h * 512:(h + 1) * 512],
                         ("act", "dve")[h]) for s in range(SLOTS // P) for h in range(2)])
    mixed = c.sig("experts_mixed")

    @c.block.tensor
    def _(pe):
        for t in range(TT):
            for h in range(2):
                for s in range(SLOTS // P):
                    last = nc.tensor.matmul(c.psum[:, 2 * t + h, :], spread[:, s, t * P:(t + 1) * P],
                                            slot_rows[:, s, h * 512:(h + 1) * 512], start=(s == 0), stop=(s == SLOTS // P - 1))
            last.then_inc(*mixed.up())

    @c.block.vector
    def _(dve):
        for t in range(TT):
            dve.wait_ge(*mixed.at(t + 1))
            nc.vector.scalar_tensor_tensor(c.x[:, t, :], c.x[:, t, :], alpha,
                                           c.psum[:, 2 * t:2 * t + 2, :].rearrange("p h n -> p (h n)"), ALU.mult, ALU.add)
    c.join()


MOE_G, MOE_E = 4, 8


def route_hier(c, layer, ctx):
    nc, arg = c.nc, c.arg
    sb = lambda name, shape, dt=F32: c.sb(f"r{layer}_" + name, shape, dt, ctx)
    n = MOE_G + MOE_G * MOE_E
    wr, br = sb("wr", [P, KD, n]), sb("br", [P, n])
    lg = sb("lg", [P, TT, n])
    g8, top, topi = sb("g8", [P, TT, 8]), sb("top", [P, TT, 8]), sb("topi", [P, TT, 8], U32)
    idx = sb("idx", [P, TT, 2])
    iota, iota_i = sb("iota", [P, 8]), sb("iota_i", [P, 8], I32)
    ohg, eg, gw = sb("ohg", [P, TT, MOE_G]), sb("eg", [P, TT, MOE_G]), sb("gw", [P, TT, 1])
    prod, es, red = sb("prod", [P, TT, MOE_G, MOE_E]), sb("es", [P, TT, MOE_E]), sb("red", [P, TT, 1])
    pw, oh8 = sb("pw", [P, TT, 2]), sb("oh8", [P, TT, 2, MOE_E])
    oh = sb("oh", [P, TT, 2, MOE_G * MOE_E])
    load_params(c, [(wr[:, :, 0:MOE_G], k_tiles(arg["moe_w_rg"][layer])), (wr[:, :, MOE_G:], k_tiles(arg["moe_w_re"][layer])),
                    (br[:, 0:MOE_G], bcast(arg["moe_b_rg"][layer])), (br[:, MOE_G:], bcast(arg["moe_b_re"][layer]))])
    iotas = c.sig("iota_ready")

    @c.block.gpsimd
    def _(pool):
        nc.gpsimd.iota(iota_i[:, :], pattern=[[1, 8]], base=0, channel_multiplier=0).then_inc(*iotas.up())
    c.join()
    logits_stage(c, wr, br[:, :], n, lg[:, :, :])
    centred, exped = c.sig("router_centred"), c.sig("router_exp")

    @c.block.vector
    def _(dve):
        c.dve(nc.vector.tensor_copy(iota[:, :], iota_i[:, :]))
        c.dve(nc.vector.memset(g8[:, :, :], -3e38))
        c.dve(nc.vector.tensor_copy(g8[:, :, 0:MOE_G], lg[:, :, 0:MOE_G]))
        for t in range(TT):
            c.dve(nc.vector.max(top[:, t, :], g8[:, t, :]))
            c.dve(nc.vector.max_index(topi[:, t, :], top[:, t, :], g8[:, t, :]))
        c.dve(nc.vector.tensor_copy(idx[:, :, 0:1], topi[:, :, 0:1]))
        for t in range(TT):
            c.dve(nc.vector.tensor_scalar(ohg[:, t, :], iota[:, 0:MOE_G], idx[:, t, 0:1], None, ALU.is_equal))
        c.dve(nc.vector.tensor_tensor(eg[:, :, :], lg[:, :, 0:MOE_G], top[:, :, 0:1].broadcast_to([P, TT, MOE_G]), ALU.subtract))
        c.dve(nc.vector.tensor_tensor(prod[:, :, :, :], lg[:, :, MOE_G:].rearrange("p t (g e) -> p t g e", g=MOE_G),
                                      ohg[:, :, :].unsqueeze(3).broadcast_to([P, TT, MOE_G, MOE_E]), ALU.mult))
        c.dve(nc.vector.tensor_reduce(es[:, :, :], prod[:, :, :, :].rearrange("p t g e -> p t e g"), AX_X, ALU.add))
        c.dve(nc.vector.tensor_reduce(red[:, :, :], es[:, :, :], AX_X, ALU.max))
        nc.vector.tensor_tensor(es[:, :, :], es[:, :, :], red[:, :, :].broadcast_to([P, TT, MOE_E]), ALU.subtract).then_inc(*centred.up())
        dve.wait_ge(*exped.at(1))
        c.dve(nc.vector.tensor_reduce(gw[:, :, :], eg[:, :, :], AX_X, ALU.add))
        c.dve(nc.vector.reciprocal(gw[:, :, :], gw[:, :, :]))
        c.dve(nc.vector.tensor_reduce(red[:, :, :], es[:, :, :], AX_X, ALU.add))
        c.dve(nc.vector.reciprocal(red[:, :, :], red[:, :, :]))
        c.dve(nc.vector.tensor_tensor(es[:, :, :], es[:, :, :], red[:, :, :].broadcast_to([P, TT, MOE_E]), ALU.mult))
        for t in range(TT):
            c.dve(nc.vector.max(top[:, t, :], es[:, t, :]))
            c.dve(nc.vector.max_index(topi[:, t, :], top[:, t, :], es[:, t, :]))
        c.dve(nc.vector.tensor_copy(idx[:, :, :], topi[:, :, 0:2]))
        c.dve(nc.vector.tensor_reduce(red[:, :, :], top[:, :, 0:2], AX_X, ALU.add))
        c.dve(nc.vector.reciprocal(red[:, :, :], red[:, :, :]))
        c.dve(nc.vector.tensor_tensor(red[:, :, :], red[:, :, :], gw[:, :, :], ALU.mult))
        c.dve(nc.vector.tensor_tensor(pw[:, :, :], top[:, :, 0:2], red[:, :, :].broadcast_to([P, TT, 2]), ALU.mult))
        for t in range(TT):
            for a in range(2):
                last = nc.vector.tensor_scalar(oh8[:, t, a, :], iota[:, :], idx[:, t, a:a + 1], None, ALU.is_equal)
        dve.drain()
        for a in range(2):
            last = nc.vector.tensor_tensor(oh[:, :, a, :].rearrange("p t (g e) -> p t g e", g=MOE_G),
                                           ohg[:, :, :].unsqueeze(3).broadcast_to([P, TT, MOE_G, MOE_E]),
                                           oh8[:, :, a, :].unsqueeze(2).broadcast_to([P, TT, MOE_G, MOE_E]), ALU.mult)

    @c.block.scalar
    def _(act):
        act.wait_ge(*centred.at(1))
        nc.scalar.activation(eg[:, :, :], eg[:, :, :], ACT.Exp)
        nc.scalar.activation(es[:, :, :], es[:, :, :], ACT.Exp)
        act.drain().then_inc(*exped.up())
    c.join()
    return oh, pw


def hier_moe(c, layer):
    nc, arg = c.nc, c.arg
    with ExitStack() as ctx:
        oh, pw = route_hier(c, layer, ctx)
        one = lambda v: (lambda e, j: v[bass.ds(e, 1)].rearrange("a p k f -> (a p) k f"))
        sparse_experts(c, MOE_G * MOE_E, 1, 4, 128, c.x, oh, pw,
                       one(arg["moe_w_gate"][layer].rearrange("e (k p) f -> e p k f", p=P)),
                       one(arg["moe_w_up"][layer].rearrange("e (k p) f -> e p k f", p=P)),
                       one(arg["moe_w_down"][layer].rearrange("e (k p) f -> e p k f", p=P)),
                       None, DN_ALPHA, ctx,
                       [(c.gain[:, :], bcast(arg["ln2_g"][layer])), (c.bias[:, :], bcast(arg["ln2_b"][layer]))])



ML_H, ML_D, FX_H, FX_D = 4, 64, 8, 64
ML_W, CF_W, FX_W = ML_H * ML_D, D // 4, FX_H * FX_D
ML_K, CF_K = 4, 31
Z_V, Z_O, Z_IF, Z_GLU = 2 * ML_W, 3 * ML_W, 4 * ML_W, 4 * ML_W + 2 * ML_H
Z_FQ = Z_GLU + 2 * CF_W
Z_FF = Z_FQ + 3 * FX_W


def pre_norm(c, gain):
    rms_scales(c, 0, c.x, gain, c.scaled, c.sig("gain_landed").now())
    rms_columns(c, [(0, c.scaled, c.xT)])


def hybrid_buffers(c, layer, ctx):
    arg = c.arg
    sb = lambda name, shape, dt=F32: c.sb(f"h{layer}_" + name, shape, dt, ctx)
    NT = 2 * ML_W // P
    qk_in, qk = sb("qk_in", [P, NT, ML_K - 1 + TOK]), sb("qk", [P, NT, TOK])
    cf_in, cf = sb("cf_in", [P, 2, CF_K - 1 + TOK]), sb("cf", [P, 2, TOK])
    sg = sb("sg", [P, 2, TOK])
    mw, mb = sb("mw", [P, NT, ML_K]), sb("mb", [P, NT])
    cw, cb = sb("cw", [P, 2, CF_K]), sb("cb", [P, 2])
    vo = sb("vo", [P, TT, 2 * ML_W])
    fq, fk, fv = sb("fq", [P, FX_H // 2, TOK]), sb("fk", [P, FX_H // 2, TOK]), sb("fv", [P, TT, FX_W])
    gates, gb = sb("gates", [P, TT, 2 * ML_H + FX_H]), sb("gb", [P, 2 * ML_H + FX_H])
    norm_w, ln_w, ln_b = sb("norm_w", [P, ML_W]), sb("ln_w", [P, CF_W]), sb("ln_b", [P, CF_W])
    NH = ML_H + FX_H
    lf, ab, F, A = (sb(x, [P, TT, NH]) for x in ("lf", "ab", "F", "A"))
    dm = sb("dm", [P, ML_H * 3 * P])
    df = sb("df", [P, FX_H * 3 * P])
    mneg, floor = sb("mneg", [P, TT, ML_H]), sb("floor", [P, TT, ML_H])

    load_ahead(c, "mixer_params_landed", [
        (mw[:, i, :], arg["mlstm_conv_w_2"][layer][:, i * P:(i + 1) * P].rearrange("k p -> p k")) for i in range(NT)] + [
        (mb[:, :], arg["mlstm_conv_b_2"][layer].rearrange("(c p) -> p c", p=P))] + [
        (cw[:, i, :], arg["conf_conv_w_2"][layer][:, i * P:(i + 1) * P].rearrange("k p -> p k")) for i in range(2)] + [
        (cb[:, :], arg["conf_conv_b_2"][layer].rearrange("(c p) -> p c", p=P)),
        (gb[:, 0:ML_H], bcast(arg["mlstm_b_i_2"][layer])), (gb[:, ML_H:2 * ML_H], bcast(arg["mlstm_b_f_2"][layer])),
        (gb[:, 2 * ML_H:], bcast(arg["fox_b_f_2"][layer])),
        (norm_w[:, :], bcast(arg["mlstm_norm_w_2"][layer])), (ln_w[:, :], bcast(arg["conf_ln_w_2"][layer])),
        (ln_b[:, :], bcast(arg["conf_ln_b_2"][layer]))])
    return qk_in, qk, cf_in, cf, sg, mw, mb, cw, cb, vo, fq, fk, fv, \
        gates, gb, norm_w, ln_w, ln_b, lf, ab, F, A, dm, df, mneg, floor


def hybrid_mixer(c, layer, cat, buffers):
    nc, arg = c.nc, c.arg
    NT, NH = 2 * ML_W // P, ML_H + FX_H
    qk_in, qk, cf_in, cf, sg, mw, mb, cw, cb, vo, fq, fk, fv, \
        gates, gb, norm_w, ln_w, ln_b, lf, ab, F, A, dm, df, mneg, floor = buffers

    def decay(buf, n, t):
        return buf[:, 0:n * P].rearrange("p (h k) -> p h k", h=n) if t == 0 else \
            buf[:, n * P:].rearrange("p (h k) -> p h k", h=n)
    w = arg["w_in_2"][layer]
    cp = lambda dst: (lambda r: nc.scalar.activation(dst, r, ACT.Copy))
    pad, cpad = ML_K - 1, CF_K - 1

    padded = c.sig("conv_padded")

    @c.block.gpsimd
    def _(pool):
        nc.gpsimd.memset(qk_in[:, :, 0:pad], 0.0)
        nc.gpsimd.memset(cf_in[:, :, 0:cpad], 0.0)
        pool.drain().then_inc(*padded.up())

    abs_ready, log_ready, lf_ready = c.sig("gate_abs"), c.sig("gate_log"), c.sig("log_forget_ready")
    sums_taken, max_ready = c.sig("forget_sums_taken"), c.sig("decay_max")
    step, convolved = c.sig("conv_step"), c.sig("convolved")
    taken_act = c.sig("results_taken_act")
    zf = gates[:, :, ML_H:]
    HV = 2 * ML_W - P
    HF = FX_W - P

    def take_edge(dst, g0, g1):
        def take(r):
            c.dve(nc.vector.tensor_copy(dst, r[:, :, 0:P]))
            return nc.vector.tensor_copy(gates[:, :, g0:g1], r[:, :, P:P + g1 - g0])
        return take

    def gate_bias(dve):
        dve.wait_ge(*c.sig("mixer_params_landed").now())
        dve.drain()
        c.dve(nc.vector.tensor_tensor(gates[:, :, :], gates[:, :, :], gb[:, :].unsqueeze(1).broadcast_to([P, TT, 2 * ML_H + FX_H]), ALU.add))
        nc.vector.scalar_tensor_tensor(ab[:, :, :], zf, -1.0, zf, ALU.mult, ALU.max).then_inc(*abs_ready.up())

    def gate_logs(act):
        act.wait_ge(*abs_ready.at(1))
        c.act(nc.scalar.activation(ab[:, :, :], ab[:, :, :], ACT.Exp, scale=-1.0))
        nc.scalar.activation(ab[:, :, :], ab[:, :, :], ACT.Ln, bias=c.ones[:, 0:1]).then_inc(*log_ready.up())

    def log_forget(dve):
        dve.wait_ge(*log_ready.at(1))
        nc.vector.scalar_tensor_tensor(lf[:, :, :], zf, 0.0, ab[:, :, :], ALU.min, ALU.subtract).then_inc(*lf_ready.up())

    def sum_products(pe, banks):
        pe.wait_ge(*lf_ready.at(1))
        nc.tensor.matmul(banks[:, 0, 0:NH], c.tri01[:, :], lf[:, 0, :], start=True, stop=True)
        nc.tensor.matmul(banks[:, 1, 0:NH], c.ones[:, :], lf[:, 0, :], start=True, stop=False)
        return nc.tensor.matmul(banks[:, 1, 0:NH], c.tri01[:, :], lf[:, 1, :], start=False, stop=True)

    def take_sums(r):
        c.dve(nc.vector.tensor_copy(F[:, :, :], r[:, :, 0:NH]))
        c.dve(nc.vector.tensor_scalar(A[:, :, :], F[:, :, :], -1.0, None, ALU.mult))
        return nc.vector.tensor_tensor(A[:, :, 0:ML_H], A[:, :, 0:ML_H], gates[:, :, 0:ML_H], ALU.add)

    def decay_rows(h0):
        def fill(pe, banks):
            if h0 == 0:
                pe.wait_ge(*c.sig("results_taken_dve").at(3))
            for a in range(4):
                for s in range(TT):
                    at = (a % 2) * TOK + s * P
                    last = nc.tensor.matmul(banks[:, a // 2, at:at + P], A[:, s, h0 + a:h0 + a + 1].broadcast_to([P, P]),
                                            c.ident[:, :], start=True, stop=True)
            return last

        def take(r):
            for h in range(h0, h0 + 4):
                n, i, buf = (ML_H, h, dm) if h < ML_H else (FX_H, h - ML_H, df)
                pos = heads_position(i, n, True)
                for t in range(TT):
                    nk = (t + 1) * P
                    src = r[:, (h - h0) // 2, (h % 2) * TOK:(h % 2) * TOK + nk]
                    last = nc.vector.scalar_tensor_tensor(decay(buf, n, t)[:, pos, :], src, F[:, t, h:h + 1],
                                                          c.mask[:, TOK - nk:], ALU.add, ALU.add)
                    if (h, t) != (h0 + 3, TT - 1):
                        c.dve(last)
            return last
        return Own(fill, "dve", take)

    def decay_maxima(dve):
        dve.drain()
        for t in range(TT):
            c.dve(nc.vector.tensor_reduce(mneg[:, t, :], decay(dm, ML_H, t), AX_X, ALU.max))
            for a in range(2):
                c.dve(nc.vector.tensor_tensor(mneg[:, t, 2 * a:2 * a + 2], mneg[:, t, 2 * a:2 * a + 2], F[:, t, a:ML_H:2], ALU.max))
        nc.vector.tensor_scalar(mneg[:, :, :], mneg[:, :, :], -1.0, None, ALU.mult).then_inc(*max_ready.up())

    def convolve(dve, taps, n, x, acc, wt, b):
        for k in range(taps):
            for i in range(n):
                if k:
                    dve.wait_ge(step.sem, step.count - n + 1)
                src = x[:, i, k:k + TOK]
                last = nc.vector.tensor_scalar(acc[:, i, :], src, wt[:, i, 0:1], b[:, i:i + 1], ALU.mult, ALU.add) if k == 0 else \
                    nc.vector.scalar_tensor_tensor(acc[:, i, :], src, wt[:, i, k:k + 1], acc[:, i, :], ALU.mult, ALU.add)
                last.then_inc(*step.up())

    def convolve_qk(dve):
        dve.wait_ge(*padded.at(1))
        dve.wait_ge(*taken_act.at(2))
        convolve(dve, ML_K, NT, qk_in, qk, mw, mb)
        dve.drain().then_inc(*convolved.up())

    def convolve_glu(dve):
        dve.wait_ge(*taken_act.at(4))
        c.dve(nc.vector.tensor_tensor(cf_in[:, :, cpad:], cf_in[:, :, cpad:], sg[:, :, :], ALU.mult))
        convolve(dve, CF_K, 2, cf_in, cf, cw, cb)

    def decay_exps(act):
        act.wait_ge(*max_ready.at(1))
        for t in range(TT):
            for pos in range(ML_H):
                d = decay(dm, ML_H, t)[:, pos, :]
                nc.scalar.activation(d, d, ACT.Exp, bias=mneg[:, t, pos:pos + 1])
        nc.scalar.activation(floor[:, :, :], mneg[:, :, :], ACT.Exp)
        act.wait_ge(*convolved.at(1))
        nc.scalar.activation(qk[:, :, :], qk[:, :, :], ACT.Silu)

    projection(c, [
        Rows(c.xT, w, Z_V + HV, P + 2 * ML_H, "dve", take_edge(vo[:, :, HV:], 0, 2 * ML_H)),
        Rows(c.xT, w, Z_FF - P, P + FX_H, "dve", take_edge(fv[:, :, HF:], 2 * ML_H, 2 * ML_H + FX_H)),
        Step("dve", gate_bias),
        Cols(c.xT, w, 0, 256, "act", cp(qk_in[:, 0:2, pad:])),
        Step("act", gate_logs),
        Step("dve", log_forget),
        Cols(c.xT, w, 256, 256, "act", cp(qk_in[:, 2:4, pad:])),
        Own(sum_products, "dve", take_sums),
        Cols(c.xT, w, Z_GLU, 256, "act", cp(cf_in[:, :, cpad:])),
        decay_rows(0), decay_rows(4),
        Cols(c.xT, w, Z_GLU + 256, 256, "act", lambda r: nc.scalar.activation(sg[:, :, :], r, ACT.Sigmoid)),
        decay_rows(8),
        Step("dve", decay_maxima), Step("dve", convolve_qk), Step("dve", convolve_glu),
        Rows(c.xT, w, Z_V, HV, "act", cp(vo[:, :, 0:HV])),
        Cols(c.xT, w, Z_FQ, 256, "act", cp(fq[:, 0:2, :])),
        Cols(c.xT, w, Z_FQ + 256, 256, "act", cp(fq[:, 2:4, :])),
        Cols(c.xT, w, Z_FQ + FX_W, 256, "act", cp(fk[:, 0:2, :])),
        Cols(c.xT, w, Z_FQ + FX_W + 256, 256, "act", cp(fk[:, 2:4, :])),
        Step("act", decay_exps),
        Rows(c.xT, w, Z_FQ + 2 * FX_W, HF, "act", cp(fv[:, :, 0:HF]))], join=False)
    c.join()
    half = lambda i: slice((i % 2) * 64, (i % 2) * 64 + 64)
    hm = vo[:, :, 0:ML_W]
    attention(c, [(t, 0) for t in range(TT)], ML_H, ML_D,
              q=lambda t, b, i: qk[half(i), i // 2, t * P:(t + 1) * P], k=lambda b, i, nk: qk[half(i), 2 + i // 2, 0:nk],
              v=lambda b, i, s: vo[:, s, i * ML_D:(i + 1) * ML_D],
              out=lambda t, b: cat[:, t, 0:ML_W].rearrange("p (h d) -> p h d", h=ML_H),
              scale=ML_D ** -0.5, bias=None,
              gated=(lambda t, nk: decay(dm, ML_H, t), lambda t: floor[:, t, :]))
    attention(c, [(t, 0) for t in range(TT)], FX_H, FX_D,
              q=lambda t, b, i: fq[half(i), i // 2, t * P:(t + 1) * P], k=lambda b, i, nk: fk[half(i), i // 2, 0:nk],
              v=lambda b, i, s: fv[:, s, i * FX_D:(i + 1) * FX_D],
              out=lambda t, b: cat[:, t, ML_W + CF_W:].rearrange("p (h d) -> p h d", h=FX_H),
              scale=FX_D ** -0.5, bias=lambda t, b, nk: decay(df, FX_H, t))

    transpose_stage(c, [([cf[:, i, t * P:(t + 1) * P] for i in range(2)], cat[:, t, ML_W:ML_W + CF_W], "dve") for t in range(TT)])
    og = vo[:, :, ML_W:]
    norm_stage(c, [dict(src=cat[:, t, 0:ML_W].rearrange("p (h d) -> p h d", h=ML_H),
                        dst=hm[:, t, :].rearrange("p (h d) -> p h d", h=ML_H), kind="rms", eps=RMS_EPS, gain=None, bias=None)
                   for t in range(TT)] +
               [dict(src=cat[:, :, ML_W:ML_W + CF_W], dst=cat[:, :, ML_W:ML_W + CF_W], kind="ln", eps=RMS_EPS,
                     gain=ln_w[:, :], bias=ln_b[:, :])])

    @c.block.scalar
    def _(act):
        nc.scalar.activation(cat[:, :, ML_W:ML_W + CF_W], cat[:, :, ML_W:ML_W + CF_W], ACT.Silu)
        nc.scalar.activation(og, og, ACT.Sigmoid).then_inc(*c.sig("output_gate").up())

    @c.block.vector
    def _(dve):
        c.dve(nc.vector.tensor_tensor(hm, hm, norm_w[:, :].unsqueeze(1).broadcast_to([P, TT, ML_W]), ALU.mult))
        dve.wait_ge(*c.sig("output_gate").at(1))
        nc.vector.tensor_tensor(cat[:, :, 0:ML_W], hm, og, ALU.mult)
    c.join()


XA_H, XA_D = 4, 128
XA_W = XA_H * XA_D


def cross_attention(c, layer, before):
    nc, arg = c.nc, c.arg
    with ExitStack() as ctx:
        sb = lambda name, shape, dt=F32: c.sb(f"x{layer}_" + name, shape, dt, ctx)
        rows, mem, memT = sb("rows", [P, TT, D]), sb("mem", [P, TT, D]), sb("memT", [P, KD, TOK])
        qT, kT, v = sb("qT", [P, XA_H, TOK]), sb("kT", [P, XA_H, TOK]), sb("v", [P, TT, XA_W])
        o, oT = sb("o", [P, TT, XA_W]), sb("oT", [P, XA_H, TOK])
        load_ahead(c, "mem_landed", [(mem[:, :, :], arg["mem_2"][0].rearrange("(t p) d -> p t d", p=P))])
        rms_scales(c, 1, mem, c.gain[:, :], rows, c.sig("mem_landed").now())
        before()
        rms_scales(c, 0, c.x, c.bias[:, :], c.scaled, c.sig("gain_landed").now())
        rms_columns(c, [(1, rows, memT), (0, c.scaled, c.xT)])
        load_ahead(c, "gain_landed", [
            (c.bias[:, :], bcast(arg["norm_ffn_w_2"][layer])),
            (c.gain[:, :], bcast(arg["norm_mix_w_2"][layer + 1] if layer < DEPTH - 1 else arg["norm_final_w_2"]))])
        cp = lambda dst: (lambda r: nc.scalar.activation(dst, r, ACT.Copy))
        dcp = lambda dst: (lambda r: nc.vector.tensor_copy(dst, r))
        wq, wkv = arg["xattn_w_q_2"][layer], arg["xattn_w_kv_2"][layer]
        projection(c, [Cols(c.xT, wq, 0, 256, "act", cp(qT[:, 0:2, :])), Cols(c.xT, wq, 256, 256, "dve", dcp(qT[:, 2:4, :])),
                       Cols(memT, wkv, 0, 256, "act", cp(kT[:, 0:2, :])), Cols(memT, wkv, 256, 256, "dve", dcp(kT[:, 2:4, :])),
                       Rows(memT, wkv, 512, 512, "act", cp(v[:, :, :]))])
        attention(c, [(t, 0) for t in range(TT)], XA_H, XA_D,
                  q=lambda t, b, i: qT[:, i, t * P:(t + 1) * P], k=lambda b, i, nk: kT[:, i, 0:nk],
                  v=lambda b, i, s: v[:, s, i * XA_D:(i + 1) * XA_D],
                  out=lambda t, b: o[:, t, :].rearrange("p (h d) -> p h d", h=XA_H),
                  scale=XA_D ** -0.5, bias=None, paired=False, causal=False)
        rows_to_columns(c, o, oT, XA_H)
        residual(c, oT, arg["xattn_w_o_2"][layer], 1.0)


F2 = 2816
FFC = F2 // CH
EXP2 = 8


def dense_ffn(c, layer):
    arg = c.arg
    with ExitStack() as ctx:
        pre_norm(c, c.bias[:, :])
        cols = lambda v: (lambda j: v.rearrange("(k p) (c f) -> c p k f", p=P, f=CH)[bass.ds(j, 1)].rearrange("a p k f -> (a p) k f"))
        rows = lambda v: (lambda j: v.rearrange("(c k p) n -> c p k n", p=P, k=2)[bass.ds(j, 1)].rearrange("a p k f -> (a p) k f"))
        stream_ffn(c, FFC, cols(arg["ffn_w_gate_2"][0]), cols(arg["ffn_w_up_2"][0]), rows(arg["ffn_w_down_2"][0]), ctx)


def flat_moe(c, layer):
    nc, arg = c.nc, c.arg
    with ExitStack() as ctx:
        sb = lambda name, shape, dt=F32: c.sb("f_" + name, shape, dt, ctx)
        wr, lg = sb("wr", [P, KD, EXP2]), sb("lg", [P, TT, EXP2])
        top, topi, idx = sb("top", [P, TT, 8]), sb("topi", [P, TT, 8], U32), sb("idx", [P, TT, 2])
        iota, iota_i = sb("iota", [P, 8]), sb("iota_i", [P, 8], I32)
        zero = sb("zero", [P, EXP2])
        e1, w = sb("e1", [P, TT, 1]), sb("w", [P, TT, 2])
        oh = sb("oh", [P, TT, 2, EXP2])
        outT = sb("outT", [P, KD, SLOTS + TOK])
        rows = outT[:, :, :].rearrange("p k s -> p (k s)")[:, 0:TT * D].rearrange("p (t d) -> p t d", t=TT)
        load_params(c, [(wr[:, :, :], k_tiles(arg["router_w_2"][0]))])
        rms_scales(c, 0, c.x, c.bias[:, :], c.scaled, c.sig("gain_landed").now())
        rms_columns(c, [(0, c.scaled, c.xT)], join=False)

        @c.block.vector
        def _(dve):
            for t in range(TT):
                nc.vector.tensor_scalar(rows[:, t, :], c.scaled[:, t, :], c.rstd[:, 0, t, :], None, ALU.mult)

        @c.block.gpsimd
        def _(pool):
            nc.gpsimd.memset(zero[:, :], 0.0)
            nc.gpsimd.iota(iota_i[:, :], pattern=[[1, 8]], base=0, channel_multiplier=0)
        c.join()
        logits_stage(c, wr, zero[:, :], EXP2, lg[:, :, :])
        centred, exped = c.sig("router_centred"), c.sig("router_exp")

        @c.block.vector
        def _(dve):
            c.dve(nc.vector.tensor_copy(iota[:, :], iota_i[:, :]))
            for t in range(TT):
                c.dve(nc.vector.max(top[:, t, :], lg[:, t, :]))
                c.dve(nc.vector.max_index(topi[:, t, :], top[:, t, :], lg[:, t, :]))
            c.dve(nc.vector.tensor_copy(idx[:, :, :], topi[:, :, 0:2]))
            nc.vector.tensor_tensor(e1[:, :, :], top[:, :, 1:2], top[:, :, 0:1], ALU.subtract).then_inc(*centred.up())
            dve.wait_ge(*exped.at(1))
            c.dve(nc.vector.tensor_scalar(w[:, :, 0:1], e1[:, :, :], 1.0, None, ALU.add))
            c.dve(nc.vector.reciprocal(w[:, :, 0:1], w[:, :, 0:1]))
            c.dve(nc.vector.tensor_tensor(w[:, :, 1:2], w[:, :, 0:1], e1[:, :, :], ALU.mult))
            for t in range(TT):
                for a in range(2):
                    last = nc.vector.tensor_scalar(oh[:, t, a, :], iota[:, :], idx[:, t, a:a + 1], None, ALU.is_equal)

        @c.block.scalar
        def _(act):
            act.wait_ge(*centred.at(1))
            nc.scalar.activation(e1[:, :, :], e1[:, :, :], ACT.Exp).then_inc(*exped.up())
        c.join()

        def cols(v):
            vv = v.rearrange("e (k p) (c f) -> e c p k f", p=P, f=CH)
            return lambda e, j: vv[bass.ds(e, 1), j:j + 1].rearrange("a b p k f -> (a b p) k f")
        down = arg["moe_w_down_2"][0].rearrange("e (c k p) n -> e c p k n", p=P, k=2)
        sparse_experts(c, EXP2, FFC, 1, 128, rows, oh, w, cols(arg["moe_w_gate_2"][0]), cols(arg["moe_w_up_2"][0]),
                       lambda e, j: down[bass.ds(e, 1), j:j + 1].rearrange("a b p k n -> (a b p) k n"), outT, 1.0, ctx)


def load_weights(c):
    ring = c.ring

    @c.block.sync
    def _(sp):
        def load(n, i, dst_n, src):
            if dst_n >= RING:
                sp.wait_ge(ring.used, n - RING + 1)
            kt, cols = src.shape[1:]
            sp.dma_start(ring.view(dst_n, kt, cols), src).then_inc(ring.full[dst_n % RING], 16)

        for entry in ring.plan:
            if entry[0] == "tile":
                _, n, dst, src = entry
                load(n, 0, n, src)
                continue
            if entry[0] == "experts":
                _, p0, n, chunks, unroll, turns, per, gate, up, down = entry

                def expert(x, i):
                    e, far = x + unroll * i, (per * unroll) * i
                    tile = lambda at, src: load(far + at, i, at, src)
                    if chunks == 1:
                        if x + 1 < n:
                            tile(p0 + 2 + 3 * x, gate(e + 1, 0))
                            tile(p0 + 3 + 3 * x, up(e + 1, 0))
                        tile(p0 + 2 + 3 * x + (2 if x + 1 < n else 0), down(e, 0))
                        return
                    at = p0 + per * x
                    tile(at, gate(e, 0))
                    tile(at + 1, up(e, 0))
                    for j in range(chunks - 1):
                        tile(at + 2 + 3 * j, gate(e, j + 1))
                        tile(at + 3 + 3 * j, up(e, j + 1))
                        tile(at + 4 + 3 * j, down(e, j))
                    tile(at + 3 * chunks - 1, down(e, chunks - 1))
                if chunks == 1:
                    load(p0, 0, p0, gate(0, 0))
                    load(p0 + 1, 0, p0 + 1, up(0, 0))
                with sp.Fori(0, turns) as i:
                    for x in range(unroll):
                        expert(x, i)
                for x in range(turns * unroll, n):
                    expert(x, 0)
                continue
            _, p0, n, gate, up, down = entry
            U = 4
            loops = max(0, (n - 2) // U)

            def chunk(j, first, i):
                at = p0 + 2 + 3 * first
                load(at + 12 * i, i, at, gate(j + 1))
                load(at + 1 + 12 * i, i, at + 1, up(j + 1))
                load(at + 2 + 12 * i, i, at + 2, down(j))
            load(p0, 0, p0, gate(0))
            load(p0 + 1, 0, p0 + 1, up(0))
            chunk(0, 0, 0)
            if loops:
                with sp.Fori(0, loops) as i:
                    for r in range(U):
                        chunk(i * U + 1 + r, 1 + r, i)
            for j in range(1 + U * loops, n - 1):
                chunk(j, j, 0)
            load(p0 + 3 * n - 1, 0, p0 + 3 * n - 1, down(n - 1))


def build(nc, arg, out):
    with ExitStack() as ctx:
        c = Core(nc, ctx)
        c.arg = arg
        c.ring = WeightRing(c)
        c.block = ctx.enter_context(nc.Block(no_gpsimd_drain=True))
        constants(c)
        rows_to_columns(c, c.x, c.xT, KD)

        def stages():
            for layer, mixer in enumerate((ab_mixer, nsa_mixer)):
                with ExitStack() as m:
                    cat = c.sb(f"cat{layer}", [P, TT, D], ctx=m)
                    mixer(c, cat, m)
                    rows_to_columns(c, cat, c.xT, KD)
                residual(c, c.xT, arg[("ab_w_o", "c_w_o")[layer]][0], DN_ALPHA,
                         [(c.gain[:, :], bcast(arg["ln1_g"][layer])), (c.bias[:, :], bcast(arg["ln1_b"][layer]))])
                post_norm(c)
                hier_moe(c, layer)
                if layer < DEPTH - 1:
                    post_norm(c)
            for layer in range(DEPTH):
                with ExitStack() as m:
                    cat = c.sb(f"cat{2 + layer}", [P, TT, D], ctx=m)
                    gain = c.gain[:, :]
                    if layer == 0:
                        gain = cat[:, 0, :]
                        load_ahead(c, "gain_landed", [(gain, bcast(arg["norm_mix_w_2"][0]))])
                        post_norm(c, columns=False)
                    hybrid_params = hybrid_buffers(c, layer, m)
                    pre_norm(c, gain)
                    load_ahead(c, "gain_landed", [(c.bias[:, :], bcast(arg["norm_xattn_w_2"][layer])),
                                                  (c.gain[:, :], bcast(arg["norm_mem_w_2"][layer]))])
                    hybrid_mixer(c, layer, cat, hybrid_params)
                    rows_to_columns(c, cat, c.xT, KD)
                cross_attention(c, layer, lambda: residual(c, c.xT, arg["w_out_2"][layer], 1.0))
                (dense_ffn, flat_moe)[layer % 2](c, layer)
        stages()
        res = c.sb("result", [P, TT, D])
        rms_scales(c, 0, c.x, c.gain[:, :], res, c.sig("gain_landed").now())
        stored, scaled = c.sig("result_stored"), c.sig("result_scaled")
        out_rows = out[0].rearrange("(t p) d -> p t d", p=P)

        @c.block.vector
        def _(dve):
            nc.vector.tensor_scalar(res[:, 0, :], res[:, 0, :], c.rstd[:, 0, 0, :], None, ALU.mult).then_inc(*scaled.up())

        @c.block.scalar
        def _(act):
            act.wait_ge(*c.sig("rms_diagonal_0").now())
            c.act(nc.scalar.activation(res[:, 1, :], res[:, 1, :], ACT.Copy, scale=c.rstd[:, 0, 1, :]))
            act.dma_start(out_rows[:, 1, :], res[:, 1, :]).then_inc(*stored.up(16))
            act.wait_ge(*scaled.at(1))
            act.dma_start(out_rows[:, 0, :], res[:, 0, :]).then_inc(*stored.up(16))
            act.wait_ge(*stored.now())

        load_weights(c)


_OUTS = [((1, TOK, D), "float32")]


def kernel(**inputs):
    import numpy as _np
    import concourse.bacc as _bacc
    from concourse import mybir as _mybir
    from concourse.bass_utils import run_bass_kernel_spmd as _run

    nc = _bacc.Bacc("TRN2", target_bir_lowering=False, num_devices=1)
    arrays, arg = {}, {}
    for name, a in inputs.items():
        a = _np.ascontiguousarray(a)
        arrays[f"in_{name}_dram"] = a
        arg[name] = nc.dram_tensor(f"in_{name}_dram", a.shape, _mybir.dt.from_np(a.dtype), kind="ExternalInput").ap()
    shape, dtype = _OUTS[0]
    out = nc.dram_tensor("out_0_dram", shape, _mybir.dt.from_np(_np.dtype(dtype)), kind="ExternalOutput").ap()
    build(nc, arg, out)
    r = _run(nc, [arrays], core_ids=[0])
    return r.results[0]["out_0_dram"]
```

```python
import math
from contextlib import ExitStack

import numpy as np

import concourse.bass as bass
from concourse import mybir

F32 = mybir.dt.float32
F32R = mybir.dt.float32r
I32 = mybir.dt.int32
U32 = mybir.dt.uint32
ALU = mybir.AluOpType
ACT = mybir.ActivationFunctionType
AX_X = mybir.AxisListType.X

P = 128
TOK = 256
TT = TOK // P
D = 1024
KD = D // P
SLOT = 2048
RING = 9
HIGHS = 3
NEG = -1e30
DEPTH = 2
DN_ALPHA = (2.0 * DEPTH) ** 0.25
LN_EPS = 1e-5
RMS_EPS = 1e-6


class Signal:

    def __init__(self, sem):
        self.sem, self.count, self.base = sem, 0, 0

    def up(self, n=1):
        self.count += n
        return self.sem, n

    def at(self, n):
        assert n > 0
        return self.sem, self.base + n

    def now(self):
        return self.sem, self.count


class WeightRing:

    def __init__(self, core):
        self.nc = core.nc
        self.buf, self.lows = core.sb_twice("weight_ring", [P, RING, SLOT])
        self.spare, self.highs = core.sb_twice("weights_high", [P, HIGHS, SLOT])
        self.full = [core.new_sem(f"weights_full_{i}") for i in range(RING)]
        self.used = core.new_sem("weights_used")
        self.high_ready, self.split_ready = core.new_sem("high_parts_ready"), core.new_sem("weights_split")
        self.loaded = [0] * RING
        self.tiles = 0
        self.split_tiles = []
        self.plan = []

    def view(self, n, kt, cols):
        return self.buf[:, n % RING, 0:kt * cols].rearrange("p (k n) -> p k n", k=kt)

    def low(self, n, kt, cols):
        return self.lows[:, n % RING, 0:kt * cols].rearrange("p (k n) -> p k n", k=kt)

    def high(self, s, kt, cols):
        return self.highs[:, s % HIGHS, 0:kt * cols].rearrange("p (k n) -> p k n", k=kt)

    def next(self, src, split=False):
        kt, cols = src.shape[1], src.shape[2]
        n = self.tiles
        self.plan.append(("tile", n, self.view(n, kt, cols)[0:src.shape[0]], src))
        self.tiles += 1
        self.loaded[n % RING] += 16
        if split:
            self.split_tiles.append(n)
        return Tile(self, n, kt, cols, (self.full[n % RING], self.loaded[n % RING]), len(self.split_tiles) - 1 if split else None)

    def take(self, pe, src):
        tile = self.next(src)
        pe.wait_ge(*tile.landed)
        return tile.whole


class Tile:

    def __init__(self, ring, n, kt, cols, landed, s):
        self.ring, self.n, self.landed, self.s = ring, n, landed, s
        self.split_by = set()
        self.whole = ring.view(n, kt, cols)
        if s is not None:
            self.high, self.low = ring.high(s, kt, cols), ring.low(n, kt, cols)

    def round_high(self, act):
        act.wait_ge(*self.landed)
        if self.s >= HIGHS:
            act.wait_ge(self.ring.used, self.ring.split_tiles[self.s - HIGHS] + 1)
        self.ring.nc.scalar.activation(self.high, self.whole, ACT.Copy).then_inc(self.ring.high_ready, 1)

    def leave_low(self, dve):
        dve.wait_ge(self.ring.high_ready, self.s + 1)
        self.ring.nc.vector.tensor_tensor(self.low, self.whole, self.high.bitcast(F32), ALU.subtract).then_inc(self.ring.split_ready, 1)

    def wait(self, pe):
        if self.s is None:
            pe.wait_ge(*self.landed)
        else:
            pe.wait_ge(self.ring.split_ready, self.s + 1)


def three_products(nc, out, left, right, start, stop):
    (lh, ll), (rh, rl) = left, right
    nc.tensor.matmul(out, lh, rh, start=start, stop=False)
    nc.tensor.matmul(out, lh, rl, start=False, stop=False)
    return nc.tensor.matmul(out, ll, rh, start=False, stop=stop)


def k_tiles(w):
    return w.rearrange("(k p) n -> p k n", p=P)


class Core:

    def __init__(self, nc, ctx):
        self.nc, self.ctx = nc, ctx
        self.signals = {}
        self.order = []
        self.ended = 0
        self.own_products = 0
        self.names = {}

    def sb(self, name, shape, dt=F32, ctx=None):
        times = self.names[name] = self.names.get(name, 0) + 1
        return (ctx or self.ctx).enter_context(
            self.nc.sbuf_tensor(name if times == 1 else f"{name}_{times}", shape, dt))

    def sb_twice(self, name, shape, ctx=None):
        with self.nc.sbuf_tensor(name + "_rounded", shape, F32R) as rounded:
            pass
        whole = self.sb(name, shape, F32, ctx)
        return whole, rounded

    def new_sem(self, name):
        return self.ctx.enter_context(self.nc.semaphore(name))

    def sig(self, name):
        if name not in self.signals:
            self.signals[name] = Signal(self.new_sem(name))
        return self.signals[name]

    def link(self, eng, ins):
        name = {self.nc.vector: "dve", self.nc.scalar: "act", self.nc.gpsimd: "pool"}[eng]
        s = self.sig(f"{name}_step")
        ins.then_inc(*s.up())
        eng.wait_ge(*s.now())

    def dve(self, ins):
        self.link(self.nc.vector, ins)

    def act(self, ins):
        self.link(self.nc.scalar, ins)

    def pool(self, ins):
        self.link(self.nc.gpsimd, ins)

    def join(self):
        s = self.sig("stage_ended")
        self.ended += 1
        total = 4 * self.ended

        @self.block.tensor
        def _(pe):
            pe.drain().then_inc(*s.up())
            pe.wait_ge(s.sem, total)

        @self.block.scalar
        def _(act):
            act.drain().then_inc(*s.up())
            act.wait_ge(s.sem, total)

        @self.block.vector
        def _(dve):
            dve.drain().then_inc(*s.up())
            dve.wait_ge(s.sem, total)

        @self.block.gpsimd
        def _(pool):
            pool.drain().then_inc(*s.up())
            pool.wait_ge(s.sem, total)

        for x in self.signals.values():
            x.base = x.count


def constants(c):
    nc = c.nc
    c.ident = c.sb("ident", [P, P])
    c.tri01 = c.sb("tri01", [P, P])
    c.ones = c.sb("ones", [P, P])
    c.S, c.S_rounded = c.sb_twice("scores", [P, 2, 8, TOK])
    c.PT = c.sb("probs_turned", [P, 2, 512])
    c.diag = c.PT[:, :, :].rearrange("p j (t n) -> p j t n", n=P)[:, :, 0:TT]
    c.scaled = c.S[:, :, :, :].rearrange("p a b t -> p (a b t)")[:, 0:TT * D].rearrange("p (t d) -> p t d", d=D)
    c.neg_max, c.row_sum = c.sb("neg_max", [P, 2, 8]), c.sb("row_sum", [P, 2, 8])
    c.recip = c.sb("recip", [P, 8])
    c.stats, c.rstd = c.sb("norm_stats", [P, 4, 8, 2]), c.sb("norm_rstd", [P, 4, 8, 1])
    c.var, c.newton = c.sb("norm_var", [P, 4, 8, 1]), c.sb("norm_newton", [P, 8, 1])
    c.bn = c.sb("norm_parts", [P, 8, 2, 6])
    c.gain, c.bias = c.sb("gain", [P, D]), c.sb("bias", [P, D])
    c.mask = c.sb("mask", [P, TOK])
    c.x = c.sb("x", [P, TT, D])
    c.xT, xl = c.sb_twice("xT", [P, KD, TOK])
    c.spare_x, c.xh = c.sb_twice("xT_high", [P, KD, TOK])
    c.xl = xl
    c.xs = (c.xh[:, :, :], xl[:, :, :])
    c.psum = c.ctx.enter_context(nc.psum_tensor("psum", [P, 8, 512], F32))
    x_landed = c.sig("params_landed")

    @c.block.gpsimd
    def _(pool):
        nc.gpsimd.memset(c.ident[:, :], 0.0)
        nc.gpsimd.memset(c.tri01[:, :], 1.0)
        nc.gpsimd.memset(c.ones[:, :], 1.0)
        c.pool(nc.gpsimd.memset(c.mask[:, :], 0.0))
        pool.drain()
        nc.gpsimd.affine_select(out=c.ident[:, :], in_=c.ident[:, :], compare_op=ALU.not_equal, fill=1.0,
                                base=0, pattern=[[-1, P]], channel_multiplier=1)
        nc.gpsimd.affine_select(out=c.tri01[:, :], in_=c.tri01[:, :], compare_op=ALU.is_ge, fill=0.0,
                                base=0, pattern=[[1, P]], channel_multiplier=-1)
        nc.gpsimd.affine_select(out=c.mask[:, :], in_=c.mask[:, :], compare_op=ALU.is_ge, fill=NEG,
                                base=P, pattern=[[-1, TOK]], channel_multiplier=1)

    @c.block.scalar
    def _(act):
        act.dma_start(c.x[:, :, :], c.arg["x"][0].rearrange("(t p) d -> p t d", p=P)).then_inc(*x_landed.up(16))
        act.wait_ge(*x_landed.now())
    c.join()


def load_ahead(c, name, items):
    landed = c.sig(name)

    @c.block.gpsimd
    def _(pool):
        for dst, src in items:
            pool.dma_start(dst, src, allow_slow_non_contiguous=True).then_inc(*landed.up(16))


def load_params(c, items):
    landed = c.sig("params_landed")

    @c.block.scalar
    def _(act):
        for dst, src in items:
            act.dma_start(dst, src, allow_slow_non_contiguous=True).then_inc(*landed.up(16))
        act.wait_ge(*landed.now())


def bcast(v, n=P):
    return v.partition_broadcast(n)


def transpose_stage(c, groups, join=True, before=None):
    nc = c.nc
    turned, copied = c.sig("blocks_turned"), {"act": c.sig("turned_copied_act"), "dve": c.sig("turned_copied_dve"),
                                              "both": c.sig("turned_split")}
    high = c.sig("turned_high")

    @c.block.tensor
    def _(pe):
        for g, (ins, dst, who) in enumerate(groups):
            if before is not None:
                pe.wait_ge(*before(g))
            if g >= 8:
                w0 = groups[g - 8][2]
                pe.wait_ge(*copied[w0].at(sum(x[2] == w0 for x in groups[:g - 7])))
            for i, a in enumerate(ins):
                last = nc.tensor.transpose(c.psum[0:a.shape[1], g % 8, i * P:(i + 1) * P], a, c.ident[:, :])
            last.then_inc(*turned.up())

    def copies(eng, name, copy):
        for g, (ins, dst, who) in enumerate(groups):
            w = ins[0].shape[1]
            src = c.psum[0:w, g % 8, 0:len(ins) * P]
            if who == "both":
                split_copy(c, name, eng, dst, src.rearrange("p (a b) -> p a b", a=dst[0].shape[1]), turned.at(g + 1), high, copied[who])
            if who != name:
                continue
            if len(dst.shape) == 3:
                src = src.rearrange("p (a b) -> p a b", a=dst.shape[1])
            eng.wait_ge(*turned.at(g + 1))
            copy(dst, src).then_inc(*copied[name].up())

    @c.block.scalar
    def _(act):
        copies(act, "act", lambda d, s: nc.scalar.activation(d, s, ACT.Copy))

    @c.block.vector
    def _(dve):
        copies(dve, "dve", nc.vector.tensor_copy)
    if join:
        c.join()


def split_copy(c, name, eng, dst, src, ready, high, done):
    hi, lo = dst
    if name == "act":
        eng.wait_ge(*ready)
        c.nc.scalar.activation(hi, src, ACT.Copy).then_inc(*high.up())
    else:
        done_now = done.up()
        eng.wait_ge(high.sem, high.base + done.count - done.base)
        c.nc.vector.tensor_tensor(lo, src, hi.bitcast(F32), ALU.subtract).then_inc(*done_now)


def rows_to_columns(c, src, dst, n, join=True):
    if isinstance(dst, tuple):
        transpose_stage(c, [([src[:, t, j * P:(j + 1) * P] for j in (k, k + 1) for t in range(TT)],
                             tuple(d[:, k:k + 2, :] for d in dst), "both") for k in range(0, n, 2)], join)
        return
    groups = []
    for k in range(0, n, 2):
        kk = min(2, n - k)
        ins = [src[:, t, j * P:(j + 1) * P] for j in range(k, k + kk) for t in range(TT)]
        groups.append((ins, dst[:, k:k + kk, :].rearrange("p k t -> p (k t)"), "dve" if k % 4 else "act"))
    transpose_stage(c, groups, join)


def norm_stage(c, items, join=True, done=None):
    nc = c.nc
    stats = c.stats
    have_stats, have_rstd = c.sig("norm_stats"), c.sig("norm_rstd")

    @c.block.vector
    def _(dve):
        for j, it in enumerate(items):
            n, w = it["src"].shape[1:]
            m = stats[:, j]
            for i in range(n):
                s = it["src"][:, i, :]
                if it["kind"] == "ln":
                    parts = max(1, w // 512)
                    for h in range(parts):
                        last = nc.vector.bn_stats(c.bn[:, i, h, :], s[:, h * (w // parts):(h + 1) * (w // parts)])
                    dve.drain()
                    nc.vector.bn_aggr(m[:, i, :], c.bn[:, i, 0:parts, :].rearrange("p a b -> p (a b)"))
                else:
                    nc.vector.tensor_tensor_reduce(it["dst"][:, i, :], s, s, 1.0 / w, 0.0, ALU.mult,
                                                   ALU.add, m[:, i, 1:2])
            dve.drain()
            nc.vector.tensor_scalar(c.var[:, j, 0:n, :], m[:, 0:n, 1:2], it["eps"], None, ALU.add).then_inc(*have_stats.up())

    @c.block.scalar
    def _(act):
        for j, it in enumerate(items):
            n = it["src"].shape[1]
            act.wait_ge(*have_stats.at(j + 1))
            nc.scalar.activation(c.rstd[:, j, 0:n, :], c.var[:, j, 0:n, :], ACT.Sqrt).then_inc(*have_rstd.up())

    @c.block.vector
    def _(dve):
        for j, it in enumerate(items):
            if it["kind"] == "ln":
                for i in range(it["src"].shape[1]):
                    nc.vector.scalar_tensor_tensor(it["dst"][:, i, :], it["src"][:, i, :], stats[:, j, i, 0:1],
                                                   it["gain"], ALU.subtract, ALU.mult)
        for j, it in enumerate(items):
            n, w = it["src"].shape[1:]
            dve.wait_ge(*have_rstd.at(j + 1))
            inverse_root(c, c.rstd[:, j, 0:n, :], c.var[:, j, 0:n, :], c.newton[:, 0:n, :])
            for i in range(n):
                src, dst, r = it["src"][:, i, :], it["dst"][:, i, :], c.rstd[:, j, i, :]
                if it["kind"] == "ln":
                    last = nc.vector.scalar_tensor_tensor(dst, dst, r, it["bias"], ALU.mult, ALU.add)
                elif it["gain"] is None:
                    last = nc.vector.tensor_scalar(dst, src, r, None, ALU.mult)
                else:
                    last = nc.vector.scalar_tensor_tensor(dst, src, r, it["gain"], ALU.mult, ALU.mult)
                if done is not None:
                    last.then_inc(*done.up())
        dve.drain()
    if join:
        c.join()


def inverse_root(c, r, v, h):
    nc = c.nc
    nc.vector.drain()
    c.dve(nc.vector.reciprocal(r, r))
    c.dve(nc.vector.tensor_tensor(h, r, r, ALU.mult))
    c.dve(nc.vector.tensor_tensor(h, h, v, ALU.mult))
    c.dve(nc.vector.tensor_scalar(h, h, -0.5, 1.5, ALU.mult, ALU.add))
    c.dve(nc.vector.tensor_tensor(r, r, h, ALU.mult))


def rms_scales(c, j, src, gain, y, landed):
    nc = c.nc
    summed, rooted, ready = c.sig(f"squares_summed_{j}"), c.sig(f"rms_root_{j}"), c.sig(f"rms_diagonal_{j}")
    ss, var, r = c.stats[:, j, 0:TT, 0:1], c.var[:, j, 0:TT, :], c.rstd[:, j, 0:TT, :]

    @c.block.scalar
    def _(act):
        if landed is not None:
            act.wait_ge(*landed)
        for t in range(TT):
            junk = c.psum[:, 4 * j + 2 * t:4 * j + 2 * t + 2, :].rearrange("p a b -> p (a b)")
            nc.scalar.activation(junk, src[:, t, :], ACT.Square, accum_out=c.stats[:, j, t, 0:1])
        act.drain().then_inc(*summed.up())

    @c.block.vector
    def _(dve):
        if landed is not None:
            dve.wait_ge(*landed)
        for t in range(TT):
            nc.vector.tensor_tensor(y[:, t, :], src[:, t, :], gain, ALU.mult)
        dve.wait_ge(*summed.now())
        nc.vector.tensor_scalar(var, ss, 1.0 / D, RMS_EPS, ALU.mult, ALU.add).then_inc(*rooted.up())

    @c.block.scalar
    def _(act):
        act.wait_ge(*rooted.now())
        nc.scalar.activation(r, var, ACT.Sqrt).then_inc(*rooted.up())

    @c.block.vector
    def _(dve):
        dve.wait_ge(*rooted.now())
        inverse_root(c, r, var, c.newton[:, 0:TT, :])
        for t in range(TT):
            nc.vector.tensor_scalar(c.diag[:, j, t, :], c.ident[:, :], c.rstd[:, j, t, :], None, ALU.mult)
        dve.drain().then_inc(*ready.up())


def rms_columns(c, parts, join=True):
    nc = c.nc
    turned, high, done = c.sig("rms_turned"), c.sig("rms_high"), c.sig("rms_split")
    groups = [(j, y, dst, k, t) for j, y, dst in parts for k in (0, 4) for t in range(TT)]
    bank = lambda g: 4 * groups[g][0] + g % 4

    @c.block.tensor
    def _(pe):
        for g, (j, y, dst, k0, t) in enumerate(groups):
            pe.wait_ge(*c.sig(f"rms_diagonal_{j}").now())
            for i in range(4):
                last = nc.tensor.matmul(c.psum[:, bank(g), i * P:(i + 1) * P], y[:, t, (k0 + i) * P:(k0 + i + 1) * P],
                                        c.diag[:, j, t, :], start=True, stop=True)
            last.then_inc(*turned.up())

    def copies(eng, which, copy):
        for g, (j, y, dst, k0, t) in enumerate(groups):
            at = lambda d: d[:, k0:k0 + 4, t * P:(t + 1) * P]
            result = c.psum[:, bank(g), :].rearrange("p (k t) -> p k t", k=4)
            if isinstance(dst, tuple):
                split_copy(c, ("act", "dve")[which], eng, tuple(at(d) for d in dst), result, turned.at(g + 1), high, done)
            elif g % 2 == which:
                eng.wait_ge(*turned.at(g + 1))
                copy(at(dst), result)

    @c.block.scalar
    def _(act):
        copies(act, 0, lambda d, s: nc.scalar.activation(d, s, ACT.Copy))

    @c.block.vector
    def _(dve):
        copies(dve, 1, nc.vector.tensor_copy)
    if join:
        c.join()


class Job:

    def __init__(self, xT, w, n0, width, who, take):
        self.xT, self.w, self.n0, self.width, self.who, self.take = xT, w, n0, width, who, take
        self.split = isinstance(xT, tuple)
        self.tiles = None

    def claim(self, c):
        if self.tiles is not None:
            return
        src = k_tiles(self.w)[:, :, self.n0:self.n0 + self.width]
        self.kt = src.shape[1]
        self.per = next(x for x in (8, 4, 2, 1) if x <= self.kt and x * self.width <= SLOT)
        self.tiles = [c.ring.next(src[:, k:k + self.per], self.split) for k in range(0, self.kt, self.per)]
        self.ready = (c.ring.used, self.tiles[-1].n + 1)


class Rows(Job):

    def multiply(self, c, pe, pair):
        for i, tile in enumerate(self.tiles):
            tile.wait(pe)
            for t in range(TT):
                ts = slice(t * P, (t + 1) * P)
                out = c.psum[:, 2 * pair + t, 0:self.width]
                for k in range(self.per):
                    g = i * self.per + k
                    start, stop = g == 0, g == self.kt - 1
                    if self.split:
                        last = three_products(c.nc, out, [x[:, g, ts] for x in self.xT],
                                              (tile.high[:, k, :], tile.low[:, k, :]), start, stop)
                    else:
                        last = c.nc.tensor.matmul(out, self.xT[:, g, ts], tile.whole[:, k, :], start=start, stop=stop)
            last.then_inc(c.ring.used, 1)

    def out(self, c, pair):
        return c.psum[:, 2 * pair:2 * pair + 2, 0:self.width]


class Cols(Job):

    def multiply(self, c, pe, pair):
        tile, = self.tiles
        tile.wait(pe)
        for m in range(self.width // P):
            ms = slice(m * P, (m + 1) * P)
            out = c.psum[:, 2 * pair, m * TOK:(m + 1) * TOK]
            for k in range(self.kt):
                start, stop = k == 0, k == self.kt - 1
                if self.split:
                    last = three_products(c.nc, out, (tile.high[:, k, ms], tile.low[:, k, ms]),
                                          [x[:, k, :] for x in self.xT], start, stop)
                else:
                    last = c.nc.tensor.matmul(out, tile.whole[:, k, ms], self.xT[:, k, :], start=start, stop=stop)
        last.then_inc(c.ring.used, 1)

    def out(self, c, pair):
        return c.psum[:, 2 * pair, 0:self.width // P * TOK].rearrange("p (m t) -> p m t", t=TOK)


class Own:

    def __init__(self, fill, who, take):
        self.fill, self.who, self.take, self.tiles = fill, who, take, []

    def claim(self, c):
        c.own_products += 1
        self.ready = (c.sig("own_products").sem, c.own_products)

    def multiply(self, c, pe, pair):
        self.fill(pe, self.out(c, pair)).then_inc(*c.sig("own_products").up())

    def out(self, c, pair):
        return c.psum[:, 2 * pair:2 * pair + 2, :]


class Step:

    def __init__(self, who, run):
        self.who, self.run = who, run


def split(eng, name, tiles):
    for tile in tiles:
        if tile.s is not None and name not in tile.split_by:
            tile.round_high(eng) if name == "act" else tile.leave_low(eng)
            tile.split_by.add(name)


def claim(c, jobs):
    jobs = [x for x in jobs if not isinstance(x, Step)]
    for job in jobs:
        job.claim(c)
    return [tile for job in jobs for tile in job.tiles][:2]


def split_ahead(c, tiles):
    @c.block.scalar
    def _(act):
        split(act, "act", tiles)

    @c.block.vector
    def _(dve):
        split(dve, "dve", tiles)


def projection(c, jobs, join=True, then=None):
    taken = {"act": c.sig("results_taken_act"), "dve": c.sig("results_taken_dve")}
    order, jobs = jobs, [x for x in jobs if not isinstance(x, Step)]
    claim(c, jobs)
    tiles = [tile for job in jobs for tile in job.tiles] + (then() if then else [])

    @c.block.tensor
    def _(pe):
        for j, job in enumerate(jobs):
            if j >= 4:
                w0 = jobs[j - 4].who
                pe.wait_ge(*taken[w0].at(sum(x.who == w0 for x in jobs[:j - 3])))
            job.multiply(c, pe, j % 4)

    def takes(eng, name):
        for job in order:
            if isinstance(job, Step):
                if job.who == name:
                    job.run(eng)
                continue
            j = jobs.index(job)
            end = min(len(tiles), sum(len(x.tiles) for x in jobs[:j + 1]) + 2)
            split(eng, name, tiles[:end])
            if job.who == name:
                eng.wait_ge(*job.ready)
                job.take(job.out(c, j % 4)).then_inc(*taken[name].up())

    @c.block.scalar
    def _(act):
        takes(act, "act")

    @c.block.vector
    def _(dve):
        takes(dve, "dve")
    if join:
        c.join()


def heads_position(i, n, paired):
    return (n // 2) * (i % 2) + i // 2 if paired else i


def attention(c, batches, n, dv, q, k, v, out, scale, bias, paired=True, causal=True, gated=None, join=True, ahead=()):
    nc = c.nc
    S, PT = c.S, c.PT
    scored, scaled, maxed = c.sig("scores_ready"), c.sig("scores_scaled"), c.sig("maxima_ready")
    probs, turned, copied = c.sig("probs_ready"), c.sig("probs_turned"), c.sig("turned_probs_copied")
    pv_group, written = c.sig("pv_group_done"), c.sig("outputs_written")
    kts = [t + 1 if causal else TT for t, _ in batches]
    groups = []
    last_group = []
    for j, kt in enumerate(kts):
        blocks = [(i, s) for i in range(n) for s in range(kt)]
        groups += [(j, blocks[a:a + 4]) for a in range(0, len(blocks), 4)]
        last_group.append(len(groups))

    @c.block.tensor
    def _(pe):
        def scores(j):
            (t, b), nk = batches[j], kts[j] * P
            if j >= 1:
                pe.wait_ge(*scaled.at(j))
            for i in range(n):
                pos = heads_position(i, n, paired)
                last = nc.tensor.matmul(c.psum[:, pos // 2, (pos % 2) * TOK:(pos % 2) * TOK + nk],
                                        q(t, b, i), k(b, i, nk), start=True, stop=True)
            last.then_inc(*scored.up())

        def turn(g):
            j, blocks = groups[g]
            if g == 0 or groups[g - 1][0] != j:
                pe.wait_ge(*probs.at(j + 1))
            if g >= 2:
                pe.wait_ge(*copied.at(g - 1))
            for a, (i, s) in enumerate(blocks):
                pos = heads_position(i, n, paired)
                last = nc.tensor.transpose(c.psum[:, 4 + g % 2, a * P:(a + 1) * P],
                                           S[:, j % 2, pos, s * P:(s + 1) * P], c.ident[:, :])
            last.then_inc(*turned.up())

        def pv(g):
            j, blocks = groups[g]
            t, b = batches[j]
            pe.wait_ge(*copied.at(g + 1))
            if j >= 2:
                pe.wait_ge(*written.at(j - 1))
            for a, (i, s) in enumerate(blocks):
                last = nc.tensor.matmul(c.psum[:, 6 + j % 2, i * dv:(i + 1) * dv], PT[:, g % 2, a * P:(a + 1) * P],
                                        v(b, i, s), start=(s == 0), stop=(s == kts[j] - 1))
            last.then_inc(*pv_group.up())

        for j in range(len(batches) + 1):
            if j < len(batches):
                scores(j)
            if j >= 1:
                mine = [g for g in range(len(groups)) if groups[g][0] == j - 1]
                for g in mine:
                    turn(g)
                    if g > mine[0]:
                        pv(g - 1)
                pv(mine[-1])

    @c.block.scalar
    def _(act):
        split(act, "act", ahead)
        for j in range(len(batches)):
            nk = kts[j] * P
            if gated is None:
                act.wait_ge(*maxed.at(j + 1))
                for pos in range(n):
                    last = nc.scalar.activation(S[:, j % 2, pos, 0:nk], S[:, j % 2, pos, 0:nk], ACT.Exp,
                                                bias=c.neg_max[:, j % 2, pos:pos + 1],
                                                accum_out=c.row_sum[:, j % 2, pos:pos + 1])
                last.then_inc(*probs.up())
            for g in [g for g in range(len(groups)) if groups[g][0] == j]:
                act.wait_ge(*turned.at(g + 1))
                if g >= 2:
                    act.wait_ge(*pv_group.at(g - 1))
                nc.scalar.activation(PT[:, g % 2, 0:len(groups[g][1]) * P],
                                     c.psum[:, 4 + g % 2, 0:len(groups[g][1]) * P], ACT.Copy).then_inc(*copied.up())

    @c.block.vector
    def _(dve):
        def finish(j):
            t, b = batches[j]
            dve.wait_ge(*pv_group.at(last_group[j]))
            r = c.row_sum[:, j % 2, 0:n]
            if gated is not None:
                c.dve(nc.vector.scalar_tensor_tensor(r, r, -1.0, r, ALU.mult, ALU.max))
                c.dve(nc.vector.tensor_tensor(r, r, gated[1](t), ALU.max))
            if j >= 1:
                dve.wait_ge(*written.at(j))
            c.dve(nc.vector.reciprocal(c.recip[:, 0:n], r))
            rr = c.recip[:, 0:n]
            o = c.psum[:, 6 + j % 2, 0:n * dv]
            if paired:
                rr = rr.rearrange("p (a b) -> p b a", a=2).unsqueeze(3).broadcast_to([P, n // 2, 2, dv])
                o = o.rearrange("p (b a d) -> p b a d", a=2, d=dv)
                dst = out(t, b).rearrange("p (b a) d -> p b a d", a=2)
            else:
                rr = rr.unsqueeze(2).broadcast_to([P, n, dv])
                o = o.rearrange("p (b d) -> p b d", d=dv)
                dst = out(t, b)
            nc.vector.tensor_tensor(dst, o, rr, ALU.mult).then_inc(*written.up())

        for j in range(len(batches)):
            (t, b), nk = batches[j], kts[j] * P
            dve.wait_ge(*scored.at(j + 1))
            if j >= 2:
                dve.wait_ge(*turned.at(last_group[j - 2]))
            sc = c.psum[:, 0:(n + 1) // 2, :].rearrange("p a (b k) -> p (a b) k", b=2)[:, 0:n, 0:nk]
            dst = S[:, j % 2, 0:n, 0:nk]
            if gated is not None:
                nc.vector.scalar_tensor_tensor(dst, sc, scale, gated[0](t, nk), ALU.mult, ALU.mult).then_inc(*scaled.up())
                dve.wait_ge(*scaled.now())
                nc.vector.tensor_reduce(c.row_sum[:, j % 2, 0:n], dst, AX_X, ALU.add).then_inc(*probs.up())
            else:
                if bias is None:
                    nc.vector.tensor_scalar(dst, sc, scale, None, ALU.mult).then_inc(*scaled.up())
                else:
                    nc.vector.scalar_tensor_tensor(dst, sc, scale, bias(t, b, nk), ALU.mult, ALU.add).then_inc(*scaled.up())
                dve.wait_ge(*scaled.now())
                nc.vector.tensor_reduce(c.neg_max[:, j % 2, 0:n], dst, AX_X, ALU.max, negate=True).then_inc(*maxed.up())
            if j == len(batches) - 1:
                split(dve, "dve", ahead)
            if j >= 1:
                finish(j - 1)
        finish(len(batches) - 1)
    if join:
        c.join()



GM_W, GM_G = 512, 4
MLA_H, MLA_NOPE, MLA_ROPE, MLA_V = 8, 64, 32, 64
MLA_QK = MLA_NOPE + MLA_ROPE
MLA_QR, MLA_KVR = 256, 128
ROPE_BASE = 10000.0


def causal_bias(c, n):
    def bias(t, b, nk):
        m = c.mask[:, TOK - nk:TOK]
        return m.unsqueeze(1).broadcast_to([P, n, nk])
    return bias


def residual_jobs(c, xs, w, alpha):
    def add(n0):
        part = c.x[:, :, n0:n0 + 512]
        return lambda r: c.nc.vector.scalar_tensor_tensor(part, part, alpha, r, ALU.mult, ALU.add)
    return [Rows(xs, w, n0, 512, "dve", add(n0)) for n0 in (0, 512)]


def post_norm(c, columns=True):
    done = c.sig("rows_normed")
    landed = c.sig("norm_params_landed").now()

    @c.block.vector
    def _(dve):
        dve.wait_ge(*landed)

    norm_stage(c, [dict(src=c.x[:, :, :], dst=c.x[:, :, :], kind="ln", eps=LN_EPS, gain=c.gain[:, :],
                        bias=c.bias[:, :])], join=False, done=done)
    if columns:
        transpose_stage(c, [([c.x[:, t, (k + i) * P:(k + i + 1) * P] for i in range(4)], c.xT[:, k:k + 4, t * P:(t + 1) * P],
                             "dve" if k else "act") for t in range(TT) for k in (0, 4)],
                        join=False, before=lambda g: done.at(g // 2 + 1))
    c.join()


def rope(c, x, cos, sin, tmp, shape):
    nc = c.nc
    x1, x2 = x
    a, b, e, f = tmp
    nc.vector.tensor_tensor(a, x1, cos, ALU.mult)
    nc.vector.tensor_tensor(b, x2, sin, ALU.mult)
    nc.vector.tensor_tensor(e, x1, sin, ALU.mult)
    c.dve(nc.vector.tensor_tensor(f, x2, cos, ALU.mult))
    nc.vector.drain()
    nc.vector.tensor_tensor(x1, a, b, ALU.subtract)
    c.dve(nc.vector.tensor_tensor(x2, e, f, ALU.add))


def ab_mixer(c, cat, ctx, ahead):
    nc, arg = c.nc, c.arg
    sb = lambda name, shape, dt=F32: c.sb("ab_" + name, shape, dt, ctx)
    half = MLA_ROPE // 2
    u, v = sb("u", [P, TT, GM_W]), sb("v", [P, TT, GM_W])
    low = sb("low", [P, TT, MLA_QR + MLA_KVR + MLA_ROPE])
    lown = sb("lown", [P, TT, MLA_QR + MLA_KVR])
    lowT = sb("lowT", [P, (MLA_QR + MLA_KVR) // P, TOK])
    gm_g, gm_b = sb("gm_g", [P, GM_W]), sb("gm_b", [P, GM_W])
    low_g = sb("low_g", [P, MLA_QR + MLA_KVR])
    bs = sb("bs", [P, GM_G])
    pos_i, pos = sb("pos_i", [P, TT], I32), sb("pos", [P, TT])
    freq, turns = sb("freq", [P, half]), sb("turns", [P, TT, half])
    ang, over = sb("ang", [P, 2, TT, half]), sb("over", [P, TT, half])
    trig = sb("trig", [P, 2, TT, half])
    wsT = sb("wsT", [P, GM_G, P])
    qrow, krow = sb("qrow", [P, TT, MLA_H, MLA_QK]), sb("krow", [P, TT, MLA_H, MLA_QK])
    vrow = sb("vrow", [P, TT, MLA_H * MLA_V])
    qT, kT = c.spare_x, c.xT
    tmp = [sb(f"rot{i}", [P, MLA_H * half]) for i in range(4)]
    load_ahead(c, "mixer_params_landed", [
        (gm_g[:, :], bcast(arg["ab_gm_ln_g"][0])), (gm_b[:, :], bcast(arg["ab_gm_ln_b"][0])),
        (low_g[:, 0:MLA_QR], bcast(arg["ab_mla_q_norm"][0])), (low_g[:, MLA_QR:], bcast(arg["ab_mla_kv_norm"][0])),
        (bs[:, :], arg["ab_gm_bs"][0].rearrange("g t -> t g")),
        (pos_i[:, :], arg["positions"][0].rearrange("(t p) -> p t", p=P))])
    w_in = arg["ab_w_in"][0]
    jobs = [
        Rows(c.xs, w_in, 0, 512, "act", lambda r: nc.scalar.activation(u[:, :, :], r, ACT.Gelu_apprx_tanh)),
        Rows(c.xs, w_in, 512, 512, "act", lambda r: nc.scalar.activation(v[:, :, :], r, ACT.Gelu_apprx_tanh)),
        Rows(c.xs, w_in, 1024, 416, "dve", lambda r: nc.vector.tensor_copy(low[:, :, :], r))]
    split_ahead(c, claim(c, jobs))
    c.join()
    projection(c, jobs)

    angles = c.sig("angles_ready")
    two_pi = 2 * math.pi
    c1 = 6.28125
    c2 = float(np.float32(round((two_pi - c1) * 2 ** 20) / 2 ** 20))
    c3 = float(np.float32(two_pi - c1 - c2))
    big = float(1.5 * 2 ** 23)
    pi_low = float(np.nextafter(np.float32(math.pi), np.float32(0)))

    @c.block.vector
    def _(dve):
        for i in range(half):
            f = float(np.exp(np.float32(-math.log(ROPE_BASE)) * np.float32(i) / np.float32(half), dtype=np.float32))
            nc.vector.memset(freq[:, i:i + 1], f)
        dve.wait_ge(*c.sig("mixer_params_landed").now())
        c.dve(nc.vector.tensor_copy(pos[:, :], pos_i[:, :]))
        dve.drain()
        for t in range(TT):
            last = nc.vector.tensor_scalar(ang[:, 0, t, :], freq[:, :], pos[:, t:t + 1], None, ALU.mult)
        c.dve(last)
        dve.drain()
        a = ang[:, 0]
        c.dve(nc.vector.tensor_scalar(turns[:, :, :], a, 1.0 / two_pi, big, ALU.mult, ALU.add))
        c.dve(nc.vector.tensor_scalar(turns[:, :, :], turns[:, :, :], big, None, ALU.subtract))
        for part in (c1, c2, c3):
            c.dve(nc.vector.scalar_tensor_tensor(a, turns[:, :, :], -part, a, ALU.mult, ALU.add))
        c.dve(nc.vector.tensor_scalar(ang[:, 1], a, math.pi / 2, None, ALU.add))
        c.dve(nc.vector.tensor_scalar(over[:, :, :], ang[:, 1], math.pi, None, ALU.is_gt))
        c.dve(nc.vector.scalar_tensor_tensor(ang[:, 1], over[:, :, :], -two_pi, ang[:, 1], ALU.mult, ALU.add))
        both = ang[:, :, :, :].rearrange("p a t f -> p (a t f)")
        nc.vector.tensor_scalar(both, both, pi_low, -pi_low, ALU.min, ALU.max).then_inc(*angles.up())

    @c.block.scalar
    def _(act):
        act.wait_ge(*angles.at(1))
        nc.scalar.activation(trig[:, :, :, :], ang[:, :, :, :], ACT.Sin)

    ws_turned, ws_masked = c.sig("spatial_turned"), c.sig("spatial_masked")

    @c.block.tensor
    def _(pe):
        ws = c.ring.take(pe, arg["ab_gm_ws"][0].rearrange("g t s -> t g s"))
        for g in range(GM_G):
            last = nc.tensor.transpose(c.psum[:, 0, g * P:(g + 1) * P], ws[:, g, :], c.ident[:, :])
        last.then_inc(c.ring.used, 1)
        c.ws_tile = c.ring.tiles

    @c.block.vector
    def _(dve):
        dve.wait_ge(c.ring.used, c.ws_tile)
        nc.vector.tensor_tensor(wsT[:, :, :], c.psum[:, 0, :].rearrange("p (g t) -> p g t", g=GM_G),
                                c.tri01[:, :].unsqueeze(1).broadcast_to([P, GM_G, P]), ALU.mult)
    norm_stage(c, [
        dict(src=v[:, :, :], dst=v[:, :, :], kind="ln", eps=LN_EPS, gain=gm_g[:, :], bias=gm_b[:, :]),
        dict(src=low[:, :, 0:MLA_QR], dst=lown[:, :, 0:MLA_QR], kind="rms", eps=LN_EPS, gain=low_g[:, 0:MLA_QR], bias=None),
        dict(src=low[:, :, MLA_QR:MLA_QR + MLA_KVR], dst=lown[:, :, MLA_QR:], kind="rms", eps=LN_EPS,
             gain=low_g[:, MLA_QR:], bias=None)])
    rows_to_columns(c, lown, lowT, 3)

    mixed = c.sig("spatial_mixed")

    @c.block.tensor
    def _(pe):
        for t in range(TT):
            for g in range(GM_G):
                last = nc.tensor.matmul(c.psum[:, t, g * P:(g + 1) * P], wsT[:, g, :], v[:, t, g * P:(g + 1) * P],
                                        start=True, stop=True)
            last.then_inc(*mixed.up())

    @c.block.vector
    def _(dve):
        for t in range(TT):
            dve.wait_ge(*mixed.at(t + 1))
            for g in range(GM_G):
                s = slice(g * P, (g + 1) * P)
                nc.vector.scalar_tensor_tensor(cat[:, t, s], c.psum[:, t, s], bs[:, g:g + 1], u[:, t, s],
                                               ALU.add, ALU.mult)
    c.join()

    qf = qrow[:, :, :, :].rearrange("p t h d -> p t (h d)")

    def keep_keys(r):
        for t in range(TT):
            last = nc.vector.tensor_copy(krow[:, t, :, 0:MLA_NOPE], r[:, t, :].rearrange("p (h d) -> p h d", h=MLA_H))
            if t == 0:
                c.dve(last)
        return last
    projection(c, [
        Rows(lowT[:, 0:2, :], arg["ab_mla_w_uq"][0], 0, 512, "act", lambda r: nc.scalar.activation(qf[:, :, 0:512], r, ACT.Copy)),
        Rows(lowT[:, 0:2, :], arg["ab_mla_w_uq"][0], 512, 256, "act", lambda r: nc.scalar.activation(qf[:, :, 512:768], r, ACT.Copy)),
        Rows(lowT[:, 2:3, :], arg["ab_mla_w_uk"][0], 0, 512, "dve", keep_keys),
        Rows(lowT[:, 2:3, :], arg["ab_mla_w_uv"][0], 0, 512, "act", lambda r: nc.scalar.activation(vrow[:, :, :], r, ACT.Copy))])

    @c.block.vector
    def _(dve):
        kr = low[:, :, MLA_QR + MLA_KVR:]
        for t in range(TT):
            cos, sin = (trig[:, i, t, :].unsqueeze(1).broadcast_to([P, MLA_H, half]) for i in (1, 0))
            q = qrow[:, t, :, MLA_NOPE:]
            rope(c, (q[:, :, 0:half], q[:, :, half:]), cos, sin,
                 [x[:, :].rearrange("p (h d) -> p h d", h=MLA_H) for x in tmp], None)
            rope(c, (kr[:, t, 0:half], kr[:, t, half:]), trig[:, 1, t, :], trig[:, 0, t, :], [x[:, 0:half] for x in tmp], None)
            dve.drain()
            nc.vector.tensor_copy(krow[:, t, :, MLA_NOPE:], kr[:, t, :].unsqueeze(1).broadcast_to([P, MLA_H, MLA_ROPE]))
    c.join()
    transpose_stage(c, [([row[:, t, h, :] for h in (2 * g, 2 * g + 1) for t in range(TT)],
                         colT[0:MLA_QK, 2 * g:2 * g + 2, :].rearrange("p h t -> p (h t)"), who)
                        for row, colT, who in ((qrow, qT, "act"), (krow, kT, "dve")) for g in range(MLA_H // 2)])
    attention(c, [(t, 0) for t in range(TT)], MLA_H, MLA_V, ahead=ahead(),
              q=lambda t, b, i: qT[0:MLA_QK, i, t * P:(t + 1) * P], k=lambda b, i, nk: kT[0:MLA_QK, i, 0:nk],
              v=lambda b, i, s: vrow[:, s, i * MLA_V:(i + 1) * MLA_V],
              out=lambda t, b: cat[:, t, GM_W:].rearrange("p (h d) -> p h d", h=MLA_H),
              scale=MLA_QK ** -0.5, bias=causal_bias(c, MLA_H), paired=False)



NSA_H, NSA_G, NSA_D = 16, 2, 64
NSA_HPG = NSA_H // NSA_G
CMP_LEN, CMP_STRIDE, CMP_HID = 32, 16, 256
NCMP = TOK // CMP_STRIDE - CMP_LEN // CMP_STRIDE + 1
C_MIX = NSA_H * NSA_D
NSA_KV = NSA_G * NSA_D
assert TOK // 64 <= 8 and TOK <= 512


def nsa_mixer(c, cat, ctx, ahead):
    nc, arg = c.nc, c.arg
    sb = lambda name, shape, dt=F32: c.sb("c_" + name, shape, dt, ctx)
    qT = sb("qT", [P, NSA_H // 2, TOK])
    kvT = sb("kvT", [P, 4, NSA_G, TOK])
    vs, vwg = sb("vs", [P, TT, NSA_KV]), sb("vwg", [P, TT, NSA_KV + 3 * NSA_H])
    blocks = sb("blocks", [P, 2, CMP_LEN // 2, NSA_G, NCMP])
    pos = sb("pos", [P, 2, CMP_LEN // 2])
    hid = sb("hid", [P, 2, CMP_HID // P, NSA_G * NCMP])
    w2 = sb("w2", [P, 2, CMP_HID // P, NSA_D])
    kc = sb("kc", [P, NSA_G * NCMP])
    vc = sb("vc", [NCMP, NSA_G, NSA_D])
    gate_b, gates = sb("gate_b", [P, 3 * NSA_H]), sb("gates", [P, TT, 3 * NSA_H])
    ends, ends01 = sb("ends", [P, TT, NCMP]), sb("ends01", [P, TT, NCMP])
    oc = sb("oc", [P, TT, C_MIX])
    osel, input_lows = c.sb_twice("c_osel", [P, TT, C_MIX], ctx)
    pcT = c.xT[0:NCMP].rearrange("p (a k) t -> p a (k t)", a=2).rearrange("p a (h q) -> p a h q", q=P)
    sc = sb("sc", [P, TT, NSA_H, NCMP])
    red = sb("red", [P, TT, NSA_H])
    posv = arg["c_cmp_pos"][0].rearrange("i (j a) d -> a d i j", a=2)
    load_params(c, [(gate_b[:, :], bcast(arg["c_gate_b"][0])),
                    (w2[:, 0], k_tiles(arg["c_w_ck2"][0])), (w2[:, 1], k_tiles(arg["c_w_cv2"][0]))] +
                [(pos[a * 64:(a + 1) * 64, i, :], posv[a, :, i, :]) for a in range(2) for i in range(2)])

    @c.block.gpsimd
    def _(pool):
        nc.gpsimd.memset(ends[:, :, :], 0.0)
        c.pool(nc.gpsimd.memset(ends01[:, :, :], 1.0))
        pool.drain()
        for t in range(TT):
            for m, fill in ((ends, NEG), (ends01, 0.0)):
                nc.gpsimd.affine_select(out=m[:, t, :], in_=m[:, t, :], compare_op=ALU.is_ge, fill=fill,
                                        base=t * P - CMP_LEN + 1, pattern=[[-CMP_STRIDE, NCMP]], channel_multiplier=1)
    w_in = arg["c_w_in"][0]
    act_copy = lambda dst: (lambda r: nc.scalar.activation(dst, r, ACT.Copy))
    dve_copy = lambda dst: (lambda r: nc.vector.tensor_copy(dst, r))
    at = lambda i: C_MIX + i * NSA_KV

    def spread(i, copy):
        def take(r):
            for g in range(NSA_G):
                for a in range(2):
                    last = copy(kvT[a * 64:(a + 1) * 64, i, g, :], r[g * 64:(g + 1) * 64, 0, :])
            return last
        return take
    parts = (c.xh[:, :, :], input_lows[:, :, :].rearrange("p t (k s) -> p (t k) s", s=TOK))
    high = c.sig("input_high")

    def input_low(dve):
        dve.wait_ge(*high.at(1))
        nc.vector.tensor_tensor(parts[1], c.xT[:, :, :], c.xh[:, :, :].bitcast(F32), ALU.subtract).then_inc(*c.sig("input_split").up())
    projection(c, [
        Step("act", lambda act: nc.scalar.activation(c.xh[:, :, :], c.xT[:, :, :], ACT.Copy).then_inc(*high.up())),
        Step("dve", input_low),
        Rows(c.xT, w_in, at(3), NSA_KV, "act", act_copy(vs[:, :, :])),
        Rows(c.xT, w_in, at(5), NSA_KV + 3 * NSA_H, "dve", dve_copy(vwg[:, :, :])),
        Cols(parts, w_in, at(0), NSA_KV, "act", spread(0, lambda d, r: nc.scalar.activation(d, r, ACT.Copy))),
        Cols(parts, w_in, at(1), NSA_KV, "dve", spread(1, nc.vector.tensor_copy)),
        Cols(parts, w_in, at(2), NSA_KV, "act", spread(2, lambda d, r: nc.scalar.activation(d, r, ACT.Copy))),
        Cols(parts, w_in, at(4), NSA_KV, "dve", spread(3, nc.vector.tensor_copy))] + [
        Cols(parts, w_in, j * 256, 256, "dve" if j % 2 else "act",
             (dve_copy if j % 2 else act_copy)(qT[:, 2 * j:2 * j + 2, :])) for j in range(4)])

    pair = CMP_LEN // 2
    built, hidden, squashed, compressed = c.sig("blocks_built"), c.sig("cmp_hidden"), c.sig("cmp_squashed"), c.sig("cmp_ready")

    @c.block.vector
    def _(dve):
        for i in range(2):
            for a in range(2):
                h = slice(a * 64, (a + 1) * 64)
                for g in range(NSA_G):
                    src = kvT[h, i, g, :].rearrange("p (m r) -> p r m", r=CMP_STRIDE)
                    for half in range(2):
                        js = slice(half * 8, half * 8 + 8)
                        last = nc.vector.tensor_tensor(
                            blocks[h, i, js, g, :], src[:, a:CMP_STRIDE:2, half:half + NCMP],
                            pos[h, i, js].unsqueeze(2).broadcast_to([64, 8, NCMP]), ALU.add)
            dve.drain().then_inc(*built.up())
        for t in range(TT):
            last = nc.vector.tensor_tensor(gates[:, t, :], vwg[:, t, NSA_KV:], gate_b[:, :], ALU.add)
        dve.drain().then_inc(*built.up())

    @c.block.tensor
    def _(pe):
        for i, name in enumerate(("c_w_ck1", "c_w_cv1")):
            pe.wait_ge(*built.at(i + 1))
            src = k_tiles(arg[name][0])
            for m in range(2):
                w1 = c.ring.take(pe, src[:, :, m * P:(m + 1) * P])
                for j in range(pair):
                    last = nc.tensor.matmul(c.psum[:, 2 * i + m, 0:NSA_G * NCMP], w1[:, j, :],
                                            blocks[:, i, j].rearrange("p g n -> p (g n)"), start=(j == 0), stop=(j == pair - 1))
                last.then_inc(c.ring.used, 1)
        c.cmp_tile = c.ring.tiles
        pe.wait_ge(*squashed.at(1))
        for m in range(2):
            last = nc.tensor.matmul(c.psum[0:64, 4, 0:NSA_G * NCMP], w2[:, 0, m, :], hid[:, 0, m, :], start=(m == 0), stop=(m == 1))
        last.then_inc(*compressed.up())
        for m in range(2):
            last = nc.tensor.matmul(c.psum[64:128, 5, 0:NSA_G * NCMP], w2[:, 0, m, :], hid[:, 0, m, :], start=(m == 0), stop=(m == 1))
        last.then_inc(*compressed.up())
        for g in range(NSA_G):
            for m in range(2):
                last = nc.tensor.matmul(c.psum[0:NCMP, 6 + g, 0:NSA_D], hid[:, 1, m, g * NCMP:(g + 1) * NCMP], w2[:, 1, m, :],
                                        start=(m == 0), stop=(m == 1))
        last.then_inc(*compressed.up())

    @c.block.scalar
    def _(act):
        act.wait_ge(c.ring.used, c.cmp_tile)
        for i in range(2):
            last = nc.scalar.activation(hid[:, i], c.psum[:, 2 * i:2 * i + 2, 0:NSA_G * NCMP], ACT.Gelu_apprx_tanh)
        act.drain().then_inc(*squashed.up())
        act.wait_ge(*built.at(3))
        nc.scalar.activation(gates[:, :, :], gates[:, :, :], ACT.Sigmoid)

    @c.block.vector
    def _(dve):
        dve.wait_ge(*compressed.at(3))
        nc.vector.tensor_copy(kc[0:64, :], c.psum[0:64, 4, 0:NSA_G * NCMP])
        nc.vector.tensor_copy(kc[64:128, :], c.psum[64:128, 5, 0:NSA_G * NCMP])
        for g in range(NSA_G):
            nc.vector.tensor_copy(vc[:, g, :], c.psum[0:NCMP, 6 + g, 0:NSA_D])
    c.join()

    scored, softened = c.sig("cmp_scores"), c.sig("cmp_probs")
    exped = c.sig("cmp_exp")
    in_exp = c.sig("cmp_centred")

    @c.block.tensor
    def _(pe):
        for t in range(TT):
            for h in range(NSA_H):
                g, a = h // NSA_HPG, h % 2
                rows = slice(a * 64, a * 64 + 64)
                last = nc.tensor.matmul(c.psum[:, 2 * a + t, (h // 2) * NCMP:(h // 2 + 1) * NCMP],
                                        qT[rows, h // 2, t * P:(t + 1) * P], kc[rows, g * NCMP:(g + 1) * NCMP], start=True, stop=True)
        last.then_inc(*scored.up())

    @c.block.vector
    def _(dve):
        dve.wait_ge(*scored.at(1))
        for t in range(TT):
            for a in range(2):
                nc.vector.scalar_tensor_tensor(
                    sc[:, t, a:NSA_H:2, :], c.psum[:, 2 * a + t, 0:8 * NCMP].rearrange("p (h n) -> p h n", n=NCMP), NSA_D ** -0.5,
                    ends[:, t, :].unsqueeze(1).broadcast_to([P, 8, NCMP]), ALU.mult, ALU.add)
        dve.drain()
        c.dve(nc.vector.tensor_reduce(red[:, :, :], sc[:, :, :, :], AX_X, ALU.max))
        nc.vector.tensor_tensor(sc[:, :, :, :], sc[:, :, :, :], red[:, :, :].unsqueeze(3).broadcast_to([P, TT, NSA_H, NCMP]),
                                ALU.subtract).then_inc(*in_exp.up())
        dve.wait_ge(*exped.at(1))
        c.dve(nc.vector.tensor_reduce(red[:, :, :], sc[:, :, :, :], AX_X, ALU.add))
        c.dve(nc.vector.reciprocal(red[:, :, :], red[:, :, :]))
        c.dve(nc.vector.tensor_tensor(sc[:, :, :, :], sc[:, :, :, :], red[:, :, :].unsqueeze(3).broadcast_to([P, TT, NSA_H, NCMP]), ALU.mult))
        nc.vector.tensor_tensor(sc[:, :, :, :], sc[:, :, :, :], ends01[:, :, :].unsqueeze(2).broadcast_to([P, TT, NSA_H, NCMP]),
                                ALU.mult).then_inc(*softened.up())

    @c.block.scalar
    def _(act):
        act.wait_ge(*in_exp.at(1))
        nc.scalar.activation(sc[:, :, :, :], sc[:, :, :, :], ACT.Exp).then_inc(*exped.up())

    turned, copied, out_ready, taken = c.sig("cmp_turned"), c.sig("cmp_copied"), c.sig("cmp_out"), c.sig("cmp_taken")

    @c.block.tensor
    def _(pe):
        pe.wait_ge(*softened.at(1))
        for t in range(TT):
            for g in range(NSA_G):
                j = 2 * t + g
                if j >= 2:
                    pe.wait_ge(*copied.at(j - 1))
                for i in range(NSA_HPG):
                    last = nc.tensor.transpose(c.psum[0:NCMP, 4 + 2 * (j % 2) + i // 4, (i % 4) * P:(i % 4 + 1) * P],
                                               sc[:, t, g * NSA_HPG + i, :], c.ident[:, :])
                last.then_inc(*turned.up())
                pe.wait_ge(*copied.at(j + 1))
                if j >= 4:
                    pe.wait_ge(*taken.at(j - 3))
                for i in range(NSA_HPG):
                    last = nc.tensor.matmul(c.psum[:, j, i * NSA_D:(i + 1) * NSA_D], pcT[:, j % 2, i, :], vc[:, g, :], start=True, stop=True)
                last.then_inc(*out_ready.up())

    @c.block.vector
    def _(dve):
        for j in range(4):
            t, g = j // 2, j % 2
            dve.wait_ge(*turned.at(j + 1))
            if j >= 2:
                dve.wait_ge(*out_ready.at(j - 1))
            b0 = [4, 6][j % 2]
            nc.vector.tensor_copy(pcT[:, j % 2].rearrange("p (b i) t -> p b (i t)", b=2), c.psum[0:NCMP, b0:b0 + 2, :]).then_inc(*copied.up())
            dve.wait_ge(*out_ready.at(j + 1))
            gt = gates[:, t, g * 8:g * 8 + 8].unsqueeze(2).broadcast_to([P, 8, NSA_D])
            nc.vector.tensor_tensor(oc[:, t, g * 512:(g + 1) * 512].rearrange("p (h d) -> p h d", d=NSA_D),
                                    c.psum[:, j, :].rearrange("p (h d) -> p h d", d=NSA_D), gt, ALU.mult).then_inc(*taken.up())
    c.join()
    for branch, (ki, vals) in enumerate(((2, vs), (3, vwg))):
        attention(c, [(t, g) for t in range(TT) for g in range(NSA_G)], NSA_HPG, NSA_D,
                  q=lambda t, g, i: qT[(i % 2) * 64:(i % 2) * 64 + 64, g * 4 + i // 2, t * P:(t + 1) * P],
                  k=lambda g, i, nk: kvT[(i % 2) * 64:(i % 2) * 64 + 64, ki, g, 0:nk],
                  v=lambda g, i, s: vals[:, s, g * NSA_D:(g + 1) * NSA_D],
                  out=lambda t, g: (osel, cat)[branch][:, t, g * 512:(g + 1) * 512].rearrange("p (h d) -> p h d", h=8),
                  scale=NSA_D ** -0.5, bias=causal_bias(c, 8), ahead=ahead() if branch else ())

    @c.block.vector
    def _(dve):
        for branch, o in ((1, osel), (2, cat)):
            for t in range(TT):
                gt = gates[:, t, branch * 16:branch * 16 + 16].unsqueeze(2).broadcast_to([P, 16, NSA_D])
                ov = o[:, t, :].rearrange("p (h d) -> p h d", d=NSA_D)
                nc.vector.tensor_tensor(ov, ov, gt, ALU.mult)
            dve.drain()
            nc.vector.tensor_tensor(o[:, :, :], o[:, :, :], (oc, osel)[branch - 1][:, :, :], ALU.add)
            dve.drain()
    c.join()



CH = 256


def claim_stream(c, n, gate, up, down):
    ring = c.ring
    p0, s0, loaded0 = ring.tiles, len(ring.split_tiles), list(ring.loaded)
    ring.plan.append(("stream", p0, n, gate, up, down))
    ring.tiles += 3 * n
    ring.split_tiles += range(p0, p0 + 3 * n)
    for x in range(p0, p0 + 3 * n):
        ring.loaded[x % RING] += 16
    return (p0, loaded0, s0), [Tile(ring, x, KD, CH, (ring.full[x % RING], loaded0[x % RING] + 16), s0 + x - p0)
                               for x in (p0, p0 + 1)]


def stream_ffn(c, n, start, then, ctx):
    nc, ring = c.nc, c.ring
    y = c.x
    squashed = c.sb("ffn_squashed", [P, 2, 2 * TOK], ctx=ctx)
    hidden, hidden_low = c.sb_twice("ffn_hidden", [P, 2, 2, TOK], ctx)
    hidden_high = c.sb("ffn_hidden_high", [P, 2, 2, TOK], F32R, ctx=ctx)
    gate_squashed, hidden_ready, added = c.sig("gate_squashed"), c.sig("hidden_ready"), c.sig("chunk_added")
    p0, loaded0, s0 = start
    FIRST, U = 1, 6
    assert 3 * U % RING == 0 and 3 * U % HIGHS == 0 and U % 2 == 0
    loops = max(0, (n - 1 - FIRST) // U)
    rest = range(FIRST + U * loops, n - 1)

    def nth_load(x):
        first = x - (x - p0) // RING * RING
        return loaded0[x % RING] + 16 * ((x - first) // RING + 1)

    def gate_tile(j):
        return p0 if j == 0 else p0 + 2 + 3 * (j - 1)

    def up_tile(j):
        return gate_tile(j) + 1

    def down_tile(j):
        return p0 + 2 + 3 * j + (2 if j < n - 1 else 0)

    def two_products(pe, j, i):
        if j >= 2:
            pe.wait_ge(hidden_ready.sem, hidden_ready.base + (j - 1) + U * i)
        for tile, bank in ((gate_tile(j), 0), (up_tile(j), 2)):
            pe.wait_ge(ring.split_ready, s0 + tile - p0 + 1 + 3 * U * i)
            high, low = ring.high(s0 + tile - p0, KD, CH), ring.low(tile, KD, CH)
            for m in range(2):
                for k in range(KD):
                    ms = slice(m * P, (m + 1) * P)
                    last = three_products(nc, c.psum[:, bank + j % 2, m * TOK:(m + 1) * TOK], (high[:, k, ms], low[:, k, ms]),
                                          [x[:, k, :] for x in c.xs], k == 0, k == KD - 1)
            last.then_inc(ring.used, 1)

    def third_product(pe, j, i):
        tile = down_tile(j)
        pe.wait_ge(hidden_ready.sem, hidden_ready.base + j + 1 + U * i)
        if j >= 1:
            pe.wait_ge(added.sem, added.base + 2 * j + 2 * U * i)
        pe.wait_ge(ring.split_ready, s0 + tile - p0 + 1 + 3 * U * i)
        high, low = ring.high(s0 + tile - p0, 2, D), ring.low(tile, 2, D)
        for t in range(TT):
            for h in range(2):
                for m in range(2):
                    ts, hs = slice(t * P, (t + 1) * P), slice(h * 512, (h + 1) * 512)
                    last = three_products(nc, c.psum[:, 4 + 2 * t + h, :],
                                          (hidden_high[:, j % 2, m, ts], hidden_low[:, j % 2, m, ts]),
                                          (high[:, m, hs], low[:, m, hs]), m == 0, m == 1)
        last.then_inc(ring.used, 1)

    def squash(act, j, i):
        act.wait_ge(ring.used, gate_tile(j) + 1 + 3 * U * i)
        nc.scalar.activation(squashed[:, j % 2, :], c.psum[:, j % 2, :], ACT.Silu).then_inc(gate_squashed.sem, 1)

    def combine(dve, j, i):
        dve.wait_ge(ring.used, up_tile(j) + 1 + 3 * U * i)
        dve.wait_ge(gate_squashed.sem, gate_squashed.base + j + 1 + U * i)
        h, hh, hl = (x[:, j % 2].rearrange("p m t -> p (m t)") for x in (hidden, hidden_high, hidden_low))
        nc.vector.tensor_tensor(h, squashed[:, j % 2, :], c.psum[:, 2 + j % 2, :], ALU.mult)
        dve.drain()
        nc.vector.tensor_copy(hh, h)
        dve.drain()
        nc.vector.tensor_tensor(hl, h, hh.bitcast(F32), ALU.subtract).then_inc(hidden_ready.sem, 1)

    def round_high(act, tile, i):
        act.wait_ge(ring.full[tile % RING], nth_load(tile) + 16 * (3 * U // RING) * i)
        if tile - p0 >= HIGHS:
            act.wait_ge(ring.used, tile - HIGHS + 1 + 3 * U * i)
        nc.scalar.activation(ring.high(s0 + tile - p0, 1, SLOT), ring.view(tile, 1, SLOT), ACT.Copy).then_inc(ring.high_ready, 1)

    def leave_low(dve, tile, i):
        dve.wait_ge(ring.high_ready, s0 + tile - p0 + 1 + 3 * U * i)
        w = ring.view(tile, 1, SLOT)
        nc.vector.tensor_tensor(ring.low(tile, 1, SLOT), w, ring.high(s0 + tile - p0, 1, SLOT).bitcast(F32), ALU.subtract).then_inc(ring.split_ready, 1)

    def add(dve, j, i):
        dve.wait_ge(ring.used, down_tile(j) + 1 + 3 * U * i)
        for t in range(TT):
            part = c.psum[:, 4 + 2 * t:6 + 2 * t, :].rearrange("p h n -> p (h n)")
            if j >= 1:
                dve.wait_ge(added.sem, added.base + 2 * j - 1 + t + 2 * U * i)
            nc.vector.tensor_tensor(y[:, t, :], part, y[:, t, :], ALU.add).then_inc(added.sem, 1)

    @c.block.tensor
    def _(pe):
        two_products(pe, 0, 0)
        for j in range(FIRST):
            two_products(pe, j + 1, 0)
            third_product(pe, j, 0)
        if loops:
            with pe.Fori(0, loops) as i:
                for j in range(FIRST, FIRST + U):
                    two_products(pe, j + 1, i)
                    third_product(pe, j, i)
        for j in rest:
            two_products(pe, j + 1, 0)
            third_product(pe, j, 0)
        third_product(pe, n - 1, 0)

    def split_first(eng, split):
        for tile in (gate_tile(1), up_tile(1)):
            split(eng, tile, 0)

    def steps(eng, step):
        step(0, 0)
        if loops:
            with eng.Fori(0, loops) as i:
                for j in range(FIRST, FIRST + U):
                    step(j, i)
        for j in rest:
            step(j, 0)

    @c.block.scalar
    def _(act):
        def step(j, i):
            if j + 2 < n:
                round_high(act, gate_tile(j + 2), i)
            squash(act, j + 1, i)
            if j + 2 < n:
                round_high(act, up_tile(j + 2), i)
            round_high(act, down_tile(j + 1), i)
        split_first(act, round_high)
        squash(act, 0, 0)
        round_high(act, down_tile(0), 0)
        steps(act, step)
        split(act, "act", then)

    @c.block.vector
    def _(dve):
        def step(j, i):
            if j + 2 < n:
                leave_low(dve, gate_tile(j + 2), i)
            combine(dve, j + 1, i)
            if j + 2 < n:
                leave_low(dve, up_tile(j + 2), i)
            leave_low(dve, down_tile(j + 1), i)
            add(dve, j, i)
        split_first(dve, leave_low)
        combine(dve, 0, 0)
        leave_low(dve, down_tile(0), 0)
        steps(dve, step)
        split(dve, "dve", then)
        add(dve, n - 1, 0)
    gate_squashed.count += n
    hidden_ready.count += n
    added.count += 2 * n
    c.join()


def logits_stage(c, wr, br, n, logits):
    nc = c.nc
    ready = c.sig("router_logits")

    @c.block.tensor
    def _(pe):
        for t in range(TT):
            for k in range(KD):
                last = nc.tensor.matmul(c.psum[:, t, 0:n], c.xT[:, k, t * P:(t + 1) * P], wr[:, k, :],
                                        start=(k == 0), stop=(k == KD - 1))
        last.then_inc(*ready.up())

    @c.block.vector
    def _(dve):
        dve.wait_ge(*ready.at(1))
        c.dve(nc.vector.tensor_tensor(logits, c.psum[:, 0:TT, 0:n], br.unsqueeze(1).broadcast_to([P, TT, n]), ALU.add))


class SplitExpert:

    def __init__(self, c, p0, per, chunks, xg, squashed, hidden, outT, landed, used):
        self.c, self.p0, self.per, self.chunks, self.xg, self.outT = c, p0, per, chunks, xg, outT
        self.landed, self.used = landed, used
        self.s0 = len(c.ring.split_tiles)
        assert (3 * chunks) % HIGHS == 0
        self.squashed, self.hidden = squashed, hidden
        parts = c.S_rounded[:, 1, :, :].rearrange("p k (a s) -> p a k s", a=2)
        self.xh, self.xl = parts[:, 0], parts[:, 1]
        flat = c.xl[:, :, :].rearrange("p k t -> p (k t)")
        self.hh, self.hl = (flat[:, a:a + 512].rearrange("p (j m s) -> p j m s", j=2, m=2) for a in (0, 512))
        self.rows = c.xT[:, :, :].rearrange("p k t -> p (k t)")[:, 1024:2048]
        self.window_low, self.turned = c.sig("window_low_ready"), c.sig("hidden_turned")
        self.hidden_high, self.hidden_low = c.sig("hidden_high_ready"), c.sig("hidden_low_ready")
        self.rows_act, self.rows_dve, self.rows_turned = c.sig("rows_taken_act"), c.sig("rows_taken_dve"), c.sig("output_turned")
        self.base = {x: x.count for x in (self.window_low, self.turned, self.hidden_high, self.hidden_low,
                                          self.rows_act, self.rows_dve, self.rows_turned)}

    def count(self, n):
        for x in self.base:
            x.count += n * (self.chunks if x in (self.turned, self.hidden_high, self.hidden_low) else 1)
        self.c.ring.split_tiles += [self.p0 + e * self.per + q for e in range(n) for q in range(3 * self.chunks)]

    def nth(self, signal, k, i, each):
        return signal.sem, each * i + (self.base[signal] + k)

    def gate(self, j):
        return 0 if j == 0 else 3 * j - 1

    def up(self, j):
        return self.gate(j) + 1

    def down(self, j):
        return 3 * j + (4 if j < self.chunks - 1 else 2)

    def parts(self, q, kt, cols):
        return self.c.ring.high(self.s0 + q, kt, cols), self.c.ring.low(self.p0 + q, kt, cols)

    def wait_split(self, pe, q, i):
        pe.wait_ge(self.c.ring.split_ready, 3 * self.chunks * i + (self.s0 + q + 1))

    def tensor(self, pe, i, wait_written, spare):
        c, nc, chunks = self.c, self.c.nc, self.chunks
        psum = c.psum

        def first(q, j, bank):
            self.wait_split(pe, q, i)
            high, low = self.parts(q, KD, CH)
            for k in range(KD):
                last = three_products(nc, psum[:, bank + j % 2, 0:CH], (self.xh[:, k, :], self.xl[:, k, :]),
                                      (high[:, k, :], low[:, k, :]), k == 0, k == KD - 1)
            last.then_inc(c.ring.used, 1)

        def turn(j):
            pe.wait_ge(*self.hidden_made(j, i))
            if j == 0:
                wait_written()
            for m in range(2):
                last = nc.tensor.transpose(psum[:, 6 + j % 2, m * P:(m + 1) * P], self.hidden[:, j % 2, 0, m * P:(m + 1) * P], c.ident[:, :])
            last.then_inc(self.turned.sem, 1)

        def third(j):
            self.wait_split(pe, self.down(j), i)
            pe.wait_ge(*self.nth(self.hidden_low, j + 1, i, chunks))
            high, low = self.parts(self.down(j), 2, D)
            for h in range(2):
                hs = slice(h * 512, (h + 1) * 512)
                for m in range(2):
                    last = three_products(nc, psum[:, 4 + h, :], (self.hh[:, j % 2, m, :], self.hl[:, j % 2, m, :]),
                                          (high[:, m, hs], low[:, m, hs]), j == 0 and m == 0, j == chunks - 1 and m == 1)
            last.then_inc(c.ring.used, 1 + (spare if j == chunks - 1 else 0))

        pe.wait_ge(*self.nth(self.window_low, 1, i, 1))
        first(self.gate(0), 0, 0)
        first(self.up(0), 0, 2)
        for j in range(chunks):
            if j + 1 < chunks:
                if j >= 1:
                    pe.wait_ge(*self.hidden_made(j - 1, i))
                first(self.gate(j + 1), j + 1, 0)
            turn(j)
            if j + 1 < chunks:
                first(self.up(j + 1), j + 1, 2)
            third(j)
        pe.wait_ge(*self.nth(self.rows_act, 1, i, 1))
        pe.wait_ge(*self.nth(self.rows_dve, 1, i, 1))
        for k in range(KD):
            last = nc.tensor.transpose(psum[:, 6 + k // 4, (k % 4) * P:(k % 4 + 1) * P], self.rows[:, k * P:(k + 1) * P], c.ident[:, :])
        last.then_inc(self.rows_turned.sem, 1)

    def hidden_made(self, j, i):
        h = self.c.sig("hidden_ready")
        return h.sem, self.chunks * i + (h.base + 1 + j + 1)

    def high(self, act, q, i):
        ring = self.c.ring
        self.landed(act, self.p0 + q, i)
        before = q - HIGHS if q >= HIGHS else q - HIGHS + 3 * self.chunks - self.per
        act.wait_ge(ring.used, self.per * i + (self.p0 + before + 1))
        self.c.nc.scalar.activation(ring.high(self.s0 + q, 1, SLOT), ring.view(self.p0 + q, 1, SLOT), ACT.Copy).then_inc(ring.high_ready, 1)

    def low(self, dve, q, i):
        ring = self.c.ring
        dve.wait_ge(ring.high_ready, 3 * self.chunks * i + (self.s0 + q + 1))
        self.c.nc.vector.tensor_tensor(ring.low(self.p0 + q, 1, SLOT), ring.view(self.p0 + q, 1, SLOT),
                                       ring.high(self.s0 + q, 1, SLOT).bitcast(F32), ALU.subtract).then_inc(ring.split_ready, 1)

    def order(self, split, squash, part, window):
        window()
        for q in (self.gate(0), self.up(0), self.gate(1)):
            split(q)
        squash(0)
        split(self.up(1))
        split(self.down(0))
        for j in range(self.chunks):
            part(j)
            if j + 2 < self.chunks:
                split(self.gate(j + 2))
            if j + 1 < self.chunks:
                squash(j + 1)
            if j + 2 < self.chunks:
                split(self.up(j + 2))
            if j + 1 < self.chunks:
                split(self.down(j + 1))

    def hidden_columns(self, j):
        return self.c.psum[:, 6 + j % 2, 0:2 * P].rearrange("p (m s) -> p m s", m=2)

    def scalar(self, act, i, o, windowed, gate_squashed):
        c, nc = self.c, self.c.nc

        def window():
            nc.scalar.activation(self.xh, self.xg[:, :, bass.ds(o, P)], ACT.Copy).then_inc(windowed.sem, 1)

        def squash(j):
            self.used(act, self.p0 + self.gate(j), i)
            nc.scalar.activation(self.squashed[:, j % 2, 0, :], c.psum[:, j % 2, 0:CH], ACT.Silu).then_inc(gate_squashed.sem, 1)

        def part(j):
            act.wait_ge(*self.nth(self.turned, j + 1, i, self.chunks))
            nc.scalar.activation(self.hh[:, j % 2], self.hidden_columns(j), ACT.Copy).then_inc(self.hidden_high.sem, 1)
        self.order(lambda q: self.high(act, q, i), squash, part, window)
        self.used(act, self.p0 + self.down(self.chunks - 1), i)
        nc.scalar.activation(self.rows[:, 0:512], c.psum[:, 4, :], ACT.Copy).then_inc(self.rows_act.sem, 1)

    def vector(self, dve, i, o, windowed, wait_squashed, hidden_ready, written):
        c, nc = self.c, self.c.nc

        def window():
            dve.wait_ge(*windowed)
            nc.vector.tensor_tensor(self.xl, self.xg[:, :, bass.ds(o, P)], self.xh.bitcast(F32), ALU.subtract).then_inc(self.window_low.sem, 1)

        def combine(j):
            self.used(dve, self.p0 + self.up(j), i)
            wait_squashed(j)
            nc.vector.tensor_tensor(self.hidden[:, j % 2, 0, :], self.squashed[:, j % 2, 0, :], c.psum[:, 2 + j % 2, 0:CH], ALU.mult).then_inc(hidden_ready.sem, 1)

        def part(j):
            dve.wait_ge(*self.nth(self.hidden_high, j + 1, i, self.chunks))
            nc.vector.tensor_tensor(self.hl[:, j % 2], self.hidden_columns(j), self.hh[:, j % 2].bitcast(F32), ALU.subtract).then_inc(self.hidden_low.sem, 1)
        self.order(lambda q: self.low(dve, q, i), combine, part, window)
        self.used(dve, self.p0 + self.down(self.chunks - 1), i)
        nc.vector.tensor_copy(self.rows[:, 512:], c.psum[:, 5, :]).then_inc(self.rows_dve.sem, 1)
        dve.wait_ge(*self.nth(self.rows_turned, 1, i, 1))
        nc.vector.tensor_copy(self.outT[:, :, bass.ds(o, P)],
                              c.psum[:, 6:8, :].rearrange("p b (k s) -> p (b k) s", k=4)).then_inc(written.sem, 1)


SLOTS = 2 * TOK


def sparse_experts(c, n, chunks, unroll, narrow, rows, oh, pw, gate, up, down, outT, alpha, ctx, params=(), meanwhile=None):
    nc, ring = c.nc, c.ring
    width = SLOTS + TOK
    sb = lambda name, shape, dt=F32: c.sb("e_" + name, shape, dt, ctx)
    if outT is None:
        outT = sb("outT", [P, KD, width])
    xg = sb("xg", [P, KD, width]) if chunks > 1 else c.ring.spare[:, :, :].rearrange("p a b -> p (a b)")[:, 0:KD * width].rearrange("p (k s) -> p k s", k=KD)
    squashed, hidden = (c.spare_x[:, a:a + 4, :].rearrange("p (a b) t -> p a b t", a=2) for a in (0, 4))
    member, place, cnt = sb("member", [P, TT, n]), sb("place", [P, TT, n]), sb("cnt", [P, n])
    off, ends, prod = sb("off", [P, n]), sb("ends", [P, n]), sb("prod", [P, TT, 2, n])
    slot = sb("slot", [P, TT, 2])
    cnt_i, off_i = sb("cnt_i", [1, n], I32), sb("off_i", [1, n], I32)
    flat = outT[:, :, :].rearrange("p k s -> p (k s)")
    G = flat[:, 2048:3072].rearrange("p (t s) -> p t s", t=TT)
    GW = flat[:, 3072:4096].rearrange("p (t s) -> p t s", t=TT)
    iota_i, iota = flat[:, 4096:4608].bitcast(I32), flat[:, 4608:5120]
    part = flat[:, 5120:6144].rearrange("p (t s) -> p t s", t=TT)
    spread = c.PT[:, :, :].rearrange("p a b -> p (a b)").rearrange("p (s t) -> p s t", t=TOK)
    if params:
        load_params(c, params)

    joined, ranked, iotas, matrices = c.sig("members_ready"), c.sig("ranks_ready"), c.sig("iota_ready"), c.sig("matrices_ready")
    gathered, padded = c.sig("rows_gathered"), c.sig("gather_copied")

    @c.block.gpsimd
    def _(pool):
        nc.gpsimd.iota(iota_i, pattern=[[1, SLOTS]], base=0, channel_multiplier=0).then_inc(*iotas.up())
        nc.gpsimd.memset(xg[:, :, SLOTS:], 0.0)

    @c.block.vector
    def _(dve):
        nc.vector.tensor_tensor(member[:, :, :], oh[:, :, 0, :], oh[:, :, 1, :], ALU.add).then_inc(*joined.up())
        dve.wait_ge(*iotas.at(1))
        c.dve(nc.vector.tensor_copy(iota, iota_i))
        dve.wait_ge(*ranked.at(1))
        c.dve(nc.vector.tensor_copy(cnt[:, :], c.psum[:, 2, 0:n]))
        c.dve(nc.vector.tensor_tensor_scan(ends[:, :], c.ones[:, 0:n], cnt[:, :], 0.0, ALU.mult, ALU.add))
        c.dve(nc.vector.tensor_tensor(off[:, :], ends[:, :], cnt[:, :], ALU.subtract))
        nc.vector.tensor_copy(cnt_i[:, :], cnt[0:1, :])
        nc.vector.tensor_copy(off_i[:, :], off[0:1, :])
        for t in range(TT):
            last = nc.vector.scalar_tensor_tensor(place[:, t, :], c.psum[:, t, 0:n], -1.0, off[:, :], ALU.add, ALU.add)
        c.dve(last)
        dve.drain()
        c.dve(nc.vector.tensor_tensor(prod[:, :, :, :], oh[:, :, :, :], place[:, :, :].unsqueeze(2).broadcast_to([P, TT, 2, n]), ALU.mult))
        c.dve(nc.vector.tensor_reduce(slot[:, :, :], prod[:, :, :, :], AX_X, ALU.add))
        for t in range(TT):
            nc.vector.tensor_scalar(G[:, t, :], iota, slot[:, t, 0:1], None, ALU.is_equal)
            nc.vector.tensor_scalar(GW[:, t, :], iota, slot[:, t, 0:1], pw[:, t, 0:1], ALU.is_equal, ALU.mult)
            nc.vector.tensor_scalar(part[:, t, :], iota, slot[:, t, 1:2], pw[:, t, 1:2], ALU.is_equal, ALU.mult)
        dve.drain()
        for t in range(TT):
            nc.vector.scalar_tensor_tensor(G[:, t, :], iota, slot[:, t, 1:2], G[:, t, :], ALU.is_equal, ALU.add)
        nc.vector.tensor_tensor(GW, GW, part, ALU.add)
        dve.drain().then_inc(*matrices.up())

    @c.block.tensor
    def _(pe):
        pe.wait_ge(*joined.at(1))
        nc.tensor.matmul(c.psum[:, 0, 0:n], c.tri01[:, :], member[:, 0, :], start=True, stop=True)
        nc.tensor.matmul(c.psum[:, 1, 0:n], c.ones[:, :], member[:, 0, :], start=True, stop=False)
        nc.tensor.matmul(c.psum[:, 1, 0:n], c.tri01[:, :], member[:, 1, :], start=False, stop=True)
        for t in range(TT):
            last = nc.tensor.matmul(c.psum[:, 2, 0:n], c.ones[:, :], member[:, t, :], start=(t == 0), stop=(t == TT - 1))
        last.then_inc(*ranked.up())
        pe.wait_ge(*matrices.at(1))
        for k in range(KD):
            for t in range(TT):
                last = nc.tensor.matmul(c.psum[:, k, :], rows[:, t, k * P:(k + 1) * P], G[:, t, :], start=(t == 0), stop=(t == TT - 1))
            last.then_inc(*gathered.up())

    @c.block.vector
    def _(dve):
        for k in range(0, KD, 2):
            dve.wait_ge(*gathered.at(k + 1))
            nc.vector.tensor_copy(xg[:, k, 0:SLOTS], c.psum[:, k, :])

    @c.block.scalar
    def _(act):
        for k in range(1, KD, 2):
            act.wait_ge(*gathered.at(k + 1))
            nc.scalar.activation(xg[:, k, 0:SLOTS], c.psum[:, k, :], ACT.Copy)
    c.join()
    transpose_stage(c, [([GW[:, t, s * P:(s + 1) * P] for s in (2 * g, 2 * g + 1) for t in range(TT)],
                         spread[:, 2 * g:2 * g + 2, :].rearrange("p s t -> p (s t)"), ("act", "dve")[g]) for g in range(2)])

    windowed, gate_squashed = c.sig("window_ready"), c.sig("gate_squashed")
    hidden_ready, written = c.sig("hidden_ready"), c.sig("expert_written")
    xw = c.S
    ahead = chunks == 1
    bufs = 2 if ahead else 1
    per = 3 if ahead else -(-3 * chunks // RING) * RING
    spare = per - 3 * chunks
    assert per * unroll % RING == 0
    p0 = ring.tiles
    loaded0 = list(ring.loaded)
    turns = (n - 3) // unroll if ahead else n // unroll
    loop_end = turns * unroll
    ring.plan.append(("experts", p0, n, chunks, unroll, turns, per, gate, up, down))
    ring.tiles += n * per

    def gate_tile(x, j=0):
        if ahead:
            return p0 if x == 0 else p0 + 2 + 3 * (x - 1)
        return p0 + x * per + (0 if j == 0 else 2 + 3 * (j - 1))

    def down_tile(x, j=0):
        if ahead:
            return p0 + 2 + 3 * x + (2 if x < n - 1 else 0)
        return p0 + x * per + 2 + 3 * j + (2 if j < chunks - 1 else 0)

    real = [p0 + e * per + k for e in range(n) for k in range(3 * chunks)]
    turn_loads = [16 * sum(1 for t in real if t % RING == q and t < p0 + per * unroll) for q in range(RING)]
    for t in real:
        ring.loaded[t % RING] += 16

    def landed(pe, tile, i):
        q = tile % RING
        pe.wait_ge(ring.full[q], turn_loads[q] * i + (loaded0[q] + 16 * sum(1 for t in real if t % RING == q and t <= tile)))

    def used(eng, tile, i):
        eng.wait_ge(ring.used, (per * unroll) * i + (tile + 1))

    def nth(signal, k, i, step):
        return signal.sem, step * i + (signal.base + 1 + k)

    def by_width(eng, x, i, body):
        e = x + unroll * i
        count = eng.value_load(cnt_i[0:1, bass.ds(e, 1)], min_val=0, max_val=TOK)
        with eng.If(count < narrow + 1):
            body(narrow)
        with eng.Else():
            body(TOK)

    def offset(eng, x, i):
        return eng.value_load(off_i[0:1, bass.ds(x + unroll * i, 1)], min_val=0, max_val=SLOTS)

    cu = chunks * unroll
    narrow_split = chunks > 1
    if narrow_split:
        way = SplitExpert(c, p0, per, chunks, xg, squashed, hidden, outT, landed, used)

    def two_products(pe, x, j, i, w):
        q = x * chunks + j
        if ahead or j >= 2:
            pe.wait_ge(*nth(hidden_ready, max(0, q - 1), i, cu))
        if j == 0:
            pe.wait_ge(*nth(windowed, x + 1, i, unroll))
        par = (x if ahead else j) % 2
        for tile, bank in ((gate_tile(x, j), 0), (gate_tile(x, j) + 1, 2)):
            landed(pe, tile, i)
            wt = ring.view(tile, KD, CH)
            for m in range(2):
                for k in range(KD):
                    last = nc.tensor.matmul(c.psum[:, bank + par, m * TOK:m * TOK + w], wt[:, k, m * P:(m + 1) * P],
                                            xw[:, x % bufs, k, 0:w], start=(k == 0), stop=(k == KD - 1))
            last.then_inc(ring.used, 1)

    def third_product(pe, x, j, i, w):
        tile = down_tile(x, j)
        par = (x if ahead else j) % 2
        pe.wait_ge(*nth(hidden_ready, x * chunks + j + 1, i, cu))
        if j == 0:
            pe.wait_ge(*nth(written, x, i, unroll))
        landed(pe, tile, i)
        wt = ring.view(tile, 2, D)
        for k in range(KD):
            for m in range(2):
                last = nc.tensor.matmul(c.psum[:, 4 + k // 2, (k % 2) * TOK:(k % 2) * TOK + w], wt[:, m, k * P:(k + 1) * P],
                                        hidden[:, par, m, 0:w], start=(j == 0 and m == 0 and k % 2 == 0),
                                        stop=(j == chunks - 1 and m == 1), skip_group_check=True)
        last.then_inc(ring.used, 1 + (spare if j == chunks - 1 else 0))

    def halves(bank, w):
        return c.psum[:, bank, :].rearrange("p (m t) -> p m t", m=2)[:, :, 0:w]

    def window(act, x, i):
        if x >= bufs:
            used(act, gate_tile(x - bufs, chunks - 1) + 1, i)
        elif not ahead:
            act.wait_ge(ring.used, per * i + (p0 - per + gate_tile(0, chunks - 1) + 2 - p0))
        o = offset(act, x, i)
        by_width(act, x, i, lambda w: nc.scalar.activation(
            xw[:, x % bufs, :, 0:w], xg[:, :, bass.ds(o, w)], ACT.Copy).then_inc(windowed.sem, 1))

    def squash(act, x, j, i, w):
        par = (x if ahead else j) % 2
        used(act, gate_tile(x, j), i)
        nc.scalar.activation(squashed[:, par, :, 0:w], halves(par, w), ACT.Silu).then_inc(gate_squashed.sem, 1)

    def combine(dve, x, j, i, w):
        par = (x if ahead else j) % 2
        used(dve, gate_tile(x, j) + 1, i)
        dve.wait_ge(*nth(gate_squashed, x * chunks + j, i, cu))
        nc.vector.tensor_tensor(hidden[:, par, :, 0:w], squashed[:, par, :, 0:w], halves(2 + par, w),
                                ALU.mult).then_inc(hidden_ready.sem, 1)

    def write(dve, x, i, w, o):
        used(dve, down_tile(x, chunks - 1), i)
        dve.wait_ge(*nth(written, x, i, unroll))
        nc.vector.tensor_copy(outT[:, :, bass.ds(o, w)],
                              c.psum[:, 4:8, :].rearrange("p b (m t) -> p (b m) t", m=2)[:, :, 0:w]).then_inc(written.sem, 1)

    def steps(eng, first, step):
        first()
        with eng.Fori(0, turns) as i:
            for x in range(unroll):
                step(x, i)
        for x in range(loop_end, n):
            step(x, 0)

    @c.block.tensor
    def _(pe):
        def step(x, i):
            if not ahead:
                def expert(w):
                    if w == narrow:
                        way.tensor(pe, i, lambda: pe.wait_ge(*nth(written, x, i, unroll)), spare)
                        return
                    pe.drain().then_inc(way.turned.sem, chunks)
                    pe.drain().then_inc(way.rows_turned.sem, 1)
                    two_products(pe, x, 0, i, w)
                    for j in range(chunks):
                        if j < chunks - 1:
                            two_products(pe, x, j + 1, i, w)
                        third_product(pe, x, j, i, w)
                by_width(pe, x, i, expert)
                return
            if x + 1 < n:
                by_width(pe, x + 1, i, lambda w: two_products(pe, x + 1, 0, i, w))
            by_width(pe, x, i, lambda w: third_product(pe, x, 0, i, w))
        steps(pe, lambda: ahead and by_width(pe, 0, 0, lambda w: two_products(pe, 0, 0, 0, w)), step)

    @c.block.scalar
    def _(act):
        nc.scalar.activation(squashed[:, 0, 0, 0:1], c.ones[:, 0:1], ACT.Copy).then_inc(windowed.sem, 1)

        def first():
            if ahead:
                window(act, 0, 0)
                window(act, 1, 0)
                by_width(act, 0, 0, lambda w: squash(act, 0, 0, 0, w))
                window(act, 2, 0)

        def step(x, i):
            if ahead:
                if x + 1 < n:
                    by_width(act, x + 1, i, lambda w: squash(act, x + 1, 0, i, w))
                if x + 3 < n:
                    window(act, x + 3, i)
            else:
                act.wait_ge(ring.used, per * i + (gate_tile(0, chunks - 1) + 2 - per))
                o = offset(act, x, i)

                def expert(w):
                    if w == narrow:
                        way.scalar(act, i, o, windowed, gate_squashed)
                        return
                    nc.scalar.activation(xw[:, 0, :, :], xg[:, :, bass.ds(o, w)], ACT.Copy).then_inc(windowed.sem, 1)
                    for signal, count in ((way.hidden_high, chunks), (way.rows_act, 1)):
                        act.drain().then_inc(signal.sem, count)
                    act.drain().then_inc(ring.high_ready, 3 * chunks)
                    for j in range(chunks):
                        squash(act, x, j, i, w)
                by_width(act, x, i, expert)
        steps(act, first, step)

    @c.block.vector
    def _(dve):
        nc.vector.memset(outT[:, 0, 0:1], 0.0).then_inc(written.sem, 1)
        nc.vector.memset(hidden[:, 0, 0, 0:1], 0.0).then_inc(hidden_ready.sem, 1)
        dve.drain()

        def step(x, i):
            o = offset(dve, x, i)
            if ahead:
                if x + 1 < n:
                    by_width(dve, x + 1, i, lambda w: combine(dve, x + 1, 0, i, w))
                by_width(dve, x, i, lambda w: write(dve, x, i, w, o))
            else:
                def expert(w):
                    if w == narrow:
                        way.vector(dve, i, o, nth(windowed, x + 1, i, unroll),
                                   lambda j: dve.wait_ge(*nth(gate_squashed, x * chunks + j, i, cu)), hidden_ready, written)
                        return
                    for signal, count in ((way.window_low, 1), (way.hidden_low, chunks), (way.rows_dve, 1)):
                        dve.drain().then_inc(signal.sem, count)
                    dve.drain().then_inc(ring.split_ready, 3 * chunks)
                    for j in range(chunks):
                        combine(dve, x, j, i, w)
                    write(dve, x, i, w, o)
                by_width(dve, x, i, expert)
        steps(dve, lambda: ahead and by_width(dve, 0, 0, lambda w: combine(dve, 0, 0, 0, w)), step)
    if narrow_split:
        way.count(n)
    windowed.count += n + 1
    gate_squashed.count += n * chunks
    hidden_ready.count += n * chunks + 1
    written.count += n + 1
    c.join()

    slot_rows = c.S[:, :, :, :].rearrange("p a b t -> p (a b t)").rearrange("p (s d) -> p s d", d=D)
    transpose_stage(c, [([outT[:, 4 * h + k, s * P:(s + 1) * P] for k in range(4)], slot_rows[:, s, h * 512:(h + 1) * 512],
                         ("act", "dve")[h]) for s in range(SLOTS // P) for h in range(2)])
    mixed = c.sig("experts_mixed")
    if meanwhile is not None:
        meanwhile()

    @c.block.tensor
    def _(pe):
        for t in range(TT):
            for h in range(2):
                for s in range(SLOTS // P):
                    last = nc.tensor.matmul(c.psum[:, 2 * t + h, :], spread[:, s, t * P:(t + 1) * P],
                                            slot_rows[:, s, h * 512:(h + 1) * 512], start=(s == 0), stop=(s == SLOTS // P - 1))
            last.then_inc(*mixed.up())

    @c.block.vector
    def _(dve):
        for t in range(TT):
            dve.wait_ge(*mixed.at(t + 1))
            nc.vector.scalar_tensor_tensor(c.x[:, t, :], c.x[:, t, :], alpha,
                                           c.psum[:, 2 * t:2 * t + 2, :].rearrange("p h n -> p (h n)"), ALU.mult, ALU.add)
    c.join()


MOE_G, MOE_E = 4, 8


def route_hier(c, layer, ctx):
    nc, arg = c.nc, c.arg
    sb = lambda name, shape, dt=F32: c.sb(f"r{layer}_" + name, shape, dt, ctx)
    n = MOE_G + MOE_G * MOE_E
    wr, br = sb("wr", [P, KD, n]), sb("br", [P, n])
    lg = sb("lg", [P, TT, n])
    g8, top, topi = sb("g8", [P, TT, 8]), sb("top", [P, TT, 8]), sb("topi", [P, TT, 8], U32)
    idx = sb("idx", [P, TT, 2])
    iota, iota_i = sb("iota", [P, 8]), sb("iota_i", [P, 8], I32)
    ohg, eg, gw = sb("ohg", [P, TT, MOE_G]), sb("eg", [P, TT, MOE_G]), sb("gw", [P, TT, 1])
    prod, es, red = sb("prod", [P, TT, MOE_G, MOE_E]), sb("es", [P, TT, MOE_E]), sb("red", [P, TT, 1])
    pw, oh8 = sb("pw", [P, TT, 2]), sb("oh8", [P, TT, 2, MOE_E])
    oh = sb("oh", [P, TT, 2, MOE_G * MOE_E])
    load_params(c, [(wr[:, :, 0:MOE_G], k_tiles(arg["moe_w_rg"][layer])), (wr[:, :, MOE_G:], k_tiles(arg["moe_w_re"][layer])),
                    (br[:, 0:MOE_G], bcast(arg["moe_b_rg"][layer])), (br[:, MOE_G:], bcast(arg["moe_b_re"][layer]))])
    iotas = c.sig("iota_ready")

    @c.block.gpsimd
    def _(pool):
        nc.gpsimd.iota(iota_i[:, :], pattern=[[1, 8]], base=0, channel_multiplier=0).then_inc(*iotas.up())
    c.join()
    logits_stage(c, wr, br[:, :], n, lg[:, :, :])
    centred, exped = c.sig("router_centred"), c.sig("router_exp")

    @c.block.vector
    def _(dve):
        c.dve(nc.vector.tensor_copy(iota[:, :], iota_i[:, :]))
        c.dve(nc.vector.memset(g8[:, :, :], -3e38))
        c.dve(nc.vector.tensor_copy(g8[:, :, 0:MOE_G], lg[:, :, 0:MOE_G]))
        for t in range(TT):
            c.dve(nc.vector.max(top[:, t, :], g8[:, t, :]))
            c.dve(nc.vector.max_index(topi[:, t, :], top[:, t, :], g8[:, t, :]))
        c.dve(nc.vector.tensor_copy(idx[:, :, 0:1], topi[:, :, 0:1]))
        for t in range(TT):
            c.dve(nc.vector.tensor_scalar(ohg[:, t, :], iota[:, 0:MOE_G], idx[:, t, 0:1], None, ALU.is_equal))
        c.dve(nc.vector.tensor_tensor(eg[:, :, :], lg[:, :, 0:MOE_G], top[:, :, 0:1].broadcast_to([P, TT, MOE_G]), ALU.subtract))
        c.dve(nc.vector.tensor_tensor(prod[:, :, :, :], lg[:, :, MOE_G:].rearrange("p t (g e) -> p t g e", g=MOE_G),
                                      ohg[:, :, :].unsqueeze(3).broadcast_to([P, TT, MOE_G, MOE_E]), ALU.mult))
        c.dve(nc.vector.tensor_reduce(es[:, :, :], prod[:, :, :, :].rearrange("p t g e -> p t e g"), AX_X, ALU.add))
        c.dve(nc.vector.tensor_reduce(red[:, :, :], es[:, :, :], AX_X, ALU.max))
        nc.vector.tensor_tensor(es[:, :, :], es[:, :, :], red[:, :, :].broadcast_to([P, TT, MOE_E]), ALU.subtract).then_inc(*centred.up())
        dve.wait_ge(*exped.at(1))
        c.dve(nc.vector.tensor_reduce(gw[:, :, :], eg[:, :, :], AX_X, ALU.add))
        c.dve(nc.vector.reciprocal(gw[:, :, :], gw[:, :, :]))
        c.dve(nc.vector.tensor_reduce(red[:, :, :], es[:, :, :], AX_X, ALU.add))
        c.dve(nc.vector.reciprocal(red[:, :, :], red[:, :, :]))
        c.dve(nc.vector.tensor_tensor(es[:, :, :], es[:, :, :], red[:, :, :].broadcast_to([P, TT, MOE_E]), ALU.mult))
        for t in range(TT):
            c.dve(nc.vector.max(top[:, t, :], es[:, t, :]))
            c.dve(nc.vector.max_index(topi[:, t, :], top[:, t, :], es[:, t, :]))
        c.dve(nc.vector.tensor_copy(idx[:, :, :], topi[:, :, 0:2]))
        c.dve(nc.vector.tensor_reduce(red[:, :, :], top[:, :, 0:2], AX_X, ALU.add))
        c.dve(nc.vector.reciprocal(red[:, :, :], red[:, :, :]))
        c.dve(nc.vector.tensor_tensor(red[:, :, :], red[:, :, :], gw[:, :, :], ALU.mult))
        c.dve(nc.vector.tensor_tensor(pw[:, :, :], top[:, :, 0:2], red[:, :, :].broadcast_to([P, TT, 2]), ALU.mult))
        for t in range(TT):
            for a in range(2):
                last = nc.vector.tensor_scalar(oh8[:, t, a, :], iota[:, :], idx[:, t, a:a + 1], None, ALU.is_equal)
        dve.drain()
        for a in range(2):
            last = nc.vector.tensor_tensor(oh[:, :, a, :].rearrange("p t (g e) -> p t g e", g=MOE_G),
                                           ohg[:, :, :].unsqueeze(3).broadcast_to([P, TT, MOE_G, MOE_E]),
                                           oh8[:, :, a, :].unsqueeze(2).broadcast_to([P, TT, MOE_G, MOE_E]), ALU.mult)

    @c.block.scalar
    def _(act):
        act.wait_ge(*centred.at(1))
        nc.scalar.activation(eg[:, :, :], eg[:, :, :], ACT.Exp)
        nc.scalar.activation(es[:, :, :], es[:, :, :], ACT.Exp)
        act.drain().then_inc(*exped.up())
    c.join()
    return oh, pw


def hier_moe(c, layer, meanwhile):
    nc, arg = c.nc, c.arg
    with ExitStack() as ctx:
        oh, pw = route_hier(c, layer, ctx)
        one = lambda v: (lambda e, j: v[bass.ds(e, 1)].rearrange("a p k f -> (a p) k f"))
        sparse_experts(c, MOE_G * MOE_E, 1, 6, 128, c.x, oh, pw,
                       one(arg["moe_w_gate"][layer].rearrange("e (k p) f -> e p k f", p=P)),
                       one(arg["moe_w_up"][layer].rearrange("e (k p) f -> e p k f", p=P)),
                       one(arg["moe_w_down"][layer].rearrange("e (k p) f -> e p k f", p=P)),
                       None, DN_ALPHA, ctx,
                       [(c.gain[:, :], bcast(arg["ln2_g"][layer])), (c.bias[:, :], bcast(arg["ln2_b"][layer]))], meanwhile)



ML_H, ML_D, FX_H, FX_D = 4, 64, 8, 64
ML_W, CF_W, FX_W = ML_H * ML_D, D // 4, FX_H * FX_D
ML_K, CF_K = 4, 31
Z_V, Z_O, Z_IF, Z_GLU = 2 * ML_W, 3 * ML_W, 4 * ML_W, 4 * ML_W + 2 * ML_H
Z_FQ = Z_GLU + 2 * CF_W
Z_FF = Z_FQ + 3 * FX_W


def pre_norm(c, gain):
    rms_scales(c, 0, c.x, gain, c.scaled, c.sig("gain_landed").now())
    rms_columns(c, [(0, c.scaled, c.xs)], join=False)


HV, HF = ML_W, FX_W // 2


def hybrid_claims(c, layer):
    w = c.arg["w_in_2"][layer]
    spans = [(Z_V + HV, HV + 2 * ML_H), (Z_FF - HF, HF + FX_H), (0, 256), (256, 256), (Z_GLU, 256), (Z_GLU + 256, 256),
             (Z_V, HV)] + [(Z_FQ + a * 256, 256) for a in range(4)] + [(Z_FQ + 2 * FX_W, HF)]
    jobs = [Job(c.xs, w, n0, width, None, None) for n0, width in spans]
    return jobs, claim(c, jobs)


def adopt(jobs, claims):
    jobs = [x for x in jobs if isinstance(x, Job)]
    assert [(x.n0, x.width) for x in jobs] == [(x.n0, x.width) for x in claims]
    for job, other in zip(jobs, claims):
        job.tiles, job.kt, job.per, job.ready = other.tiles, other.kt, other.per, other.ready


def hybrid_buffers(c, layer, ctx):
    arg = c.arg
    sb = lambda name, shape, dt=F32: c.sb(f"h{layer}_" + name, shape, dt, ctx)
    NT = 2 * ML_W // P
    flat, at = c.S[:, :, :, :].rearrange("p a b t -> p (a b t)"), 0
    views = []
    for n, width in ((NT, ML_K - 1 + TOK), (2, CF_K - 1 + TOK), (2, TOK)):
        views.append(flat[:, at:at + n * width].rearrange("p (n t) -> p n t", n=n))
        at += n * width
    qk_in, cf_in, sg = views
    qk, cf = sb("qk", [P, NT, TOK]), sb("cf", [P, 2, TOK])
    mw, mb = sb("mw", [P, NT, ML_K]), sb("mb", [P, NT])
    cw, cb = sb("cw", [P, 2, CF_K]), sb("cb", [P, 2])
    vo = sb("vo", [P, TT, 2 * ML_W])
    fq, fk, fv = sb("fq", [P, FX_H // 2, TOK]), sb("fk", [P, FX_H // 2, TOK]), sb("fv", [P, TT, FX_W])
    gates, gb = sb("gates", [P, TT, 2 * ML_H + FX_H]), sb("gb", [P, 2 * ML_H + FX_H])
    norm_w, ln_w, ln_b = sb("norm_w", [P, ML_W]), sb("ln_w", [P, CF_W]), sb("ln_b", [P, CF_W])
    NH = ML_H + FX_H
    lf, ab, F, A = (sb(x, [P, TT, NH]) for x in ("lf", "ab", "F", "A"))
    dm = sb("dm", [P, ML_H * 3 * P])
    df = sb("df", [P, FX_H * 3 * P])
    mneg, floor = sb("mneg", [P, TT, ML_H]), sb("floor", [P, TT, ML_H])

    load_ahead(c, "mixer_params_landed", [
        (mw[:, i, :], arg["mlstm_conv_w_2"][layer][:, i * P:(i + 1) * P].rearrange("k p -> p k")) for i in range(NT)] + [
        (mb[:, :], arg["mlstm_conv_b_2"][layer].rearrange("(c p) -> p c", p=P))] + [
        (cw[:, i, :], arg["conf_conv_w_2"][layer][:, i * P:(i + 1) * P].rearrange("k p -> p k")) for i in range(2)] + [
        (cb[:, :], arg["conf_conv_b_2"][layer].rearrange("(c p) -> p c", p=P)),
        (gb[:, 0:ML_H], bcast(arg["mlstm_b_i_2"][layer])), (gb[:, ML_H:2 * ML_H], bcast(arg["mlstm_b_f_2"][layer])),
        (gb[:, 2 * ML_H:], bcast(arg["fox_b_f_2"][layer])),
        (norm_w[:, :], bcast(arg["mlstm_norm_w_2"][layer])), (ln_w[:, :], bcast(arg["conf_ln_w_2"][layer])),
        (ln_b[:, :], bcast(arg["conf_ln_b_2"][layer]))])
    return qk_in, qk, cf_in, cf, sg, mw, mb, cw, cb, vo, fq, fk, fv, \
        gates, gb, norm_w, ln_w, ln_b, lf, ab, F, A, dm, df, mneg, floor


def hybrid_mixer(c, layer, cat, buffers, claims, ahead):
    nc, arg = c.nc, c.arg
    NT, NH = 2 * ML_W // P, ML_H + FX_H
    qk_in, qk, cf_in, cf, sg, mw, mb, cw, cb, vo, fq, fk, fv, \
        gates, gb, norm_w, ln_w, ln_b, lf, ab, F, A, dm, df, mneg, floor = buffers

    def decay(buf, n, t):
        return buf[:, 0:n * P].rearrange("p (h k) -> p h k", h=n) if t == 0 else \
            buf[:, n * P:].rearrange("p (h k) -> p h k", h=n)
    w = arg["w_in_2"][layer]
    cp = lambda dst: (lambda r: nc.scalar.activation(dst, r, ACT.Copy))
    pad, cpad = ML_K - 1, CF_K - 1

    padded = c.sig("conv_padded")

    abs_ready, log_ready, lf_ready = c.sig("gate_abs"), c.sig("gate_log"), c.sig("log_forget_ready")
    sums_taken, max_ready = c.sig("forget_sums_taken"), c.sig("decay_max")
    step, convolved = c.sig("conv_step"), c.sig("convolved")
    taken_act = c.sig("results_taken_act")
    zf = gates[:, :, ML_H:]

    def take_edge(dst, g0, g1):
        def take(r):
            c.dve(nc.vector.tensor_copy(dst, r[:, :, 0:HV]))
            return nc.vector.tensor_copy(gates[:, :, g0:g1], r[:, :, HV:HV + g1 - g0])
        return take

    def gate_bias(dve):
        dve.wait_ge(*c.sig("mixer_params_landed").now())
        dve.drain()
        c.dve(nc.vector.tensor_tensor(gates[:, :, :], gates[:, :, :], gb[:, :].unsqueeze(1).broadcast_to([P, TT, 2 * ML_H + FX_H]), ALU.add))
        nc.vector.scalar_tensor_tensor(ab[:, :, :], zf, -1.0, zf, ALU.mult, ALU.max).then_inc(*abs_ready.up())

    def gate_logs(act):
        act.wait_ge(*abs_ready.at(1))
        c.act(nc.scalar.activation(ab[:, :, :], ab[:, :, :], ACT.Exp, scale=-1.0))
        nc.scalar.activation(ab[:, :, :], ab[:, :, :], ACT.Ln, bias=c.ones[:, 0:1]).then_inc(*log_ready.up())

    def log_forget(dve):
        dve.wait_ge(*log_ready.at(1))
        nc.vector.scalar_tensor_tensor(lf[:, :, :], zf, 0.0, ab[:, :, :], ALU.min, ALU.subtract).then_inc(*lf_ready.up())

    def sum_products(pe, banks):
        pe.wait_ge(*lf_ready.at(1))
        nc.tensor.matmul(banks[:, 0, 0:NH], c.tri01[:, :], lf[:, 0, :], start=True, stop=True)
        nc.tensor.matmul(banks[:, 1, 0:NH], c.ones[:, :], lf[:, 0, :], start=True, stop=False)
        return nc.tensor.matmul(banks[:, 1, 0:NH], c.tri01[:, :], lf[:, 1, :], start=False, stop=True)

    def take_sums(r):
        c.dve(nc.vector.tensor_copy(F[:, :, :], r[:, :, 0:NH]))
        c.dve(nc.vector.tensor_scalar(A[:, :, :], F[:, :, :], -1.0, None, ALU.mult))
        return nc.vector.tensor_tensor(A[:, :, 0:ML_H], A[:, :, 0:ML_H], gates[:, :, 0:ML_H], ALU.add)

    def decay_rows(h0):
        def fill(pe, banks):
            if h0 == 0:
                pe.wait_ge(*c.sig("results_taken_dve").at(3))
            for a in range(4):
                for s in range(TT):
                    at = (a % 2) * TOK + s * P
                    last = nc.tensor.matmul(banks[:, a // 2, at:at + P], A[:, s, h0 + a:h0 + a + 1].broadcast_to([P, P]),
                                            c.ident[:, :], start=True, stop=True)
            return last

        def take(r):
            for h in range(h0, h0 + 4):
                n, i, buf = (ML_H, h, dm) if h < ML_H else (FX_H, h - ML_H, df)
                pos = heads_position(i, n, True)
                for t in range(TT):
                    nk = (t + 1) * P
                    src = r[:, (h - h0) // 2, (h % 2) * TOK:(h % 2) * TOK + nk]
                    last = nc.vector.scalar_tensor_tensor(decay(buf, n, t)[:, pos, :], src, F[:, t, h:h + 1],
                                                          c.mask[:, TOK - nk:], ALU.add, ALU.add)
                    if (h, t) != (h0 + 3, TT - 1):
                        c.dve(last)
            return last
        return Own(fill, "dve", take)

    def decay_maxima(dve):
        dve.drain()
        for t in range(TT):
            c.dve(nc.vector.tensor_reduce(mneg[:, t, :], decay(dm, ML_H, t), AX_X, ALU.max))
            for a in range(2):
                c.dve(nc.vector.tensor_tensor(mneg[:, t, 2 * a:2 * a + 2], mneg[:, t, 2 * a:2 * a + 2], F[:, t, a:ML_H:2], ALU.max))
        nc.vector.tensor_scalar(mneg[:, :, :], mneg[:, :, :], -1.0, None, ALU.mult).then_inc(*max_ready.up())

    def convolve(dve, taps, n, x, acc, wt, b):
        for k in taps:
            for i in range(n):
                if k:
                    dve.wait_ge(step.sem, step.count - n + 1)
                src = x[:, i, k:k + TOK]
                last = nc.vector.tensor_scalar(acc[:, i, :], src, wt[:, i, 0:1], b[:, i:i + 1], ALU.mult, ALU.add) if k == 0 else \
                    nc.vector.scalar_tensor_tensor(acc[:, i, :], src, wt[:, i, k:k + 1], acc[:, i, :], ALU.mult, ALU.add)
                last.then_inc(*step.up())

    def convolve_qk(dve):
        dve.wait_ge(*padded.at(1))
        dve.wait_ge(*taken_act.at(2))
        convolve(dve, range(ML_K), NT, qk_in, qk, mw, mb)
        dve.drain().then_inc(*convolved.up())

    def gate_glu(dve):
        dve.wait_ge(*taken_act.at(4))
        c.dve(nc.vector.tensor_tensor(cf_in[:, :, cpad:], cf_in[:, :, cpad:], sg[:, :, :], ALU.mult))

    def taps_glu(k0, k1):
        return lambda dve: convolve(dve, range(k0, k1), 2, cf_in, cf, cw, cb)

    def decay_exps(act):
        act.wait_ge(*max_ready.at(1))
        for t in range(TT):
            for pos in range(ML_H):
                d = decay(dm, ML_H, t)[:, pos, :]
                nc.scalar.activation(d, d, ACT.Exp, bias=mneg[:, t, pos:pos + 1])
        nc.scalar.activation(floor[:, :, :], mneg[:, :, :], ACT.Exp)
        act.wait_ge(*convolved.at(1))
        nc.scalar.activation(qk[:, :, :], qk[:, :, :], ACT.Silu)

    glu = [Step("dve", gate_glu)] + [Step("dve", taps_glu(k, min(k + 4, CF_K))) for k in range(0, CF_K, 4)]
    more = [
        Rows(c.xs, w, Z_V, HV, "act", cp(vo[:, :, 0:HV])),
        Cols(c.xs, w, Z_FQ, 256, "act", cp(fq[:, 0:2, :])),
        Cols(c.xs, w, Z_FQ + 256, 256, "act", cp(fq[:, 2:4, :])),
        Cols(c.xs, w, Z_FQ + FX_W, 256, "act", cp(fk[:, 0:2, :])),
        Cols(c.xs, w, Z_FQ + FX_W + 256, 256, "act", cp(fk[:, 2:4, :])),
        Step("act", decay_exps),
        Rows(c.xs, w, Z_FQ + 2 * FX_W, HF, "act", cp(fv[:, :, 0:HF]))]
    jobs = [
        Rows(c.xs, w, Z_V + HV, HV + 2 * ML_H, "dve", take_edge(vo[:, :, HV:], 0, 2 * ML_H)),
        Rows(c.xs, w, Z_FF - HF, HF + FX_H, "dve", take_edge(fv[:, :, HF:], 2 * ML_H, 2 * ML_H + FX_H)),
        Step("dve", gate_bias),
        Cols(c.xs, w, 0, 256, "act", cp(qk_in[:, 0:2, pad:])),
        Step("act", gate_logs),
        Step("dve", log_forget),
        Cols(c.xs, w, 256, 256, "act", cp(qk_in[:, 2:4, pad:])),
        Own(sum_products, "dve", take_sums),
        Cols(c.xs, w, Z_GLU, 256, "act", cp(cf_in[:, :, cpad:])),
        decay_rows(0), decay_rows(4),
        Cols(c.xs, w, Z_GLU + 256, 256, "act", lambda r: nc.scalar.activation(sg[:, :, :], r, ACT.Sigmoid)),
        decay_rows(8),
        Step("dve", decay_maxima), more[0], Step("dve", convolve_qk)] + (
        glu[:2] + more[1:2] + glu[2:4] + more[2:3] + glu[4:5] + more[3:4] + glu[5:7] + more[4:6] + glu[7:8] + more[6:] + glu[8:])
    adopt(jobs, claims)
    c.join()
    load_ahead(c, "gain_landed", [(c.bias[:, :], bcast(arg["norm_xattn_w_2"][layer])),
                                  (c.gain[:, :], bcast(arg["norm_mem_w_2"][layer]))])

    @c.block.gpsimd
    def _(pool):
        nc.gpsimd.memset(qk_in[:, :, 0:pad], 0.0)
        nc.gpsimd.memset(cf_in[:, :, 0:cpad], 0.0)
        pool.drain().then_inc(*padded.up())
    projection(c, jobs, join=False)
    c.join()
    half = lambda i: slice((i % 2) * 64, (i % 2) * 64 + 64)
    hm = vo[:, :, 0:ML_W]
    attention(c, [(t, 0) for t in range(TT)], ML_H, ML_D,
              q=lambda t, b, i: qk[half(i), i // 2, t * P:(t + 1) * P], k=lambda b, i, nk: qk[half(i), 2 + i // 2, 0:nk],
              v=lambda b, i, s: vo[:, s, i * ML_D:(i + 1) * ML_D],
              out=lambda t, b: cat[:, t, 0:ML_W].rearrange("p (h d) -> p h d", h=ML_H),
              scale=ML_D ** -0.5, bias=None,
              gated=(lambda t, nk: decay(dm, ML_H, t), lambda t: floor[:, t, :]))
    attention(c, [(t, 0) for t in range(TT)], FX_H, FX_D, ahead=ahead(),
              q=lambda t, b, i: fq[half(i), i // 2, t * P:(t + 1) * P], k=lambda b, i, nk: fk[half(i), i // 2, 0:nk],
              v=lambda b, i, s: fv[:, s, i * FX_D:(i + 1) * FX_D],
              out=lambda t, b: cat[:, t, ML_W + CF_W:].rearrange("p (h d) -> p h d", h=FX_H),
              scale=FX_D ** -0.5, bias=lambda t, b, nk: decay(df, FX_H, t))

    transpose_stage(c, [([cf[:, i, t * P:(t + 1) * P] for i in range(2)], cat[:, t, ML_W:ML_W + CF_W], "dve") for t in range(TT)])
    og = vo[:, :, ML_W:]
    norm_stage(c, [dict(src=cat[:, t, 0:ML_W].rearrange("p (h d) -> p h d", h=ML_H),
                        dst=hm[:, t, :].rearrange("p (h d) -> p h d", h=ML_H), kind="rms", eps=RMS_EPS, gain=None, bias=None)
                   for t in range(TT)] +
               [dict(src=cat[:, :, ML_W:ML_W + CF_W], dst=cat[:, :, ML_W:ML_W + CF_W], kind="ln", eps=RMS_EPS,
                     gain=ln_w[:, :], bias=ln_b[:, :])])

    @c.block.scalar
    def _(act):
        nc.scalar.activation(cat[:, :, ML_W:ML_W + CF_W], cat[:, :, ML_W:ML_W + CF_W], ACT.Silu)
        nc.scalar.activation(og, og, ACT.Sigmoid).then_inc(*c.sig("output_gate").up())

    @c.block.vector
    def _(dve):
        c.dve(nc.vector.tensor_tensor(hm, hm, norm_w[:, :].unsqueeze(1).broadcast_to([P, TT, ML_W]), ALU.mult))
        dve.wait_ge(*c.sig("output_gate").at(1))
        nc.vector.tensor_tensor(cat[:, :, 0:ML_W], hm, og, ALU.mult)
    c.join()


XA_H, XA_D = 4, 128
XA_W = XA_H * XA_D


def cross_attention(c, layer, before, after):
    nc, arg = c.nc, c.arg
    with ExitStack() as ctx:
        sb = lambda name, shape, dt=F32: c.sb(f"x{layer}_" + name, shape, dt, ctx)
        rows, mem = sb("rows", [P, TT, D]), sb("mem", [P, TT, D])
        memT = (sb("mem_high", [P, KD, TOK], F32R)[:, :, :], sb("mem_low", [P, KD, TOK], F32R)[:, :, :])
        qT, kT, v = sb("qT", [P, XA_H, TOK]), sb("kT", [P, XA_H, TOK]), sb("v", [P, TT, XA_W])
        o, oT = sb("o", [P, TT, XA_W]), tuple(x[:, 0:XA_H, :] for x in c.xs)
        cp = lambda dst: (lambda r: nc.scalar.activation(dst, r, ACT.Copy))
        dcp = lambda dst: (lambda r: nc.vector.tensor_copy(dst, r))
        wq, wkv = arg["xattn_w_q_2"][layer], arg["xattn_w_kv_2"][layer]
        jobs = [Cols(c.xs, wq, 0, 256, "act", cp(qT[:, 0:2, :])), Cols(c.xs, wq, 256, 256, "dve", dcp(qT[:, 2:4, :])),
                Cols(memT, wkv, 0, 256, "act", cp(kT[:, 0:2, :])), Cols(memT, wkv, 256, 256, "dve", dcp(kT[:, 2:4, :])),
                Rows(memT, wkv, 512, 512, "act", cp(v[:, :, :]))]
        load_ahead(c, "mem_landed", [(mem[:, :, :], arg["mem_2"][0].rearrange("(t p) d -> p t d", p=P))])
        rms_scales(c, 1, mem, c.gain[:, :], rows, c.sig("mem_landed").now())
        projection(c, before, then=lambda: claim(c, jobs))
        rms_scales(c, 0, c.x, c.bias[:, :], c.scaled, c.sig("gain_landed").now())
        rms_columns(c, [(1, rows, memT), (0, c.scaled, c.xs)])
        load_ahead(c, "gain_landed", [
            (c.bias[:, :], bcast(arg["norm_ffn_w_2"][layer])),
            (c.gain[:, :], bcast(arg["norm_mix_w_2"][layer + 1] if layer < DEPTH - 1 else arg["norm_final_w_2"]))])
        projection(c, jobs)
        jobs = residual_jobs(c, oT, arg["xattn_w_o_2"][layer], 1.0)
        attention(c, [(t, 0) for t in range(TT)], XA_H, XA_D, ahead=claim(c, jobs),
                  q=lambda t, b, i: qT[:, i, t * P:(t + 1) * P], k=lambda b, i, nk: kT[:, i, 0:nk],
                  v=lambda b, i, s: v[:, s, i * XA_D:(i + 1) * XA_D],
                  out=lambda t, b: o[:, t, :].rearrange("p (h d) -> p h d", h=XA_H),
                  scale=XA_D ** -0.5, bias=None, paired=False, causal=False)
        rows_to_columns(c, o, oT, XA_H)
        projection(c, jobs, then=after)


F2 = 2816
FFC = F2 // CH
EXP2 = 8


def claim_dense_ffn(c):
    cols = lambda v: (lambda j: v.rearrange("(k p) (c f) -> c p k f", p=P, f=CH)[bass.ds(j, 1)].rearrange("a p k f -> (a p) k f"))
    rows = lambda v: (lambda j: v.rearrange("(c k p) n -> c p k n", p=P, k=2)[bass.ds(j, 1)].rearrange("a p k f -> (a p) k f"))
    arg = c.arg
    return claim_stream(c, FFC, cols(arg["ffn_w_gate_2"][0]), cols(arg["ffn_w_up_2"][0]), rows(arg["ffn_w_down_2"][0]))


def dense_ffn(c, start):
    with ExitStack() as ctx:
        pre_norm(c, c.bias[:, :])
        c.join()
        claims, then = hybrid_claims(c, 1)
        stream_ffn(c, FFC, start, then, ctx)
    return claims


def flat_moe(c, layer):
    nc, arg = c.nc, c.arg
    with ExitStack() as ctx:
        sb = lambda name, shape, dt=F32: c.sb("f_" + name, shape, dt, ctx)
        wr, lg = sb("wr", [P, KD, EXP2]), sb("lg", [P, TT, EXP2])
        top, topi, idx = sb("top", [P, TT, 8]), sb("topi", [P, TT, 8], U32), sb("idx", [P, TT, 2])
        iota, iota_i = sb("iota", [P, 8]), sb("iota_i", [P, 8], I32)
        zero = sb("zero", [P, EXP2])
        e1, w = sb("e1", [P, TT, 1]), sb("w", [P, TT, 2])
        oh = sb("oh", [P, TT, 2, EXP2])
        outT = sb("outT", [P, KD, SLOTS + TOK])
        rows = outT[:, :, :].rearrange("p k s -> p (k s)")[:, 0:TT * D].rearrange("p (t d) -> p t d", t=TT)
        load_params(c, [(wr[:, :, :], k_tiles(arg["router_w_2"][0]))])
        rms_scales(c, 0, c.x, c.bias[:, :], c.scaled, c.sig("gain_landed").now())
        rms_columns(c, [(0, c.scaled, c.xT)], join=False)

        @c.block.vector
        def _(dve):
            for t in range(TT):
                nc.vector.tensor_scalar(rows[:, t, :], c.scaled[:, t, :], c.rstd[:, 0, t, :], None, ALU.mult)

        @c.block.gpsimd
        def _(pool):
            nc.gpsimd.memset(zero[:, :], 0.0)
            nc.gpsimd.iota(iota_i[:, :], pattern=[[1, 8]], base=0, channel_multiplier=0)
        c.join()
        logits_stage(c, wr, zero[:, :], EXP2, lg[:, :, :])
        centred, exped = c.sig("router_centred"), c.sig("router_exp")

        @c.block.vector
        def _(dve):
            c.dve(nc.vector.tensor_copy(iota[:, :], iota_i[:, :]))
            for t in range(TT):
                c.dve(nc.vector.max(top[:, t, :], lg[:, t, :]))
                c.dve(nc.vector.max_index(topi[:, t, :], top[:, t, :], lg[:, t, :]))
            c.dve(nc.vector.tensor_copy(idx[:, :, :], topi[:, :, 0:2]))
            nc.vector.tensor_tensor(e1[:, :, :], top[:, :, 1:2], top[:, :, 0:1], ALU.subtract).then_inc(*centred.up())
            dve.wait_ge(*exped.at(1))
            c.dve(nc.vector.tensor_scalar(w[:, :, 0:1], e1[:, :, :], 1.0, None, ALU.add))
            c.dve(nc.vector.reciprocal(w[:, :, 0:1], w[:, :, 0:1]))
            c.dve(nc.vector.tensor_tensor(w[:, :, 1:2], w[:, :, 0:1], e1[:, :, :], ALU.mult))
            for t in range(TT):
                for a in range(2):
                    last = nc.vector.tensor_scalar(oh[:, t, a, :], iota[:, :], idx[:, t, a:a + 1], None, ALU.is_equal)

        @c.block.scalar
        def _(act):
            act.wait_ge(*centred.at(1))
            nc.scalar.activation(e1[:, :, :], e1[:, :, :], ACT.Exp).then_inc(*exped.up())
        c.join()

        def cols(v):
            vv = v.rearrange("e (k p) (c f) -> e c p k f", p=P, f=CH)
            return lambda e, j: vv[bass.ds(e, 1), j:j + 1].rearrange("a b p k f -> (a b p) k f")
        down = arg["moe_w_down_2"][0].rearrange("e (c k p) n -> e c p k n", p=P, k=2)
        sparse_experts(c, EXP2, FFC, 1, 128, rows, oh, w, cols(arg["moe_w_gate_2"][0]), cols(arg["moe_w_up_2"][0]),
                       lambda e, j: down[bass.ds(e, 1), j:j + 1].rearrange("a b p k n -> (a b p) k n"), outT, 1.0, ctx)


def load_weights(c):
    ring = c.ring

    @c.block.sync
    def _(sp):
        def load(n, i, dst_n, src):
            if dst_n >= RING:
                sp.wait_ge(ring.used, n - RING + 1)
            kt, cols = src.shape[1:]
            sp.dma_start(ring.view(dst_n, kt, cols), src).then_inc(ring.full[dst_n % RING], 16)

        for entry in ring.plan:
            if entry[0] == "tile":
                _, n, dst, src = entry
                load(n, 0, n, src)
                continue
            if entry[0] == "experts":
                _, p0, n, chunks, unroll, turns, per, gate, up, down = entry

                def expert(x, i):
                    e, far = x + unroll * i, (per * unroll) * i
                    tile = lambda at, src: load(far + at, i, at, src)
                    if chunks == 1:
                        if x + 1 < n:
                            tile(p0 + 2 + 3 * x, gate(e + 1, 0))
                            tile(p0 + 3 + 3 * x, up(e + 1, 0))
                        tile(p0 + 2 + 3 * x + (2 if x + 1 < n else 0), down(e, 0))
                        return
                    at = p0 + per * x
                    tile(at, gate(e, 0))
                    tile(at + 1, up(e, 0))
                    for j in range(chunks - 1):
                        tile(at + 2 + 3 * j, gate(e, j + 1))
                        tile(at + 3 + 3 * j, up(e, j + 1))
                        tile(at + 4 + 3 * j, down(e, j))
                    tile(at + 3 * chunks - 1, down(e, chunks - 1))
                if chunks == 1:
                    load(p0, 0, p0, gate(0, 0))
                    load(p0 + 1, 0, p0 + 1, up(0, 0))
                with sp.Fori(0, turns) as i:
                    for x in range(unroll):
                        expert(x, i)
                for x in range(turns * unroll, n):
                    expert(x, 0)
                continue
            _, p0, n, gate, up, down = entry
            U = 6
            loops = max(0, (n - 2) // U)

            def chunk(j, first, i):
                at = p0 + 2 + 3 * first
                load(at + 3 * U * i, i, at, gate(j + 1))
                load(at + 1 + 3 * U * i, i, at + 1, up(j + 1))
                load(at + 2 + 3 * U * i, i, at + 2, down(j))
            load(p0, 0, p0, gate(0))
            load(p0 + 1, 0, p0 + 1, up(0))
            chunk(0, 0, 0)
            if loops:
                with sp.Fori(0, loops) as i:
                    for r in range(U):
                        chunk(i * U + 1 + r, 1 + r, i)
            for j in range(1 + U * loops, n - 1):
                chunk(j, j, 0)
            load(p0 + 3 * n - 1, 0, p0 + 3 * n - 1, down(n - 1))


def build(nc, arg, out):
    with ExitStack() as ctx:
        c = Core(nc, ctx)
        c.arg = arg
        c.ring = WeightRing(c)
        c.block = ctx.enter_context(nc.Block(no_gpsimd_drain=True))
        constants(c)
        rows_to_columns(c, c.x, c.xs, KD, join=False)

        def stages():
            for layer, mixer in enumerate((ab_mixer, nsa_mixer)):
                with ExitStack() as m:
                    cat = c.sb(f"cat{layer}", [P, TT, D], ctx=m)
                    jobs = residual_jobs(c, c.xs, arg[("ab_w_o", "c_w_o")[layer]][0], DN_ALPHA)
                    mixer(c, cat, m, lambda: claim(c, jobs))
                    load_ahead(c, "norm_params_landed", [(c.gain[:, :], bcast(arg["ln1_g"][layer])),
                                                         (c.bias[:, :], bcast(arg["ln1_b"][layer]))])
                    rows_to_columns(c, cat, c.xs, KD)
                projection(c, jobs)
                post_norm(c)
                claims = []

                def claim_hybrid():
                    jobs, tiles = hybrid_claims(c, 0)
                    claims.extend(jobs)
                    split_ahead(c, tiles)
                hier_moe(c, layer, claim_hybrid if layer == DEPTH - 1 else None)
                if layer < DEPTH - 1:
                    post_norm(c)
            for layer in range(DEPTH):
                with ExitStack() as m:
                    cat = c.sb(f"cat{2 + layer}", [P, TT, D], ctx=m)
                    gain = c.gain[:, :]
                    if layer == 0:
                        gain = cat[:, 0, :]
                        load_ahead(c, "gain_landed", [(gain, bcast(arg["norm_mix_w_2"][0]))])
                        post_norm(c, columns=False)
                    hybrid_params = hybrid_buffers(c, layer, m)
                    pre_norm(c, gain)
                    jobs = residual_jobs(c, c.xs, arg["w_out_2"][layer], 1.0)
                    hybrid_mixer(c, layer, cat, hybrid_params, claims, lambda: claim(c, jobs))
                    rows_to_columns(c, cat, c.xs, KD)
                dense = []

                def claim_dense():
                    start, tiles = claim_dense_ffn(c)
                    dense.append(start)
                    return tiles
                cross_attention(c, layer, jobs, claim_dense if layer == 0 else None)
                if layer == 0:
                    claims = dense_ffn(c, dense[0])
                else:
                    flat_moe(c, layer)
        stages()
        res = c.sb("result", [P, TT, D])
        rms_scales(c, 0, c.x, c.gain[:, :], res, c.sig("gain_landed").now())
        stored, scaled = c.sig("result_stored"), c.sig("result_scaled")
        out_rows = out[0].rearrange("(t p) d -> p t d", p=P)

        @c.block.vector
        def _(dve):
            nc.vector.tensor_scalar(res[:, 0, :], res[:, 0, :], c.rstd[:, 0, 0, :], None, ALU.mult).then_inc(*scaled.up())

        @c.block.scalar
        def _(act):
            act.wait_ge(*c.sig("rms_diagonal_0").now())
            c.act(nc.scalar.activation(res[:, 1, :], res[:, 1, :], ACT.Copy, scale=c.rstd[:, 0, 1, :]))
            act.dma_start(out_rows[:, 1, :], res[:, 1, :]).then_inc(*stored.up(16))
            act.wait_ge(*scaled.at(1))
            act.dma_start(out_rows[:, 0, :], res[:, 0, :]).then_inc(*stored.up(16))
            act.wait_ge(*stored.now())

        load_weights(c)


_OUTS = [((1, TOK, D), "float32")]


def kernel(**inputs):
    import numpy as _np
    import concourse.bacc as _bacc
    from concourse import mybir as _mybir
    from concourse.bass_utils import run_bass_kernel_spmd as _run

    nc = _bacc.Bacc("TRN2", target_bir_lowering=False, num_devices=1)
    arrays, arg = {}, {}
    for name, a in inputs.items():
        a = _np.ascontiguousarray(a)
        arrays[f"in_{name}_dram"] = a
        arg[name] = nc.dram_tensor(f"in_{name}_dram", a.shape, _mybir.dt.from_np(a.dtype), kind="ExternalInput").ap()
    shape, dtype = _OUTS[0]
    out = nc.dram_tensor("out_0_dram", shape, _mybir.dt.from_np(_np.dtype(dtype)), kind="ExternalOutput").ap()
    build(nc, arg, out)
    r = _run(nc, [arrays], core_ids=[0])
    return r.results[0]["out_0_dram"]
```
